# Optimizing a Trainium2 kernel written in Bass

```python
import jax, jax.numpy as jnp
from jax import lax
import numpy as np

D_MODEL = 1024
BATCH = 1
SEQ = 512
DEPTH = 2
DEC_BATCH = 1
DEC_SEQ = 32
PAST_LEN = 128

CHUNK = 64
BAND_CHUNKS = 8
HEAD_DIM = 64
A_HEADS = 8
B_HEADS = 8
B_KEY_DIM = 64
B_VAL_DIM = 64
D_A = A_HEADS * HEAD_DIM
D_B = B_HEADS * B_KEY_DIM
AB_IN = 3 * D_A + 4 * D_B
REL_CLIP = 128
HGRN_BLOCK = 16
CONV_WIDTH = 3
N_GROUPS = 4
EXPERTS_PER_GROUP = 8
N_EXPERTS = N_GROUPS * EXPERTS_PER_GROUP
TOP_K_IN_GROUP = 2
D_EXPERT = 256
N_AB = (DEPTH + 1) // 2
N_C = DEPTH // 2
RMS_EPS = 1e-6
NEG_INF = -1e30

kernel_name = "chunk_band_hgrn2_shortconv_hmoe_step"

def rmsnorm(x, gain):
    xf = x.astype(jnp.float32)
    y = xf * lax.rsqrt(jnp.mean(xf * xf, axis=-1, keepdims=True) + RMS_EPS)
    return (y * gain.astype(jnp.float32)).astype(x.dtype)

def ab_project(xn, w_in, q_gain, k_gain, lb):
    B, T, _ = xn.shape
    z = xn @ w_in
    idx = [D_A, 2 * D_A, 3 * D_A, 3 * D_A + D_B, 3 * D_A + 2 * D_B, 3 * D_A + 3 * D_B]
    qa, ka, va, fb, ib, qb, gb = jnp.split(z, idx, axis=-1)
    qa = rmsnorm(qa.reshape(B, T, A_HEADS, HEAD_DIM), q_gain)
    ka = rmsnorm(ka.reshape(B, T, A_HEADS, HEAD_DIM), k_gain)
    va = va.reshape(B, T, A_HEADS, HEAD_DIM)
    lbf = lb.astype(jnp.float32)
    f = lbf + (1.0 - lbf) * jax.nn.sigmoid(fb.astype(jnp.float32))
    logf = jnp.log(f).reshape(B, T, B_HEADS, B_KEY_DIM)
    kb = (1.0 - f).reshape(B, T, B_HEADS, B_KEY_DIM)
    qb = jax.nn.silu(qb.astype(jnp.float32)).reshape(B, T, B_HEADS, B_KEY_DIM)
    vb = ib.astype(jnp.float32).reshape(B, T, B_HEADS, B_VAL_DIM)
    return qa, ka, va, qb, kb, vb, logf, gb

def rel_bias_lookup(rel_bias, rel):
    idx = jnp.clip(rel, -REL_CLIP, REL_CLIP) + REL_CLIP
    return jnp.take(rel_bias, idx, axis=1)

def band_attention_prompt(q, k, v, rel_bias):
    B, T, H, Dh = q.shape
    nc = T // CHUNK
    nb = BAND_CHUNKS + 1
    pad = ((0, 0), (BAND_CHUNKS * CHUNK, 0), (0, 0), (0, 0))
    kp = jnp.pad(k, pad).reshape(B, nc + BAND_CHUNKS, CHUNK, H, Dh)
    vp = jnp.pad(v, pad).reshape(B, nc + BAND_CHUNKS, CHUNK, H, Dh)
    band = jnp.arange(nc)[:, None] + jnp.arange(nb)[None, :]
    kb = kp[:, band].reshape(B, nc, nb * CHUNK, H, Dh)
    vb = vp[:, band].reshape(B, nc, nb * CHUNK, H, Dh)
    qc = q.reshape(B, nc, CHUNK, H, Dh)
    r = jnp.arange(CHUNK)
    j = jnp.arange(nb)
    rel = (BAND_CHUNKS - j)[None, :, None] * CHUNK + r[:, None, None] - r[None, None, :]
    bias = rel_bias_lookup(rel_bias, rel.reshape(CHUNK, nb * CHUNK)).astype(jnp.float32)
    valid = (jnp.arange(nc)[:, None] - BAND_CHUNKS + j[None, :]) >= 0
    valid = jnp.repeat(valid, CHUNK, axis=1)
    s = jnp.einsum('bcqhd,bckhd->bhcqk', qc, kb).astype(jnp.float32) * (Dh ** -0.5) + bias[:, None]
    s = jnp.where(valid[:, None, :], s, NEG_INF)
    p = jax.nn.softmax(s, axis=-1).astype(v.dtype)
    o = jnp.einsum('bhcqk,bckhd->bcqhd', p, vb)
    return o.reshape(B, T, H, Dh)

def band_attention_sample(q, k_all, v_all, rel_bias):
    B, Tn, H, Dh = q.shape
    K = k_all.shape[1]
    L = K - Tn
    rel = (L + jnp.arange(Tn))[:, None] - jnp.arange(K)[None, :]
    bias = rel_bias_lookup(rel_bias, rel).astype(jnp.float32)
    s = jnp.einsum('bqhd,bkhd->bhqk', q, k_all).astype(jnp.float32) * (Dh ** -0.5) + bias
    p = jax.nn.softmax(s, axis=-1).astype(v_all.dtype)
    return jnp.einsum('bhqk,bkhd->bqhd', p, v_all)

def hgrn2_blocked(q, k, v, logf, s0):
    B, T, H, Dk = q.shape
    Dv = v.shape[-1]
    nb = -(-T // HGRN_BLOCK)
    pad = nb * HGRN_BLOCK - T
    pw = ((0, 0), (0, pad), (0, 0), (0, 0))
    rs = lambda a: jnp.pad(a, pw).reshape(B, nb, HGRN_BLOCK, H, a.shape[-1]).astype(jnp.float32)
    q, k, v, logf = rs(q), rs(k), rs(v), rs(logf)
    b = jnp.cumsum(logf, axis=2)
    b_last = b[:, :, -1:]
    q_dec = q * jnp.exp(b)
    k_in = k * jnp.exp(-b)
    k_out = k * jnp.exp(b_last - b)
    mask = jnp.tril(jnp.ones((HGRN_BLOCK, HGRN_BLOCK), jnp.float32))
    attn = jnp.einsum('bnthk,bnshk->bnhts', q_dec, k_in) * mask
    o_intra = jnp.einsum('bnhts,bnshv->bnthv', attn, v)
    u = jnp.einsum('bnshk,bnshv->bnhkv', k_out, v)
    decay = jnp.exp(b_last[:, :, 0])

    def step(s, inp):
        d, uu = inp
        return d[..., None] * s + uu, s

    s_final, s_prev = lax.scan(step, s0.astype(jnp.float32),
                               (jnp.moveaxis(decay, 1, 0), jnp.moveaxis(u, 1, 0)))
    s_prev = jnp.moveaxis(s_prev, 0, 1)
    o_inter = jnp.einsum('bnthk,bnhkv->bnthv', q_dec, s_prev)
    o = (o_intra + o_inter).reshape(B, nb * HGRN_BLOCK, H, Dv)[:, :T]
    return o, s_final

def ab_output(oa, ob, gb, out_gain, w_out):
    B, T = oa.shape[:2]
    ob = rmsnorm(ob, out_gain.reshape(B_HEADS, B_VAL_DIM)).reshape(B, T, D_B)
    ob = ob * jax.nn.silu(gb.astype(jnp.float32))
    z = jnp.concatenate([oa.reshape(B, T, D_A), ob.astype(oa.dtype)], axis=-1)
    return z @ w_out

def short_conv(xn, w_in, conv_w, w_out, prev):
    T = xn.shape[1]
    z = xn @ w_in
    bg, cg, h = jnp.split(z, 3, axis=-1)
    u = cg * h
    up = jnp.concatenate([prev.astype(u.dtype), u], axis=1)
    conv = up[:, 0:T] * conv_w[0]
    for j in range(1, CONV_WIDTH):
        conv = conv + up[:, j:j + T] * conv_w[j]
    y = (bg * conv) @ w_out
    return y, up[:, -(CONV_WIDTH - 1):]

def hier_moe(x, w_group, b_group, w_expert, b_expert, w1, w3, w2):
    B, T, D = x.shape
    xt = x.reshape(B * T, D)
    g_logits = (xt @ w_group).astype(jnp.float32) + b_group.astype(jnp.float32)
    g_prob = jax.nn.softmax(g_logits, axis=-1)
    grp = jnp.argmax(g_logits, axis=-1)
    p_grp = jnp.take_along_axis(g_prob, grp[:, None], axis=-1)
    e_logits = ((xt @ w_expert).astype(jnp.float32) + b_expert.astype(jnp.float32)).reshape(-1, N_GROUPS, EXPERTS_PER_GROUP)
    sel = jnp.take_along_axis(e_logits, grp[:, None, None], axis=1)[:, 0]
    topv, topi = lax.top_k(sel, TOP_K_IN_GROUP)
    w_top = jax.nn.softmax(topv, axis=-1)
    gate_in = jnp.sum(jax.nn.one_hot(topi, EXPERTS_PER_GROUP, dtype=jnp.float32) * w_top[..., None], axis=1)
    gates = (jax.nn.one_hot(grp, N_GROUPS, dtype=jnp.float32)[:, :, None] * gate_in[:, None, :] * p_grp[:, :, None])
    gates = gates.reshape(-1, N_EXPERTS).astype(x.dtype)
    h = jax.nn.silu(jnp.einsum('nd,edf->nef', xt, w1)) * jnp.einsum('nd,edf->nef', xt, w3) * gates[..., None]
    out = jnp.einsum('nef,efd->nd', h, w2)
    return out.reshape(B, T, D)

def setup_inputs(seed: int = 0) -> dict:
    key = jax.random.key(seed)
    ks = jax.random.split(key, 32)
    f32 = jnp.float32
    nrm = lambda k, shape, scale: jax.random.normal(k, shape, f32) * scale
    L_A = min(BAND_CHUNKS * CHUNK, PAST_LEN)
    return {
        "x_prompt": nrm(ks[0], (BATCH, SEQ, D_MODEL), 1.0),
        "x_sample": nrm(ks[1], (DEC_BATCH, DEC_SEQ, D_MODEL), 1.0),
        "cache_a_k": nrm(ks[2], (N_AB, DEC_BATCH, L_A, A_HEADS, HEAD_DIM), 1.0),
        "cache_a_v": nrm(ks[3], (N_AB, DEC_BATCH, L_A, A_HEADS, HEAD_DIM), 1.0),
        "state_hgrn": nrm(ks[4], (N_AB, DEC_BATCH, B_HEADS, B_KEY_DIM, B_VAL_DIM), 0.3),
        "state_conv": nrm(ks[5], (N_C, DEC_BATCH, CONV_WIDTH - 1, D_MODEL), 0.5),
        "norm_mix": 1.0 + nrm(ks[6], (DEPTH, D_MODEL), 0.01),
        "norm_ffn": 1.0 + nrm(ks[7], (DEPTH, D_MODEL), 0.01),
        "w_in_ab": nrm(ks[8], (N_AB, D_MODEL, AB_IN), D_MODEL ** -0.5),
        "w_out_ab": nrm(ks[9], (N_AB, D_A + D_B, D_MODEL), (D_A + D_B) ** -0.5),
        "q_norm": 1.0 + nrm(ks[10], (N_AB, HEAD_DIM), 0.01),
        "k_norm": 1.0 + nrm(ks[11], (N_AB, HEAD_DIM), 0.01),
        "rel_bias": nrm(ks[12], (N_AB, A_HEADS, 2 * REL_CLIP + 1), 0.1),
        "hgrn_lb_logits": nrm(ks[13], (N_AB + 1, D_B), 0.5),
        "hgrn_out_norm": 1.0 + nrm(ks[14], (N_AB, D_B), 0.01),
        "w_in_c": nrm(ks[15], (N_C, D_MODEL, 3 * D_MODEL), D_MODEL ** -0.5),
        "conv_w": nrm(ks[16], (N_C, CONV_WIDTH, D_MODEL), CONV_WIDTH ** -0.5),
        "w_out_c": nrm(ks[17], (N_C, D_MODEL, D_MODEL), D_MODEL ** -0.5),
        "w_group": nrm(ks[18], (DEPTH, D_MODEL, N_GROUPS), D_MODEL ** -0.5),
        "b_group": nrm(ks[19], (DEPTH, N_GROUPS), 0.01),
        "w_expert": nrm(ks[20], (DEPTH, D_MODEL, N_EXPERTS), D_MODEL ** -0.5),
        "b_expert": nrm(ks[21], (DEPTH, N_EXPERTS), 0.01),
        "w1": nrm(ks[22], (DEPTH, N_EXPERTS, D_MODEL, D_EXPERT), D_MODEL ** -0.5),
        "w3": nrm(ks[23], (DEPTH, N_EXPERTS, D_MODEL, D_EXPERT), D_MODEL ** -0.5),
        "w2": nrm(ks[24], (DEPTH, N_EXPERTS, D_EXPERT, D_MODEL), D_EXPERT ** -0.5),
    }

def reference(x_prompt, x_sample, cache_a_k, cache_a_v, state_hgrn, state_conv,
              norm_mix, norm_ffn, w_in_ab, w_out_ab, q_norm, k_norm, rel_bias,
              hgrn_lb_logits, hgrn_out_norm, w_in_c, conv_w, w_out_c,
              w_group, b_group, w_expert, b_expert, w1, w3, w2):
    hp, hs = x_prompt, x_sample
    lb_all = jnp.cumsum(jax.nn.softmax(hgrn_lb_logits.astype(jnp.float32), axis=0), axis=0)
    L_A = cache_a_k.shape[2]
    nk_p, nv_p, nk_s, nv_s, nh_p, nh_s, nc_p, nc_s = [], [], [], [], [], [], [], []
    for layer in range(DEPTH):
        l = layer // 2
        if layer % 2 == 0:
            qa, ka, va, qb, kb, vb, logf, gb = ab_project(rmsnorm(hp, norm_mix[layer]), w_in_ab[l], q_norm[l], k_norm[l], lb_all[l])
            oa = band_attention_prompt(qa, ka, va, rel_bias[l])
            s0 = jnp.zeros((hp.shape[0], B_HEADS, B_KEY_DIM, B_VAL_DIM), jnp.float32)
            ob, sp = hgrn2_blocked(qb, kb, vb, logf, s0)
            mix_p = ab_output(oa, ob, gb, hgrn_out_norm[l], w_out_ab[l])
            keep = min(BAND_CHUNKS * CHUNK, hp.shape[1])
            nk_p.append(ka[:, -keep:])
            nv_p.append(va[:, -keep:])
            nh_p.append(sp)
            qa, ka, va, qb, kb, vb, logf, gb = ab_project(rmsnorm(hs, norm_mix[layer]), w_in_ab[l], q_norm[l], k_norm[l], lb_all[l])
            k_all = jnp.concatenate([cache_a_k[l].astype(ka.dtype), ka], axis=1)
            v_all = jnp.concatenate([cache_a_v[l].astype(va.dtype), va], axis=1)
            oa = band_attention_sample(qa, k_all, v_all, rel_bias[l])
            ob, ss = hgrn2_blocked(qb, kb, vb, logf, state_hgrn[l])
            mix_s = ab_output(oa, ob, gb, hgrn_out_norm[l], w_out_ab[l])
            nk_s.append(k_all[:, -L_A:])
            nv_s.append(v_all[:, -L_A:])
            nh_s.append(ss)
        else:
            zeros_prev = jnp.zeros((hp.shape[0], CONV_WIDTH - 1, D_MODEL), hp.dtype)
            mix_p, cp = short_conv(rmsnorm(hp, norm_mix[layer]), w_in_c[l], conv_w[l], w_out_c[l], zeros_prev)
            mix_s, cs = short_conv(rmsnorm(hs, norm_mix[layer]), w_in_c[l], conv_w[l], w_out_c[l], state_conv[l])
            nc_p.append(cp)
            nc_s.append(cs)
        hp = hp + mix_p
        hs = hs + mix_s
        hp = hp + hier_moe(rmsnorm(hp, norm_ffn[layer]), w_group[layer], b_group[layer], w_expert[layer], b_expert[layer], w1[layer], w3[layer], w2[layer])
        hs = hs + hier_moe(rmsnorm(hs, norm_ffn[layer]), w_group[layer], b_group[layer], w_expert[layer], b_expert[layer], w1[layer], w3[layer], w2[layer])
    return (hp, hs, jnp.stack(nk_p), jnp.stack(nv_p), jnp.stack(nk_s), jnp.stack(nv_s),
            jnp.stack(nh_p), jnp.stack(nh_s), jnp.stack(nc_p), jnp.stack(nc_s))


_drawn_inputs = setup_inputs


def setup_inputs(seed=0):
    import zlib

    import numpy as np

    out = dict(_drawn_inputs(seed))
    spreads = {}
    factors = {}
    for name, (base, spread) in spreads.items():
        noise = np.random.default_rng([zlib.crc32(name.encode()), seed]).standard_normal(out[name].shape)
        drawn = base * np.exp(spread * noise) if base else spread * noise
        out[name] = __import__('jax').numpy.asarray(drawn.astype(out[name].dtype))
    for name, factor in factors.items():
        out[name] = (out[name] * factor).astype(out[name].dtype)
    return out
```

```python
from contextlib import ExitStack

import numpy as np
import concourse.bass as bass
from concourse import mybir

F32 = mybir.dt.float32
BF16 = mybir.dt.bfloat16
I32 = mybir.dt.int32
U32 = mybir.dt.uint32
ALU = mybir.AluOpType
ACT = mybir.ActivationFunctionType
AX = mybir.AxisListType

P = 128
D = 1024
KT = D // P
SEQ, DEC, PAST = 512, 32, 128
T = SEQ + DEC
NC = 5
ROWS = [128, 128, 128, 128, 32]
HALF = T // 2
NH, HD = 8, 64
DA = NH * HD
CH = 64
REL = 128
BLK = 16
NBLK = T // BLK
EPS = 1e-6
NG, EPG = 4, 8
NE = NG * EPG
DE = 256
CAP = 64
ROUNDS = -(-T // CAP)
NR = NG + NE
RKW = NE + 2
GROUPS = [3, 5, 6, 4, 0, 1, 2]
UNIT_END = [8, 16, 24, 29, 34, 39, 44]
MASKED = -1e30
DROP = 5000


def hmoe_step(nc, x_prompt, x_sample, cache_a_k, cache_a_v, state_hgrn, state_conv, norm_mix, norm_ffn,
              w_in_ab, w_out_ab, q_norm, k_norm, rel_bias, hgrn_lb_logits, hgrn_out_norm, w_in_c, conv_w,
              w_out_c, w_group, b_group, w_expert, b_expert, w1, w3, w2,
              y_prompt, y_sample, nk_p, nv_p, nk_s, nv_s, nh_p, nh_s, nconv_p, nconv_s):
    ctx = ExitStack()
    KB = 1024
    BASE = 16512

    def at(name, kb, shape, dt=F32):
        return nc.alloc_sbuf_tensor_at(name, shape, dt, offset=BASE + int(kb * KB))

    def sem(name):
        return ctx.enter_context(nc.semaphore(name))

    with ctx:
        H = at("H", 0, [P, NC, D])
        ident = at("ident", 20, [P, P])
        upper = at("upper", 20.5, [P, P])
        ones = at("ones", 21, [P, P])
        head_mean = at("head_mean", 21.5, [P, P])
        blk_mask = at("blk_mask", 22, [P, P])
        slot_no = at("slot_no", 22.5, [P, CAP])
        junk = at("junk", 22.75, [P, D], BF16)
        sm = 24.75
        def small(name, n, dt=F32):
            nonlocal sm
            t = at(name, sm, [P, n], dt)
            sm += -(-n * 4 // 32) * 32 / KB
            return t
        blk_sel = small("blk_sel", 4)
        even = small("even", 1)
        odd = small("odd", 1)
        frame_no = small("frame_no", NC)
        frame_ok = small("frame_ok", NC)
        rev4 = small("rev4", NG)
        rev8 = small("rev8", EPG)
        half_no = small("half_no", 1)
        epsc = small("epsc", 1)
        ssq = small("ssq", NC)
        rms = small("rms", NC)
        rstd = small("rstd", NC)
        lbl = small("lbl", 8)
        lbe = small("lbe", 8)
        lb = small("lb", 4)
        lbs = small("lbs", 4)
        onorm = small("onorm", 4)
        convw = small("convw", 3 * KT)
        qgain = small("qgain", HD)
        kgain = small("kgain", HD)
        hss = small("hss", 2 * NH)
        hms = small("hms", 2 * NH)
        hrs = small("hrs", 2 * NH)
        rsum = small("rsum", NC * NH)
        rinv = small("rinv", 2 * NH)
        nmaxs = small("nmaxs", NC * NH)
        dec = small("dec", 4 * NBLK)
        biasr = small("biasr", NR)
        cnt = small("cnt", 4)
        cnt_i = small("cnt_i", 2, I32)
        assert sm <= 28, sm
        gmix = at("gmix", 28, [P, D])
        gffn = at("gffn", 32, [P, D])
        RING = 36
        w13 = [at(f"w13_{s}", RING + 24 * s, [P, KT, 2, DE]) for s in range(4)]
        w2s = [at(f"w2_{s}", RING + 24 * s + 16, [P, 2, D]) for s in range(4)]
        XN = at("XN", 132, [P, NC, D])
        XT = at("XT", 152, [P, KT, T])
        MISC = 169
        wab = [at(f"wab{s}", RING + 16 * s, [P, KT, DA]) for s in range(3)]
        HI = RING + 48
        q_tok = at("q_tok", HI, [P, NC, DA])
        k_tok = at("k_tok", HI + 10, [P, NC, DA])
        kinT = at("kinT", HI + 20, [P, 4, T])
        koutT = at("koutT", HI + 28.5, [P, 4, T])
        qdecT = at("qdecT", HI + 37, [P, 4, T])
        fT = at("fT", 132, [P, 4, T])
        gateT = at("gateT", 140.5, [P, 4, T])
        kcT = at("kcT", 149, [P, 4, P])
        va = at("va", MISC, [P, NC, DA])
        vb = at("vb", MISC + 10, [P, NC, DA])
        qT = at("qT", MISC + 20, [P, 4, T])
        kT = at("kT", MISC + 28.5, [P, 4, T])
        bias = at("bias", 152, [P, NH, 512])
        zA = at("zA", MISC + 10, [P, 4, T])
        zB = at("zB", 132, [P, 4, T])
        reset = at("reset", MISC + 20, [P, T])
        st = [at(f"st{i}", RING + 9 * i, [P, 9, 4, HD]) for i in range(2)]
        kout = [at(f"kout{i}", RING + 18 + 2 * i, [P, DA]) for i in range(2)]
        vx = [at(f"vx{i}", RING + 22 + 4 * i, [P, NH, 2, HD]) for i in range(2)]
        am = [at(f"am{i}", RING + 30 + 4 * i, [P, 2, 4, P]) for i in range(2)]
        osq = at("osq", RING + 38, [P, 4, P])
        orms = at("orms", RING + 40, [P, 4, P])
        dS = at("dS", RING + 42, [P, 4, HD])
        sneg = [at(f"sneg{i}", HI + 2 * i, [P, 512]) for i in range(2)]
        pr = [at(f"pr{i}", HI + 4 + 2 * i, [P, 512]) for i in range(2)]
        prT = [at(f"prT{i}", HI + 8 + 2 * i, [P, 4, P]) for i in range(2)]
        oa = [at(f"oa{i}", HI + 12 + 2 * i, [P, DA]) for i in range(2)]
        kc = at("kc", HI + 16, [P, DA])
        vc = at("vc", HI + 18, [P, DA])
        qsq = [at(f"qsq{i}", MISC + 24 + 2 * i, [P, DA]) for i in range(2)]
        wo = [at(f"wo{s}", RING + 16 * s, [P, KT, 512]) for s in range(2)]
        wr = at("wr", MISC + 36.5, [P, KT, NR])
        lg = at("lg", MISC + 1.25, [P, NC, NR])
        rt = [at(f"rt{i}", MISC + 2 + 0.75 * i, [P, NC, NE]) for i in range(5)]
        m1 = at("m1", MISC + 5.75, [P, NC, NE])
        m2 = at("m2", MISC + 6.5, [P, NC, NE])
        rk = at("rk", MISC + 7.25, [P, NC, RKW])
        dv = at("dv", MISC + 8, [P, NC, RKW])
        c1 = [at(f"c{i}", MISC + 8.75 + i * 0.03125, [P, NC]) for i in range(8)]
        gate = [at(f"gate{i}", MISC + 9 + i * 0.03125, [P, NC]) for i in range(2)]
        seln = [at(f"sel{i}", MISC + 9.25 + 2.5 * i, [P, NC, 2, CAP]) for i in range(2)]
        xg = [at(f"xg{i}", MISC + 14.25 + 4 * i, [P, KT, 2, CAP]) for i in range(2)]
        sg = [at(f"sg{i}", MISC + 22.25 + 0.5 * i, [P, P]) for i in range(2)]
        hh = [at(f"hh{i}", MISC + 23.25 + 0.5 * i, [P, P]) for i in range(2)]
        hT = [at(f"hT{i}", MISC + 24.25 + 0.5 * i, [P, P]) for i in range(2)]
        ys = [at(f"ys{i}", MISC + 25.25 + 2 * i, [P, 512]) for i in range(2)]
        idx = [at(f"idx{i}", MISC + 29.25 + 0.03125 * i, [P, 1], I32) for i in range(4)]
        ya = [at(f"ya{i}", 132 + 8 * i, [P, D]) for i in range(2)]
        yb = [at(f"yb{i}", 136 + 8 * i, [P, D]) for i in range(2)]
        wc = [at(f"wc{s}", RING + 12 * s, [P, KT, 3, P]) for s in range(2)]
        woc0 = at("woc0", RING + 24, [P, KT, 512])
        woc1 = [at("woc1_lo", RING + 40, [P, KT // 2, 512]), at("woc1_hi", MISC + 27.5, [P, KT // 2, 512])]
        UW = 2 + SEQ + 2 + DEC
        gT = at("gT", MISC, [P, KT, T])
        u = at("u", MISC + 17, [P, UW])
        hc = [at(f"hc{i}", MISC + 21.5 + 1.25 * i, [P, HALF]) for i in range(2)]
        cv = at("cv", MISC + 24, [P, T])
        hist = at("hist", MISC + 26.25, [P, KT, 2])
        tails = at("tails", MISC + 26.5, [P, 2, KT, 2])

        bank = [ctx.enter_context(nc.psum_tensor(f"bank{i}", [P, 512], F32)) for i in range(8)]

        rev_dram = nc.dram_tensor("rev_bias", [NH, 640], F32, kind="Internal").ap()
        revs_dram = nc.dram_tensor("rev_bias_copies", [NH, 32, 640], F32, kind="Internal").ap()
        y_dram = [nc.dram_tensor(f"y_rows{i}", [2 * T * 2, 512], F32, kind="Internal").ap() for i in range(2)]

        x_in = sem("x_in"); gmix_in = sem("gmix_in"); gffn_in = sem("gffn_in"); tab_in = sem("tab_in");
        pool_c = sem("pool_c"); const_ok = sem("const_ok")
        h_ok = sem("h_ok")
        sq_done = sem("sq_done"); ms_ok = sem("ms_ok"); rt_ok = sem("rt_ok")
        xn_ok = sem("xn_ok"); xt_mm = sem("xt_mm"); xt_a = sem("xt_a"); xt_d = sem("xt_d")
        dch = sem("dch"); ach = sem("ach")
        wab_in = [sem(f"wab_in{s}") for s in range(3)]
        z_mm = sem("z_mm"); z_free = [sem(f"z_free{b}") for b in range(4)]

        f_ok = sem("f_ok"); ln_ok = sem("ln_ok"); cum_ok = sem("cum_ok"); exp_ok = sem("exp_ok")
        hg_ok = sem("hg_ok")
        qsq_ok = sem("qsq_ok"); qms_ok = sem("qms_ok"); qrt_ok = sem("qrt_ok"); qk_ok = sem("qk_ok")
        v_ok = sem("v_ok"); out_dma = sem("out_dma"); qkT_mm = sem("qkT_mm"); qkT_ok = sem("qkT_ok")
        rb_dma = sem("rb_dma"); rc_dma = sem("rc_dma"); bias_in = sem("bias_in");
        cache_in = sem("cache_in"); kc_mm = sem("kc_mm"); kc_ok = sem("kc_ok"); st_in = sem("st_in")
        ko_mm = sem("ko_mm"); ko_ok = sem("ko_ok"); vx_ok = sem("vx_ok"); a_mm = sem("a_mm"); a_ok = sem("a_ok")
        u_mm = sem("u_mm"); st_ok = sem("st_ok"); o_mm = sem("o_mm"); osq_ok = sem("osq_ok")
        stat_mm = sem("stat_mm"); orms_ok = sem("orms_ok"); zB_ok = sem("zB_ok")
        s_mm = sem("s_mm"); s_ok = sem("s_ok"); p_ok = sem("p_ok"); pT_mm = sem("pT_mm")
        pT_a = sem("pT_a"); pT_d = sem("pT_d"); pv_mm = sem("pv_mm"); oa_ok = sem("oa_ok")
        oaT_mm = sem("oaT_mm"); zA_ok = sem("zA_ok")
        wo_in = [sem(f"wo_in{s}") for s in range(2)]
        op_mm = sem("op_mm"); op_add = sem("op_add")
        wr_in = sem("wr_in"); lg_mm = sem("lg_mm"); lg_ok = sem("lg_ok"); ge_ok = sem("ge_ok"); gx_ok = sem("gx_ok")
        e2_ok = sem("e2_ok"); ex_ok = sem("ex_ok")
        msk_ok = sem("msk_ok"); rk_mm = sem("rk_mm"); rk_ok = sem("rk_ok"); cm_mm = sem("cm_mm"); cnt_ok = sem("cnt_ok")
        w13_in = [sem(f"w13_in{s}") for s in range(4)]
        w2_in = [sem(f"w2_in{s}") for s in range(4)]
        sel_ok = sem("sel_ok"); g_mm = sem("g_mm"); ix_mm = sem("ix_mm"); xg_a = sem("xg_a"); xg_d = sem("xg_d")
        ix_ok = sem("ix_ok"); h_mm = sem("h_mm"); sg_ok = sem("sg_ok"); hh_ok = sem("hh_ok"); t_mm = sem("t_mm")
        ht_ok = sem("ht_ok"); y_mm = sem("y_mm"); ys_ok = sem("ys_ok"); scat = sem("scat")
        yab_in = [sem(f"yab_in{i}") for i in range(2)]

        ov = [{n: sem(f"ov{l}_{n}") for n in ("free", "w", "rk", "sel", "g", "xg", "ixm", "ix", "h", "sg", "hh", "t", "ht", "y", "ys", "sc")}
              for l in range(2)]
        wc_in = [sem(f"wc_in{s}") for s in range(2)]
        c_mm = sem("c_mm"); hc_ok = sem("hc_ok"); cg_ok = sem("cg_ok"); tail_ok = sem("tail_ok")
        lbm_ok = sem("lbm_ok"); lbe_ok = sem("lbe_ok"); st0_ok = sem("st0_ok"); ys_free = sem("ys_free")
        woc_in = [sem(f"woc_in{s}") for s in range(2)]
        y_out = sem("y_out")

        NXT = 2 * NC
        PAIRS = NE // 2

        block = ctx.enter_context(nc.Block())


        class Chain:
            def __init__(self, eng, done):
                self.eng, self.done, self.n, self.run_on = eng, done, 0, 0

            def __call__(self, ins):
                self.n += 1
                ins.then_inc(self.done, 1)
                self.eng.wait_ge(self.done, self.n + self.run_on)

            def loop(self, i, steps, times):
                self.run_on, self.steps, self.times, self.first = i * steps, steps, times, self.n

            def end(self):
                assert self.n == self.first + self.steps, (self.n - self.first, self.steps)
                self.n, self.run_on = self.first + self.steps * self.times, 0

        def bc(ap, shape):
            return ap.to_broadcast(shape)

        @block.sync
        def _(sp):
            for c in range(4):
                sp.dma_start(H[:, c, :], x_prompt[0, c * P:(c + 1) * P, :]).then_inc(x_in, 16)
            sp.dma_start(H[0:DEC, 4, :], x_sample[0, :, :]).then_inc(x_in, 16)
            sp.dma_start(gmix[:], norm_mix[0:1, :].partition_broadcast(P)).then_inc(gmix_in, 16)

            def group_load(n):
                g = GROUPS[n]
                sp.dma_start(wab[n % 3][:], w_in_ab[0, :, g * DA:(g + 1) * DA].rearrange("(k p) n -> p k n", p=P))\
                    .then_inc(wab_in[n % 3], 16)
            for n in range(3):
                group_load(n)
            with nc.allow_non_contiguous_dma(reason="per-feature tables, one element per partition"):
                sp.dma_start(lbl[:].rearrange("p (r m) -> p r m", r=2), hgrn_lb_logits.rearrange("r (m p) -> p r m", p=P)).then_inc(tab_in, 16)
                sp.dma_start(onorm[:], hgrn_out_norm[0].rearrange("(m p) -> p m", p=P)).then_inc(tab_in, 16)
                sp.dma_start(convw[:].rearrange("p (j k) -> p j k", j=3), conv_w[0].rearrange("j (k p) -> p j k", p=P)).then_inc(tab_in, 16)
                sp.dma_start(rev_dram[:, 384:639].unsqueeze(2), bass.AP(rel_bias.tensor, 2 * REL - 1, [[2 * REL + 1, NH], [-1, 255], [1, 1]])).then_inc(rb_dma, 16)
                sp.dma_start(rev_dram[:, 0:384].unsqueeze(2), bass.AP(rel_bias.tensor, 2 * REL, [[2 * REL + 1, NH], [0, 384], [1, 1]])).then_inc(rb_dma, 16)
            sp.dma_start(qgain[:], q_norm[0:1, :].partition_broadcast(P)).then_inc(tab_in, 16)
            sp.dma_start(kgain[:], k_norm[0:1, :].partition_broadcast(P)).then_inc(tab_in, 16)
            sp.dma_start(gffn[:], norm_ffn[0:1, :].partition_broadcast(P)).then_inc(gffn_in, 16)
            for n in range(3, 7):
                sp.wait_ge(z_mm, UNIT_END[n - 3])
                group_load(n)
            sp.wait_ge(rb_dma, 32)
            sp.dma_start(revs_dram[:, :, 0:639], bc(rev_dram[:, 0:639].unsqueeze(1), [NH, 32, 639])).then_inc(rc_dma, 16)
            sp.dma_start(nk_s[0, 0, 0:PAST - DEC], cache_a_k[0, 0, DEC:]).then_inc(out_dma, 16)
            sp.dma_start(nv_s[0, 0, 0:PAST - DEC], cache_a_v[0, 0, DEC:]).then_inc(out_dma, 16)
            sp.wait_ge(qk_ok, 2 * NC)
            sp.dma_start(nk_p[0, 0].rearrange("(c p) h d -> p c (h d)", p=P), k_tok[:, 0:4, :]).then_inc(out_dma, 16)
            sp.dma_start(nk_s[0, 0, PAST - DEC:].rearrange("t h d -> t (h d)"), k_tok[0:DEC, 4, :]).then_inc(out_dma, 16)
            sp.wait_ge(rc_dma, 16)
            sp.wait_ge(z_mm, UNIT_END[-1])
            for a in range(4):
                sp.dma_start(bias[32 * a:32 * a + 32, :, :],
                             bass.AP(revs_dram.tensor, P - 1 - 32 * a, [[639, 32], [32 * 640, NH], [1, 512]])).then_inc(bias_in, 16)
            sp.wait_ge(v_ok, NC)
            sp.dma_start(nv_p[0, 0].rearrange("(c p) h d -> p c (h d)", p=P), va[:, 0:4, :]).then_inc(out_dma, 16)
            sp.dma_start(nv_s[0, 0, PAST - DEC:].rearrange("t h d -> t (h d)"), va[0:DEC, 4, :]).then_inc(out_dma, 16)
            sp.wait_ge(qkT_mm, 2 * NC)
            sp.wait_ge(out_dma, 16 * 6)
            sp.dma_start(kc[:], cache_a_k[0, 0].rearrange("t h d -> t (h d)")).then_inc(cache_in, 16)
            sp.dma_start(vc[:], cache_a_v[0, 0].rearrange("t h d -> t (h d)")).then_inc(cache_in, 16)
            sp.wait_ge(o_mm, 3)
            sp.wait_ge(st_ok, 4)
            sp.dma_start(st[0][:, 0, :, :], state_hgrn[0, 0].rearrange("(a b) k v -> (b k) a v", b=2)).then_inc(st_in, 16)
            sp.dma_start(nh_p[0, 0].rearrange("(a b) k v -> (b k) a v", b=2), st[1][:, 8, :, :]).then_inc(out_dma, 16)
            sp.wait_ge(st_ok, 5)
            sp.dma_start(nh_s[0, 0].rearrange("(a b) k v -> (b k) a v", b=2), st[0][:, 2, :, :]).then_inc(out_dma, 16)
            sp.wait_ge(zB_ok, NC)
            sp.wait_ge(out_dma, 16 * 8)
            for s in range(2):
                sp.dma_start(wo[s][:], w_out_ab[0, :, s * 512:(s + 1) * 512].rearrange("(k p) n -> p k n", p=P)).then_inc(wo_in[s], 16)

            def w13_load(l, e, s, done):
                for part, w in enumerate((w1, w3)):
                    sp.dma_start(w13[s][:, :, part, :], w[l, bass.ds(e, 1)].rearrange("e (k p) f -> p (e k) f", p=P)).then_inc(done, 16)

            def w2_load(l, e, s, done):
                sp.dma_start(w2s[s][:], w2[l, bass.ds(e, 1)].rearrange("e (a p) n -> p (e a) n", p=P)).then_inc(done, 16)

            def first_load(l, j):
                s = (j + 2) % 4
                w13_load(l, j, s, w13_in[s])
                w2_load(l, j, s, w2_in[s])

            def router_load(l):
                sp.dma_start(wr[:, :, 0:NG], w_group[l].rearrange("(k p) n -> p k n", p=P)).then_inc(wr_in, 16)
                sp.dma_start(wr[:, :, NG:NR], w_expert[l].rearrange("(k p) n -> p k n", p=P)).then_inc(wr_in, 16)
                sp.dma_start(biasr[:, 0:NG], b_group[l:l + 1, :].partition_broadcast(P)).then_inc(wr_in, 16)
                sp.dma_start(biasr[:, NG:NR], b_expert[l:l + 1, :].partition_broadcast(P)).then_inc(wr_in, 16)

            def mixture(l):
                with sp.Fori(0, NE // 4 - 1) as i:
                    for j in range(4):
                        s = (j + 2) % 4
                        sp.wait_ge(h_mm, i * 4 + (l * NE + j + 1))
                        w13_load(l, 4 * i + 4 + j, s, w13_in[s])
                        sp.wait_ge(y_mm, i * 4 + (l * NE + j + 1))
                        w2_load(l, 4 * i + 4 + j, s, w2_in[s])
                sp.wait_ge(y_mm, NE * (l + 1))
                sp.wait_ge(cnt_ok, l + 1)
                sp.wait_ge(scat, 16 * NE * (l + 1))
                most = sp.value_load(cnt_i[0:1, l:l + 1], min_val=0, max_val=T)
                with sp.Fori(0, ROUNDS - 1) as r:
                    with sp.If(most > CAP * r + CAP):
                        with sp.Fori(0, NE) as e:
                            sp.wait_ge(ov[l]["free"], r * NE + e + 1)
                            w13_load(l, e, 0, ov[l]["w"])
                            w2_load(l, e, 0, ov[l]["w"])
                        sp.wait_ge(ov[l]["free"], r * NE + NE + 1)
                        sp.nop(nofuse=True)
                rows = y_dram[l].rearrange("(r b) d -> r (b d)", b=2)
                for c in range(NC):
                    if c >= 2:
                        sp.wait_ge(h_ok, NC * (2 * l + 1) + c - 1)
                    for i, buf in enumerate((ya, yb)):
                        first = i * T + c * P
                        sp.dma_start(buf[c % 2][0:ROWS[c], :], rows[first:first + ROWS[c], :]).then_inc(yab_in[c % 2], 16)

            sp.wait_ge(zA_ok, NC)
            router_load(0)
            first_load(0, 0)
            first_load(0, 1)
            sp.wait_ge(op_mm, 2 * NC)
            first_load(0, 2)
            first_load(0, 3)
            sp.wait_ge(xn_ok, NC)
            sp.dma_start(gmix[:], norm_mix[1:2, :].partition_broadcast(P)).then_inc(gmix_in, 16)
            mixture(0)

            wcv = w_in_c[0].rearrange("(k p) (a m n) -> a m p k n", p=P, a=3, n=P)

            def conv_load(m, s):
                for a in range(3):
                    sp.dma_start(wc[s][:, :, a, :], wcv[a, bass.ds(m, 1)].rearrange("m p k n -> p (m k) n")).then_inc(wc_in[s], 16)
            for s in range(2):
                conv_load(s, s)
            sp.wait_ge(xn_ok, 2 * NC)
            sp.dma_start(gffn[:], norm_ffn[1:2, :].partition_broadcast(P)).then_inc(gffn_in, 16)
            sp.wait_ge(lg_ok, 1)
            sp.wait_ge(lg_mm, 1)
            router_load(1)
            with nc.allow_non_contiguous_dma(reason="two frames of each feature"):
                for r in range(2):
                    sp.dma_start(hist[:, :, r], state_conv[0, 0, r].rearrange("(k p) -> p k", p=P)).then_inc(st_in, 16)
            sp.dma_start(woc0[:], w_out_c[0, :, 0:512].rearrange("(k p) n -> p k n", p=P)).then_inc(woc_in[0], 16)
            w_out_hi = w_out_c[0, :, 512:1024].rearrange("(i k p) n -> i p k n", i=2, p=P)
            for i in range(2):
                sp.dma_start(woc1[i][:], w_out_hi[i]).then_inc(woc_in[1], 16)
            with sp.Fori(0, KT // 2 - 1) as i:
                for s in range(2):
                    sp.wait_ge(c_mm, i * 4 + (2 * s + 2))
                    conv_load(2 * i + (2 + s), s)
            sp.wait_ge(tail_ok, KT)
            with nc.allow_non_contiguous_dma(reason="two frames of each feature"):
                for j, dst in enumerate((nconv_p, nconv_s)):
                    for r in range(2):
                        sp.dma_start(dst[0, 0, r, :].rearrange("(k p) -> p k", p=P), tails[:, j, :, r]).then_inc(out_dma, 16)
            first_load(1, 1)
            sp.wait_ge(op_mm, 4 * NC)
            for j in (0, 2, 3):
                first_load(1, j)
            mixture(1)
            for c in range(NC):
                sp.wait_ge(h_ok, 3 * NC + c + 1)
                dst = y_prompt[0, c * P:(c + 1) * P, :] if c < 4 else y_sample[0, :, :]
                sp.dma_start(dst, H[0:ROWS[c], c, :]).then_inc(y_out, 16)
            sp.wait_ge(y_out, 16 * NC)
            sp.wait_ge(out_dma, 16 * 12)

        @block.gpsimd
        def _(pool):
            tie = Chain(pool, pool_c)

            def tri(t, view, pattern, base, mult, op, fill=0.0):
                tie(pool.affine_select(out=view, in_=view, compare_op=op, fill=fill, base=base, pattern=pattern,
                                       channel_multiplier=mult))
            tie(pool.memset(H[32:64, 4, :], 0.0))
            tie(pool.memset(H[64:128, 4, :], 0.0))
            tie(pool.memset(ident[:], 0.0))
            tri(ident, ident[:], [[-1, P]], 0, 1, ALU.not_equal, 1.0)
            tie(pool.memset(upper[:], 1.0))
            tri(upper, upper[:], [[1, P]], 0, -1, ALU.is_gt)
            tie(pool.memset(ones[:], 1.0))
            tie(pool.memset(head_mean[:], 0.0))
            tie(pool.memset(head_mean[0:HD, 0:HD], 1.0 / HD))
            tie(pool.memset(head_mean[HD:P, HD:P], 1.0 / HD))
            tie(pool.memset(blk_mask[:], 1.0))
            tri(blk_mask, blk_mask[:], [[1, P]], 0, -1, ALU.is_ge)
            tri(blk_mask, blk_mask[:].rearrange("p (b t) -> p b t", t=BLK), [[-BLK, P // BLK], [0, BLK]], 0, 1, ALU.is_ge)
            tie(pool.memset(blk_sel[:], 1.0))
            tri(blk_sel, blk_sel[:], [[-32, 4]], 0, 1, ALU.is_ge)
            tri(blk_sel, blk_sel[:], [[32, 4]], BLK - 1, -1, ALU.is_ge)
            tie(pool.iota(slot_no[:], [[1, CAP]], base=0, channel_multiplier=0, allow_small_or_imprecise_dtypes=True))
            tie(pool.iota(frame_no[:], [[P, NC]], base=0, channel_multiplier=1, allow_small_or_imprecise_dtypes=True))
            tie(pool.iota(rev4[:], [[-1, NG]], base=NG, channel_multiplier=0, allow_small_or_imprecise_dtypes=True))
            tie(pool.iota(rev8[:], [[-1, EPG]], base=EPG, channel_multiplier=0, allow_small_or_imprecise_dtypes=True))
            tie(pool.memset(frame_ok[:], 1.0))
            tri(frame_ok, frame_ok[:], [[-P, NC]], T - 1, -1, ALU.is_ge)
            tie(pool.memset(epsc[:], EPS))
            tie(pool.memset(reset[:], 1.0))
            tie(pool.memset(reset[:].rearrange("p (b t) -> p b t", t=BLK)[:, :, 0], 0.0))
            pool.nop().then_inc(const_ok, 1)
            pool.nop().then_inc(ys_free, 2)

            for l in range(2):
                yd = y_dram[l]

                def scatter(i, done):
                    pool.indirect_dma_start(yd[:, :], bass.IndirectOffsetOnAxis(ap=idx[i][:, 0:1].bitcast(U32), axis=0),
                                            ys[i % 2][:, :], None, bounds_check=4 * T - 1, oob_is_err=False).then_inc(done, 16)
                with pool.Fori(0, NE // 4) as i:
                    for j in range(4):
                        pool.wait_ge(ix_ok, i * 2 + (l * (PAIRS + 1) + j // 2 + 1))
                        pool.wait_ge(ys_ok, i * 4 + (l * NE + j + 3))
                        pool.nop(nofuse=True)
                        scatter(j, scat)
                        pool.wait_ge(scat, i * 64 + 16 * (l * NE + j + 1))
                        pool.nop().then_inc(ys_free, 1)
                pool.wait_ge(cnt_ok, l + 1)
                most = pool.value_load(cnt_i[0:1, l:l + 1], min_val=0, max_val=T)
                o = ov[l]
                pool.nop().then_inc(o["free"], 1)
                with pool.Fori(0, ROUNDS - 1) as r:
                    with pool.If(most > CAP * r + CAP):
                        with pool.Fori(0, NE) as e:
                            pool.wait_ge(o["ix"], r * NE + e + 1)
                            pool.wait_ge(o["ys"], r * NE + e + 1)
                            pool.nop(nofuse=True)
                            scatter(0, o["sc"])
                            pool.wait_ge(o["sc"], r * (16 * NE) + e * 16 + 16)
                            pool.nop().then_inc(o["free"], 1)

        @block.tensor
        def _(pe):
            def norm_transposes(n):
                for c in range(NC):
                    pe.wait_ge(xn_ok, NC * n + c + 1)
                    if n == 0 and c == 0:
                        pe.wait_ge(const_ok, 1)
                    for half in range(2):
                        step = NXT * n + 2 * c + half
                        if c > 0:
                            pe.wait_ge(xt_a if half == 0 else xt_d, NC * n + c)
                        for kk in range(4):
                            k = 4 * half + kk
                            last = pe.transpose(bank[6 + half][:, kk * P:kk * P + ROWS[c]], XN[0:ROWS[c], c, k * P:(k + 1) * P],
                                                ident[0:ROWS[c], 0:ROWS[c]])
                        last.then_inc(xt_mm, 1)

            norm_transposes(0)
            pe.wait_ge(xt_a, NC)
            pe.wait_ge(xt_d, NC)
            u_ = 0
            for n in range(7):
                pe.wait_ge(wab_in[n % 3], 16 * (n // 3 + 1))
                w = wab[n % 3]
                for a in range(8 if n < 3 else NC):
                    if u_ >= 4:
                        pe.wait_ge(z_free[u_ % 4], u_ // 4)
                    for k in range(KT):
                        if n < 3:
                            m, half = a // 2, a % 2
                            last = pe.matmul(bank[u_ % 4][:, 0:HALF], w[:, k, m * P:(m + 1) * P],
                                             XT[:, k, half * HALF:(half + 1) * HALF], start=k == 0, stop=k == KT - 1)
                        else:
                            last = pe.matmul(bank[u_ % 4][0:ROWS[a], :], XT[:, k, a * P:a * P + ROWS[a]], w[:, k, :],
                                             start=k == 0, stop=k == KT - 1)
                    last.then_inc(z_mm, 1)
                    u_ += 1
            for i in range(2 * NC):
                c, src = i // 2, (q_tok, k_tok)[i % 2]
                if i == 0:
                    pe.wait_ge(qk_ok, 2 * NC)
                if i >= 2:
                    pe.wait_ge(qkT_ok, i - 1)
                for m in range(4):
                    last = pe.transpose(bank[4 + i % 2][:, m * P:m * P + ROWS[c]], src[0:ROWS[c], c, m * P:(m + 1) * P],
                                        ident[0:ROWS[c], 0:ROWS[c]])
                last.then_inc(qkT_mm, 1)

            def hgrn_in(c):
                n, t0 = ROWS[c], c * P
                if c == 0:
                    pe.wait_ge(hg_ok, 3)
                    for b in range(4):
                        pe.wait_ge(z_free[b], 11)
                    pe.wait_ge(qkT_ok, 2 * NC)
                else:
                    pe.wait_ge(orms_ok, c - 1) if c > 1 else None
                for m in range(4):
                    last = pe.transpose(bank[0][0:n, m * P:(m + 1) * P], koutT[:, m, t0:t0 + n], ident[:])
                last.then_inc(ko_mm, 1)
                if c > 0:
                    pe.wait_ge(a_ok, 2 * c)
                for par in range(2):
                    for m in range(4):
                        last = pe.matmul(bank[1 + par][0:n, m * P:m * P + n], kinT[64 * par:64 * par + 64, m, t0:t0 + n],
                                         qdecT[64 * par:64 * par + 64, m, t0:t0 + n], start=True, stop=True)
                last.then_inc(a_mm, 1)
                pe.wait_ge(ko_ok, c + 1)
                pe.wait_ge(vx_ok, c + 1)
                if c > 0:
                    pe.wait_ge(st_ok, c)
                for r in range(n // 32):
                    for h in range(NH):
                        last = pe.matmul(bank[3 + r][64 * (h % 2):64 * (h % 2) + 64, (h // 2) * P:(h // 2 + 1) * P],
                                         kout[c % 2][32 * r:32 * r + 32, h * HD:(h + 1) * HD],
                                         vx[c % 2][32 * r:32 * r + 32, h, :, :].rearrange("p i v -> p (i v)"), start=True, stop=True)
                last.then_inc(u_mm, 1)

            def hgrn_out(c):
                n, t0 = ROWS[c], c * P
                pe.wait_ge(a_ok, 2 * c + 2)
                pe.wait_ge(st_ok, c + 1)
                if c > 0:
                    pe.wait_ge(zB_ok, c)
                for m in range(4):
                    for par in range(2):
                        h, lo = 2 * m + par, 64 * par
                        out = bank[7][lo:lo + 64, m * P:m * P + n]
                        pe.matmul(out, vb[0:n, c, h * HD:(h + 1) * HD], am[c % 2][0:n, par, m, 0:n], start=True, stop=False)
                        for b in range(n // BLK):
                            last = pe.matmul(out[:, b * BLK:(b + 1) * BLK], st[c % 2][lo:lo + 64, b, m, :],
                                             qdecT[lo:lo + 64, m, t0 + b * BLK:t0 + (b + 1) * BLK],
                                             start=False, stop=b == n // BLK - 1)
                last.then_inc(o_mm, 1)
                pe.wait_ge(osq_ok, c + 1)
                pe.wait_ge(ko_ok, min(c + 2, NC))
                for m in range(4):
                    last = pe.matmul(bank[0][:, m * P:m * P + n], head_mean[:], osq[:, m, 0:n], start=True, stop=True)
                last.then_inc(stat_mm, 1)

            hgrn_in(0)
            for c in range(NC):
                if c + 1 < NC:
                    hgrn_in(c + 1)
                hgrn_out(c)

            NU = NC * NH
            pe.wait_ge(cache_in, 32)
            pe.wait_ge(zB_ok, NC)
            pe.wait_ge(orms_ok, NC)
            for m in range(4):
                last = pe.transpose(bank[6][:, m * P:(m + 1) * P], kc[:, m * P:(m + 1) * P], ident[:])
            last.then_inc(kc_mm, 1)

            def scores(i):
                c, h = divmod(i, NH)
                lo, m = 64 * (h % 2), h // 2
                if i >= 2:
                    pe.wait_ge(s_ok, i - 1)
                q = qT[lo:lo + 64, m, c * P:c * P + ROWS[c]]
                if c < 4:
                    last = pe.matmul(bank[i % 2][:, 0:P * (c + 1)], q, kT[lo:lo + 64, m, 0:P * (c + 1)], start=True, stop=True)
                else:
                    pe.matmul(bank[i % 2][0:DEC, 0:PAST], q, kcT[lo:lo + 64, m, :], start=True, stop=True)
                    last = pe.matmul(bank[i % 2][0:DEC, PAST:PAST + DEC], q, kT[lo:lo + 64, m, SEQ:T], start=True, stop=True)
                last.then_inc(s_mm, 1)

            def keys(c):
                return [(P * j, P) for j in range(c + 1)] if c < 4 else [(0, PAST), (PAST, DEC)]

            def probs_T(i):
                c, h = divmod(i, NH)
                n = ROWS[c]
                pe.wait_ge(p_ok, i + 1)
                if i >= 2:
                    pe.wait_ge(pT_a if i % 2 == 0 else pT_d, i // 2)
                for j, (k0, nk) in enumerate(keys(c)):
                    last = pe.transpose(bank[2 + i % 2][0:nk, j * P:j * P + n], pr[i % 2][0:n, k0:k0 + nk], ident[0:n, 0:n])
                last.then_inc(pT_mm, 1)

            def values(i):
                c, h = divmod(i, NH)
                n = ROWS[c]
                pe.wait_ge(pT_a if i % 2 == 0 else pT_d, i // 2 + 1)
                if h == 0 and c >= 2:
                    pe.wait_ge(oa_ok, c - 1)
                for j, (k0, nk) in enumerate(keys(c)):
                    v = va[:, j, :] if c < 4 else (vc[:, :], va[0:DEC, 4, :])[j]
                    last = pe.matmul(bank[4 + c % 2][0:n, h * HD:(h + 1) * HD], prT[i % 2][0:nk, j, 0:n],
                                     v[:, h * HD:(h + 1) * HD], start=j == 0, stop=j == len(keys(c)) - 1)
                last.then_inc(pv_mm, 1)

            def heads_T(c):
                n = ROWS[c]
                pe.wait_ge(oa_ok, c + 1)
                pe.wait_ge(kc_ok, 1) if c == 0 else pe.wait_ge(zA_ok, c)
                for m in range(4):
                    last = pe.transpose(bank[6][:, m * P:m * P + n], oa[c % 2][0:n, m * P:(m + 1) * P], ident[0:n, 0:n])
                last.then_inc(oaT_mm, 1)

            pe.wait_ge(kc_ok, 1)
            for i in range(NU + 4):
                if i < NU:
                    scores(i)
                if 1 <= i <= NU:
                    probs_T(i - 1)
                if 2 <= i <= NU + 1:
                    values(i - 2)
                if i >= 11 and (i - 11) % NH == 0:
                    heads_T((i - 11) // NH)
            pe.wait_ge(zA_ok, NC)

            def project_out(n, lhsT, rhs, arrived):
                for i in range(2 * NC):
                    c, s = i // 2, i % 2
                    if c == 0:
                        for a in arrived[s]:
                            pe.wait_ge(*a)
                    if i >= 4:
                        pe.wait_ge(op_add, 2 * NC * n + i - 3)
                    for k in range(KT):
                        last = pe.matmul(bank[i % 4][0:ROWS[c], :], lhsT(k, c), rhs(k, s), start=k == 0, stop=k == KT - 1)
                    last.then_inc(op_mm, 1)

            def z_ab(k, c):
                return (zA if k < 4 else zB)[:, k % 4, c * P:c * P + ROWS[c]]
            project_out(0, z_ab, lambda k, s: wo[s][:, k, :], [[(wo_in[0], 16)], [(wo_in[1], 16)]])

            def mixture(l):
                norm_transposes(2 * l + 1)
                pe.wait_ge(xt_a, NC * (2 * l + 2))
                pe.wait_ge(xt_d, NC * (2 * l + 2))
                pe.wait_ge(op_add, 2 * NC * (l + 1))
                pe.wait_ge(wr_in, 64 * (l + 1))
                for c in range(NC):
                    for k in range(KT):
                        last = pe.matmul(bank[0][0:ROWS[c], c * NR:(c + 1) * NR], XT[:, k, c * P:c * P + ROWS[c]], wr[:, k, :],
                                         start=k == 0, stop=k == KT - 1)
                last.then_inc(lg_mm, 1)
                pe.wait_ge(msk_ok, l + 1)
                for c in range(NC):
                    for b in range(c + 1):
                        last = pe.matmul(bank[1][:, c * NE:(c + 1) * NE], (ones if b < c else upper)[:], rt[0][:, b, :],
                                         start=b == 0, stop=b == c)
                last.then_inc(rk_mm, 1)
                pe.wait_ge(rk_ok, l + 1)
                pe.matmul(bank[2][0:1, 0:P], c1[7][:, 0:1], ident[:], start=True, stop=True).then_inc(cm_mm, 1)

                def gather(p, q):
                    for k in range(KT):
                        for c in range(NC):
                            last = pe.matmul(bank[k // 4][:, (k % 4) * P:(k % 4 + 1) * P], XN[:, c, k * P:(k + 1) * P],
                                             seln[p % 2][:, c, :, :].rearrange("p a s -> p (a s)"), start=c == 0, stop=c == NC - 1)
                    last.then_inc(q["g"], 1)

                def numbers(p, e, q):
                    for c in range(NC):
                        last = pe.matmul(bank[2][:, 0:2], seln[p % 2][:, c, :, :].rearrange("p a s -> p (a s)"),
                                         dv[:, c, bass.ds(e, 2)], start=c == 0, stop=c == NC - 1)
                    last.then_inc(q["ixm"], 1)

                def hidden(s, buf, ab, hb, q):
                    for k in range(KT):
                        for f in range(2):
                            last = pe.matmul(bank[hb][64 * f:64 * f + 64, 0:2 * P].rearrange("p (w j) -> p w j", w=2), xg[buf][:, k, ab, :],
                                             w13[s][:, k, :, f * P:(f + 1) * P], start=k == 0, stop=k == KT - 1)
                    last.then_inc(q["h"], 1)

                def hidden_T(ab, q):
                    pe.transpose(bank[5][:, ab * P:(ab + 1) * P], hh[ab][:], ident[:]).then_inc(q["t"], 1)

                def rows_out(s, ab, q):
                    for f in range(2):
                        for n in range(2):
                            last = pe.matmul(bank[6 + ab][64 * n:64 * n + 64, :], hT[ab][:, 64 * f:64 * f + 64],
                                             w2s[s][:, f, n * 512:(n + 1) * 512], start=f == 0, stop=f == 1)
                    last.then_inc(q["y"], 1)

                q = dict(g=g_mm, ixm=ix_mm, h=h_mm, t=t_mm, y=y_mm)
                G = l * (PAIRS + 1)
                E = l * NE
                pe.wait_ge(sel_ok, G + 1)
                gather(0, q)
                pe.wait_ge(cnt_ok, l + 1)
                numbers(0, 0, q)
                with pe.Fori(0, NE // 4) as i:
                    for p in range(2):
                        sl = [(2 * p + ab + 2) % 4 for ab in range(2)]
                        pe.wait_ge(xg_a, i * 2 + (G + p + 1))
                        pe.wait_ge(xg_d, i * 2 + (G + p + 1))
                        for ab in range(2):
                            pe.wait_ge(w13_in[sl[ab]], i * 32 + 32 * (8 * l + 1))
                            pe.wait_ge(hh_ok, i * 4 + (E + 2 * p + ab + 1))
                            hidden(sl[ab], p, ab, 3 + ab, q)
                        pe.wait_ge(hh_ok, i * 4 + (E + 2 * p + 3))
                        hidden_T(0, q)
                        pe.wait_ge(sel_ok, i * 2 + (G + p + 2))
                        gather(p + 1, q)
                        pe.wait_ge(ix_ok, i * 2 + (G + p + 1))
                        numbers(p + 1, 4 * i + (2 * p + 2), q)
                        pe.wait_ge(hh_ok, i * 4 + (E + 2 * p + 4))
                        pe.wait_ge(ht_ok, i * 4 + (E + 2 * p + 1))
                        hidden_T(1, q)
                        for ab in range(2):
                            pe.wait_ge(ht_ok, i * 4 + (E + 2 * p + ab + 1))
                            pe.wait_ge(w2_in[sl[ab]], i * 16 + 16 * (8 * l + 1))
                            pe.wait_ge(ys_ok, i * 4 + (E + 2 * p + ab + 1))
                            rows_out(sl[ab], ab, q)
                pe.wait_ge(ys_ok, NE * (l + 1) + 2)
                pe.wait_ge(xg_a, (l + 1) * (PAIRS + 1))
                pe.wait_ge(xg_d, (l + 1) * (PAIRS + 1))
                pe.wait_ge(ix_ok, (l + 1) * (PAIRS + 1))
                most = pe.value_load(cnt_i[0:1, l:l + 1], min_val=0, max_val=T)
                o = ov[l]
                with pe.Fori(0, ROUNDS - 1) as r:
                    with pe.If(most > CAP * r + CAP):
                        with pe.Fori(0, NE) as e:
                            n = r * NE + e
                            pe.wait_ge(o["sel"], n + 1)
                            gather(0, o)
                            numbers(0, e, o)
                            pe.wait_ge(o["xg"], n + 1)
                            pe.wait_ge(o["w"], n * 48 + 48)
                            hidden(0, 0, 0, 3, o)
                            pe.wait_ge(o["hh"], n + 1)
                            hidden_T(0, o)
                            pe.wait_ge(o["ht"], n + 1)
                            rows_out(0, 0, o)
            mixture(0)

            norm_transposes(2)
            pe.wait_ge(xt_a, NC * 3)
            pe.wait_ge(xt_d, NC * 3)
            with pe.Fori(0, KT // 2) as i:
                for s in range(2):
                    pe.wait_ge(wc_in[s], i * 48 + 48)
                    for half in range(2):
                        pe.wait_ge(cg_ok, i * 4 + (2 * s + half + 1))
                        for a in range(3):
                            for k in range(KT):
                                last = pe.matmul(bank[3 * half + a][:, 0:HALF], wc[s][:, k, a, :],
                                                 XT[:, k, half * HALF:(half + 1) * HALF], start=k == 0, stop=k == KT - 1)
                        last.then_inc(c_mm, 1)
            pe.wait_ge(cg_ok, 2 * KT + 2)
            project_out(1, lambda k, c: gT[:, k, c * P:c * P + ROWS[c]],
                        lambda k, s: woc0[:, k, :] if s == 0 else woc1[k // 4][:, k % 4, :],
                        [[(woc_in[0], 16)], [(woc_in[1], 32)]])
            mixture(1)

        @block.scalar
        def _(act):
            act.nop().then_inc(ys_ok, 2)

            def squares(n):
                for c in range(NC):
                    if n == 0:
                        act.wait_ge(x_in, 16 * NC)
                        act.wait_ge(const_ok, 1)
                    else:
                        act.wait_ge(h_ok, NC * (n - 1) + c + 1)
                    act.activation(junk[:], H[:, c, :], ACT.Square, accum_out=ssq[:, c:c + 1]).then_inc(sq_done, 1)
                    act.wait_ge(ms_ok, NC * n + c + 1)
                    act.activation(rms[:, c:c + 1], rms[:, c:c + 1], ACT.Sqrt).then_inc(rt_ok, 1)

            def xt_low(n):
                for c in range(NC):
                    act.wait_ge(xt_mm, NXT * n + 2 * c + 1)
                    act.activation(XT[:, 0:4, c * P:c * P + ROWS[c]],
                                   bank[6][:, :].rearrange("p (k t) -> p k t", k=4)[:, :, 0:ROWS[c]], ACT.Copy).then_inc(xt_a, 1)
            squares(0)
            xt_low(0)
            act.wait_ge(lbm_ok, 1)
            act.activation(lbe[:], lbe[:], ACT.Exp).then_inc(lbe_ok, 1)

            def half_of(t, a):
                m, half = a // 2, a % 2
                return t[:, m, half * HALF:(half + 1) * HALF]
            for n, (dst, fn) in enumerate(((fT, ACT.Sigmoid), (qdecT, ACT.Silu), (gateT, ACT.Silu))):
                for a in range(8):
                    act.wait_ge(z_mm, 8 * n + a + 1)
                    act.activation(half_of(dst, a), bank[a % 4][:, 0:HALF], fn).then_inc(z_free[a % 4], 1)
            act.wait_ge(f_ok, 5)
            act.activation(fT[:], fT[:], ACT.Ln).then_inc(ln_ok, 1)
            act.wait_ge(cum_ok, 4)
            act.activation(fT[:], koutT[:], ACT.Exp).then_inc(exp_ok, 1)
            act.activation(koutT[:], koutT[:], ACT.Exp, scale=-1.0).then_inc(exp_ok, 1)
            for i in range(2 * NC):
                un = 29 + i
                n = ROWS[i % NC]
                act.wait_ge(z_mm, un + 1)
                if i >= 2:
                    act.wait_ge(qms_ok, i - 1)
                act.activation(qsq[i % 2][0:n, :], bank[un % 4][0:n, :], ACT.Square).then_inc(qsq_ok, 1)
                act.wait_ge(qms_ok, i + 1)
                act.activation(hms[0:n, (i % 2) * NH:(i % 2 + 1) * NH], hms[0:n, (i % 2) * NH:(i % 2 + 1) * NH], ACT.Sqrt).then_inc(qrt_ok, 1)
            for c in range(NC):
                un = 39 + c
                act.wait_ge(z_mm, un + 1)
                act.activation(va[0:ROWS[c], c, :], bank[un % 4][0:ROWS[c], :], ACT.Copy).then_inc(z_free[un % 4], 1)
                act.wait_ge(z_free[un % 4], un // 4 + 1)
                act.nop().then_inc(v_ok, 1)
            for c in range(NC):
                n = ROWS[c]
                act.wait_ge(o_mm, c + 1)
                act.activation(osq[:, :, 0:n], bank[7][:, :].rearrange("p (m t) -> p m t", m=4)[:, :, 0:n], ACT.Square).then_inc(osq_ok, 1)
                act.wait_ge(stat_mm, c + 1)
                if c > 0:
                    act.wait_ge(zB_ok, c)
                act.activation(orms[:, :, 0:n], bank[0][:, :].rearrange("p (m t) -> p m t", m=4)[:, :, 0:n], ACT.Sqrt,
                               bias=epsc[:, 0:1]).then_inc(orms_ok, 1)
            act.wait_ge(kc_mm, 1)
            act.activation(kcT[:], bank[6][:, :].rearrange("p (m t) -> p m t", m=4), ACT.Copy).then_inc(kc_ok, 1)
            NU = NC * NH

            def prob_copy(i):
                if i % 2 == 0:
                    c = i // NH
                    act.wait_ge(pT_mm, i + 1)
                    if i >= 2:
                        act.wait_ge(pv_mm, i - 1)
                    if c < 4:
                        act.activation(prT[0][:, 0:c + 1, :], bank[2][:, 0:P * (c + 1)].rearrange("p (k t) -> p k t", t=P), ACT.Copy).then_inc(pT_a, 1)
                    else:
                        tie(act.activation(prT[0][:, 0, 0:DEC], bank[2][:, 0:DEC], ACT.Copy))
                        act.activation(prT[0][0:DEC, 1, 0:DEC], bank[2][0:DEC, P:P + DEC], ACT.Copy).then_inc(pT_a, 1)
            tie = Chain(act, ach)
            for i in range(NU + 2):
                if i < NU:
                    c, n = i // NH, ROWS[i // NH]
                    w = P * (c + 1) if c < 4 else PAST + DEC
                    act.wait_ge(s_ok, i + 1)
                    if i >= 2:
                        act.wait_ge(pT_mm, i - 1)
                    act.activation(pr[i % 2][0:n, 0:w], sneg[i % 2][0:n, 0:w], ACT.Exp, bias=nmaxs[0:n, i:i + 1], scale=-1.0,
                                   accum_out=rsum[0:n, i:i + 1]).then_inc(p_ok, 1)
                if 1 <= i <= NU:
                    prob_copy(i - 1)
                if i >= 11 and (i - 11) % NH == 0:
                    c = (i - 11) // NH
                    act.wait_ge(oaT_mm, c + 1)
                    act.activation(zA[:, :, c * P:c * P + ROWS[c]], bank[6][:, :].rearrange("p (m t) -> p m t", m=4)[:, :, 0:ROWS[c]],
                                   ACT.Copy).then_inc(zA_ok, 1)
            c = NC - 1
            act.wait_ge(oaT_mm, NC)
            act.activation(zA[:, :, c * P:T], bank[6][:, :].rearrange("p (m t) -> p m t", m=4)[:, :, 0:DEC], ACT.Copy).then_inc(zA_ok, 1)

            def mixture(l):
                squares(2 * l + 1)
                xt_low(2 * l + 1)
                act.wait_ge(ge_ok, l + 1)
                act.activation(rt[3][:, :, 0:NG], rt[3][:, :, 0:NG], ACT.Exp).then_inc(gx_ok, 1)
                act.wait_ge(e2_ok, l + 1)
                act.activation(c1[5][:], c1[5][:], ACT.Exp).then_inc(ex_ok, 1)
                G = l * (PAIRS + 1)
                E = l * NE

                def xg_low(p):
                    return act.activation(xg[p % 2][:, 0:4, :, :].rearrange("p k a s -> p (k a s)"), bank[0][:, :], ACT.Copy)
                act.wait_ge(g_mm, G + 1)
                xg_low(0).then_inc(xg_a, 1)
                with act.Fori(0, NE // 4) as i:
                    for p in range(2):
                        for ab in range(2):
                            act.wait_ge(h_mm, i * 4 + (E + 2 * p + ab + 1))
                            act.activation(sg[ab][:], bank[3 + ab][:, 0:P], ACT.Silu).then_inc(sg_ok, 1)
                        act.wait_ge(g_mm, i * 2 + (G + p + 2))
                        xg_low(p + 1).then_inc(xg_a, 1)
                        for ab in range(2):
                            act.wait_ge(y_mm, i * 4 + (E + 2 * p + ab + 1))
                            act.wait_ge(ys_free, i * 4 + (E + 2 * p + ab + 1))
                            act.activation(ys[ab][:], bank[6 + ab][:, :], ACT.Copy).then_inc(ys_ok, 1)
                act.wait_ge(cnt_ok, l + 1)
                most = act.value_load(cnt_i[0:1, l:l + 1], min_val=0, max_val=T)
                o = ov[l]
                with act.Fori(0, ROUNDS - 1) as r:
                    with act.If(most > CAP * r + CAP):
                        with act.Fori(0, NE) as e:
                            n = r * NE + e
                            act.wait_ge(o["h"], n + 1)
                            act.activation(sg[0][:], bank[3][:, 0:P], ACT.Silu).then_inc(o["sg"], 1)
                            act.wait_ge(o["y"], n + 1)
                            act.wait_ge(o["free"], n + 1)
                            act.activation(ys[0][:], bank[6][:, :], ACT.Copy).then_inc(o["ys"], 1)
            mixture(0)

            squares(2)
            xt_low(2)
            with act.Fori(0, KT) as m:
                for half in range(2):
                    act.wait_ge(c_mm, m * 2 + (half + 1))
                    act.activation(hc[half][:], bank[3 * half + 2][:, 0:HALF], ACT.Copy).then_inc(hc_ok, 1)
            mixture(1)

        @block.vector
        def _(dve):
            tie = Chain(dve, dch)
            dve.nop().then_inc(hh_ok, 2)
            dve.nop().then_inc(cg_ok, 2)

            def norms(n):
                gain = gmix if n % 2 == 0 else gffn
                if n == 1:
                    dve.wait_ge(op_mm, 2 * NC)
                for c in range(NC):
                    dve.wait_ge(sq_done, NC * n + c + 1)
                    dve.tensor_scalar(rms[:, c:c + 1], ssq[:, c:c + 1], 1.0 / D, EPS, ALU.mult, ALU.add).then_inc(ms_ok, 1)
                    dve.wait_ge(rt_ok, NC * n + c + 1)
                    tie(dve.reciprocal(rstd[:, c:c + 1], rms[:, c:c + 1]))
                    if c == 0:
                        dve.wait_ge(gmix_in if n % 2 == 0 else gffn_in, 16 * (n // 2 + 1))
                    dve.scalar_tensor_tensor(XN[:, c, :], H[:, c, :], rstd[:, c:c + 1], gain[:], ALU.mult, ALU.mult).then_inc(xn_ok, 1)

            def xt_high(n):
                for c in range(NC):
                    dve.wait_ge(xt_mm, NXT * n + 2 * c + 2)
                    dve.tensor_copy(XT[:, 4:8, c * P:c * P + ROWS[c]],
                                    bank[7][:, :].rearrange("p (k t) -> p k t", k=4)[:, :, 0:ROWS[c]]).then_inc(xt_d, 1)

            norms(0)
            xt_high(0)
            dve.wait_ge(tab_in, 16 * 5)
            tie(dve.tensor_tensor(lb[:], lbl[:, 0:4], lbl[:, 4:8], ALU.max))
            dve.tensor_tensor(lbe[:].rearrange("p (r m) -> p r m", r=2), lbl[:].rearrange("p (r m) -> p r m", r=2),
                              bc(lb[:].unsqueeze(1), [P, 2, 4]), ALU.subtract).then_inc(lbm_ok, 1)
            dve.wait_ge(lbe_ok, 1)
            tie(dve.tensor_tensor(lbs[:], lbe[:, 0:4], lbe[:, 4:8], ALU.add))
            tie(dve.reciprocal(lbs[:], lbs[:]))
            tie(dve.tensor_tensor(lb[:], lbe[:, 0:4], lbs[:], ALU.mult))
            tie(dve.tensor_scalar(lbs[:], lb[:], -1.0, 1.0, ALU.mult, ALU.add))
            tie(dve.tensor_scalar(qgain[:], qgain[:], HD ** -0.5, None, ALU.mult))
            dve.wait_ge(const_ok, 1)
            tie(dve.tensor_reduce(even[:], blk_sel[:], AX.X, ALU.add))
            tie(dve.tensor_scalar(odd[:], even[:], -1.0, 1.0, ALU.mult, ALU.add))
            for b in range(4):
                dve.wait_ge(z_free[b], 2)
            for m in range(4):
                dve.tensor_scalar(fT[:, m, :], fT[:, m, :], lbs[:, m:m + 1], lb[:, m:m + 1], ALU.mult, ALU.add).then_inc(f_ok, 1)
            dve.wait_ge(f_ok, 4)
            dve.tensor_scalar(kinT[:], fT[:], -1.0, 1.0, ALU.mult, ALU.add).then_inc(f_ok, 1)
            dve.wait_ge(ln_ok, 1)
            for m in range(4):
                dve.tensor_tensor_scan(koutT[:, m, :], reset[:], fT[:, m, :], 0.0, ALU.mult, ALU.add).then_inc(cum_ok, 1)
            dve.wait_ge(exp_ok, 2)
            dve.wait_ge(f_ok, 5)
            tie(dve.tensor_copy(dec[:].rearrange("p (m b) -> p m b", m=4), fT[:, :, BLK - 1::BLK]))
            dve.tensor_tensor(kinT[:], kinT[:], koutT[:], ALU.mult).then_inc(hg_ok, 1)
            for b in range(4):
                dve.wait_ge(z_free[b], 6)
            dve.tensor_tensor(qdecT[:], qdecT[:], fT[:], ALU.mult).then_inc(hg_ok, 1)
            dve.wait_ge(hg_ok, 2)
            dve.tensor_tensor(koutT[:].rearrange("p m (b t) -> p (m b) t", t=BLK), kinT[:].rearrange("p m (b t) -> p (m b) t", t=BLK),
                              bc(dec[:].unsqueeze(2), [P, 4 * NBLK, BLK]), ALU.mult).then_inc(hg_ok, 1)
            for m in range(4):
                tie(dve.tensor_scalar(gateT[:, m, :], gateT[:, m, :], onorm[:, m:m + 1], None, ALU.mult))
            for c in range(NC):
                un = 24 + c
                dve.wait_ge(z_mm, un + 1)
                dve.tensor_copy(vb[0:ROWS[c], c, :], bank[un % 4][0:ROWS[c], :]).then_inc(z_free[un % 4], 1)
            for i in range(2 * NC):
                un, c, n = 29 + i, i % NC, ROWS[i % NC]
                dst, gain = (q_tok, qgain) if i < NC else (k_tok, kgain)
                sl = slice((i % 2) * NH, (i % 2 + 1) * NH)
                dve.wait_ge(qsq_ok, i + 1)
                tie(dve.tensor_reduce(hss[0:n, sl], qsq[i % 2][0:n, :].rearrange("p (h d) -> p h d", h=NH), AX.X, ALU.add))
                dve.tensor_scalar(hms[0:n, sl], hss[0:n, sl], 1.0 / HD, EPS, ALU.mult, ALU.add).then_inc(qms_ok, 1)
                dve.wait_ge(qrt_ok, i + 1)
                tie(dve.reciprocal(hrs[0:n, sl], hms[0:n, sl]))
                dve.tensor_tensor(dst[0:n, c, :].rearrange("p (h d) -> p h d", h=NH), bank[un % 4][0:n, :].rearrange("p (h d) -> p h d", h=NH),
                                  bc(hrs[0:n, sl].unsqueeze(2), [n, NH, HD]), ALU.mult).then_inc(z_free[un % 4], 1)
                dve.wait_ge(z_free[un % 4], un // 4 + 1)
                dve.tensor_tensor(dst[0:n, c, :].rearrange("p (h d) -> p h d", h=NH), dst[0:n, c, :].rearrange("p (h d) -> p h d", h=NH),
                                  bc(gain[0:n, :].unsqueeze(1), [n, NH, HD]), ALU.mult).then_inc(qk_ok, 1)
            for i in range(2 * NC):
                c, dst = i // 2, (qT, kT)[i % 2]
                dve.wait_ge(qkT_mm, i + 1)
                dve.tensor_copy(dst[:, :, c * P:c * P + ROWS[c]],
                                bank[4 + i % 2][:, :].rearrange("p (m t) -> p m t", m=4)[:, :, 0:ROWS[c]]).then_inc(qkT_ok, 1)
            dve.memset(st[0][:, 0, :, :], 0.0).then_inc(st0_ok, 1)
            dve.wait_ge(st0_ok, 1)
            def hgrn_chain(c):
                n = ROWS[c]
                dve.wait_ge(ko_mm, c + 1)
                if c >= 2:
                    dve.wait_ge(u_mm, c - 1)
                dve.tensor_copy(kout[c % 2][0:n, :], bank[0][0:n, :]).then_inc(ko_ok, 1)
                v = vb[0:n, c, :].rearrange("p (h d) -> p h d", h=NH)
                if c == 0:
                    for b in range(4):
                        dve.wait_ge(z_free[b], 11)
                dve.tensor_scalar(vx[c % 2][0:n, :, 0, :], v, even[0:n, :], None, ALU.mult)
                tie(dve.tensor_scalar(vx[c % 2][0:n, :, 1, :], v, odd[0:n, :], None, ALU.mult))
                dve.nop().then_inc(vx_ok, 1)
                dve.wait_ge(a_mm, c + 1)
                if c >= 2:
                    dve.wait_ge(o_mm, c - 1)
                for par in range(2):
                    dve.tensor_tensor(am[c % 2][0:n, par, :, 0:n], bank[1 + par][0:n, :].rearrange("p (m t) -> p m t", m=4)[:, :, 0:n],
                                      bc(blk_mask[0:n, 0:n].unsqueeze(1), [n, 4, n]), ALU.mult).then_inc(a_ok, 1)
                dve.wait_ge(u_mm, c + 1)
                if c == 4:
                    dve.wait_ge(st_in, 16)
                for b in range(n // BLK):
                    t = dec[:].rearrange("p (m b) -> p m b", m=4)[:, :, 8 * c + b:8 * c + b + 1]
                    upd = bank[3 + b // 2][:, :].rearrange("p (m i v) -> p m i v", m=4, i=2)[:, :, b % 2, :]
                    tie(dve.tensor_tensor(dS[:], st[c % 2][:, b, :, :], bc(t, [P, 4, HD]), ALU.mult))
                    tie(dve.tensor_tensor(st[c % 2][:, b + 1, :, :], upd, dS[:], ALU.add))
                if c < 3:
                    if c >= 1:
                        dve.wait_ge(o_mm, c)
                    dve.tensor_copy(st[(c + 1) % 2][:, 0, :, :], st[c % 2][:, 8, :, :]).then_inc(st0_ok, 1)
                    dve.wait_ge(st0_ok, c + 2)
                dve.nop().then_inc(st_ok, 1)

            def hgrn_norm(c):
                n = ROWS[c]
                dve.wait_ge(orms_ok, c + 1)
                tie(dve.reciprocal(orms[:, :, 0:n], orms[:, :, 0:n]))
                z = zB[:, :, c * P:c * P + n]
                tie(dve.tensor_tensor(z, bank[7][:, :].rearrange("p (m t) -> p m t", m=4)[:, :, 0:n], orms[:, :, 0:n], ALU.mult))
                dve.tensor_tensor(z, z, gateT[:, :, c * P:c * P + n], ALU.mult).then_inc(zB_ok, 1)
            hgrn_chain(0)
            for c in range(NC):
                if c + 1 < NC:
                    hgrn_chain(c + 1)
                hgrn_norm(c)

            dve.wait_ge(bias_in, 16 * 4)
            tie(dve.memset(bias[0:CH, :, 512 - CH:512], MASKED))
            NU = NC * NH

            def score_max(i):
                c, h = divmod(i, NH)
                n = ROWS[c]
                w, b0 = (P * (c + 1), 384 - P * c) if c < 4 else (PAST + DEC, 256)
                dve.wait_ge(s_mm, i + 1)
                if i >= 2:
                    dve.wait_ge(p_ok, i - 1)
                dve.tensor_tensor_reduce(out=sneg[i % 2][0:n, 0:w], in0=bank[i % 2][0:n, 0:w], in1=bias[0:n, h, b0:b0 + w],
                                         scale=-1.0, scalar=-MASKED, op0=ALU.add, op1=ALU.min,
                                         accum_out=nmaxs[0:n, i:i + 1]).then_inc(s_ok, 1)

            def prob_copy(i):
                if i % 2 == 1:
                    c = i // NH
                    dve.wait_ge(pT_mm, i + 1)
                    if i >= 3:
                        dve.wait_ge(pv_mm, i - 1)
                    if c < 4:
                        dve.tensor_copy(prT[1][:, 0:c + 1, :], bank[3][:, 0:P * (c + 1)].rearrange("p (k t) -> p k t", t=P)).then_inc(pT_d, 1)
                    else:
                        tie(dve.tensor_copy(prT[1][:, 0, 0:DEC], bank[3][:, 0:DEC]))
                        dve.tensor_copy(prT[1][0:DEC, 1, 0:DEC], bank[3][0:DEC, P:P + DEC]).then_inc(pT_d, 1)

            def head_scale(c):
                n = ROWS[c]
                sl = slice((c % 2) * NH, (c % 2 + 1) * NH)
                dve.wait_ge(pv_mm, NH * (c + 1))
                tie(dve.reciprocal(rinv[0:n, sl], rsum[0:n, c * NH:(c + 1) * NH]))
                if c >= 2:
                    dve.wait_ge(oaT_mm, c - 1)
                dve.tensor_tensor(oa[c % 2][0:n, :].rearrange("p (h d) -> p h d", h=NH), bank[4 + c % 2][0:n, :].rearrange("p (h d) -> p h d", h=NH),
                                  bc(rinv[0:n, sl].unsqueeze(2), [n, NH, HD]), ALU.mult).then_inc(oa_ok, 1)
            for i in range(NU + 3):
                if i < NU:
                    score_max(i)
                if 1 <= i <= NU:
                    prob_copy(i - 1)
                if i >= 10 and (i - 10) % NH == 0:
                    head_scale((i - 10) // NH)

            def residual(n):
                for i in range(2 * NC):
                    c, s = i // 2, i % 2
                    dve.wait_ge(op_mm, 2 * NC * n + i + 1)
                    h = H[0:ROWS[c], c, s * 512:(s + 1) * 512]
                    dve.tensor_tensor(h, bank[i % 4][0:ROWS[c], :], h, ALU.add).then_inc(op_add, 1)
                    if s == 1:
                        dve.wait_ge(op_add, 2 * NC * n + i + 1)
                        dve.nop().then_inc(h_ok, 1)
            residual(0)

            def route(l):
                lgg, lge = lg[:, :, 0:NG], lg[:, :, NG:NR].rearrange("p c (g j) -> p c g j", g=NG)
                if l == 0:
                    tie(dve.memset(lg[:], 0.0))
                    tie(dve.memset(rk[:, :, NE:RKW], -1.0))
                    tie(dve.memset(dv[:, :, NE:RKW], 0.0))
                else:
                    tie(dve.memset(lg[:], 0.0))
                    tie(dve.memset(rk[:, :, NE:RKW], -1.0))
                    tie(dve.memset(dv[:, :, NE:RKW], 0.0))
                dve.wait_ge(lg_mm, l + 1)
                dve.wait_ge(wr_in, 64 * (l + 1))
                z = bank[0][:, 0:NC * NR].rearrange("p (c n) -> p c n", c=NC)
                tie(dve.tensor_tensor(lg[:, 0:4, :], z[:, 0:4, :], bc(biasr[:].unsqueeze(1), [P, 4, NR]), ALU.add))
                dve.tensor_tensor(lg[0:DEC, 4, :], z[0:DEC, 4, :], biasr[0:DEC, :], ALU.add).then_inc(lg_ok, 1)
                dve.wait_ge(lg_ok, l + 1)

                def first_max(v, w, rev, eq, key, hot, top):
                    tie(dve.tensor_reduce(top, v, AX.X, ALU.max))
                    tie(dve.tensor_tensor(eq, v, bc(top.unsqueeze(2), [P, NC, w]), ALU.is_equal))
                    tie(dve.tensor_tensor(key, eq, bc(rev.unsqueeze(1), [P, NC, w]), ALU.mult))
                    tie(dve.tensor_reduce(c1[1][:], key, AX.X, ALU.max))
                    tie(dve.tensor_tensor(hot, key, bc(c1[1][:].unsqueeze(2), [P, NC, w]), ALU.is_equal))
                hot_g, hot1, hot2 = rt[2][:, :, 0:4], rt[2][:, :, 4:12], rt[2][:, :, 12:20]
                first_max(lgg, NG, rev4[:], rt[0][:, :, 0:4], rt[1][:, :, 0:4], hot_g, c1[0][:])
                dve.tensor_tensor(rt[3][:, :, 0:NG], lgg, bc(c1[0][:].unsqueeze(2), [P, NC, NG]), ALU.subtract).then_inc(ge_ok, 1)
                four = [P, NC, NG, EPG]
                r4 = [t[:].rearrange("p c (g j) -> p c g j", g=NG) for t in rt]
                tie(dve.tensor_tensor(r4[0], lge, bc(hot_g.unsqueeze(3), four), ALU.mult))
                sel8 = rt[1][:, :, 8:16]
                tie(dve.tensor_reduce(sel8, rt[0][:].rearrange("p c (g j) -> p c j g", g=NG), AX.X, ALU.add))
                first_max(sel8, EPG, rev8[:], rt[1][:, :, 16:24], rt[1][:, :, 24:32], hot1, c1[3][:])
                sel7 = rt[4][:, :, 0:8]
                tie(dve.scalar_tensor_tensor(sel7, hot1, -3e38, sel8, ALU.mult, ALU.add))
                first_max(sel7, EPG, rev8[:], rt[1][:, :, 16:24], rt[1][:, :, 24:32], hot2, c1[4][:])
                dve.tensor_tensor(c1[5][:], c1[4][:], c1[3][:], ALU.subtract).then_inc(e2_ok, 1)
                tie(dve.tensor_tensor(hot_g, hot_g, bc(frame_ok[:].unsqueeze(2), [P, NC, NG]), ALU.mult))
                for hot, m in ((hot1, m1), (hot2, m2)):
                    tie(dve.tensor_tensor(m[:].rearrange("p c (g j) -> p c g j", g=NG), bc(hot_g.unsqueeze(3), four),
                                          bc(hot.unsqueeze(2), four), ALU.mult))
                dve.tensor_tensor(rt[0][:], m1[:], m2[:], ALU.add).then_inc(msk_ok, 1)
                dve.wait_ge(gx_ok, l + 1)
                tie(dve.tensor_reduce(c1[2][:], rt[3][:, :, 0:NG], AX.X, ALU.add))
                tie(dve.reciprocal(c1[2][:], c1[2][:]))
                dve.wait_ge(ex_ok, l + 1)
                tie(dve.tensor_scalar(c1[6][:], c1[5][:], 1.0, None, ALU.add))
                tie(dve.reciprocal(c1[6][:], c1[6][:]))
                tie(dve.tensor_tensor(c1[2][:], c1[2][:], c1[6][:], ALU.mult))
                tie(dve.tensor_copy(gate[0][:], c1[2][:]))
                tie(dve.tensor_tensor(gate[1][:], c1[2][:], c1[5][:], ALU.mult))
                tie(dve.tensor_scalar(c1[3][:], frame_no[:], 2.0, -2.0 * DROP, ALU.mult, ALU.add))
                tie(dve.tensor_scalar(c1[4][:], frame_no[:], 2.0, 2.0 * T - 2.0 * DROP, ALU.mult, ALU.add))
                tie(dve.tensor_tensor(rt[1][:], m1[:], bc(c1[3][:].unsqueeze(2), [P, NC, NE]), ALU.mult))
                tie(dve.tensor_tensor(rt[4][:], m2[:], bc(c1[4][:].unsqueeze(2), [P, NC, NE]), ALU.mult))
                tie(dve.tensor_tensor(dv[:, :, 0:NE], rt[1][:], rt[4][:], ALU.add))
                dve.wait_ge(rk_mm, l + 1)
                dve.wait_ge(msk_ok, l + 1)
                tie(dve.scalar_tensor_tensor(rt[3][:], bank[1][:, 0:NC * NE].rearrange("p (c n) -> p c n", c=NC), 1.0, rt[0][:], ALU.add, ALU.mult))
                tie(dve.tensor_reduce(c1[7][:, 0:1], rt[3][:], AX.XY, ALU.max))
                dve.tensor_scalar(rk[:, :, 0:NE], rt[3][:], -1.0, None, ALU.add).then_inc(rk_ok, 1)
                dve.wait_ge(rk_ok, l + 1)
                dve.wait_ge(cm_mm, l + 1)
                tie(dve.tensor_reduce(cnt[0:1, 0:1], bank[2][0:1, 0:P], AX.X, ALU.max))
                dve.tensor_copy(cnt_i[0:1, l:l + 1], cnt[0:1, 0:1]).then_inc(cnt_ok, 1)

            def select(p, e):
                full = [P, NC, 2, CAP]
                return dve.tensor_tensor(seln[p % 2][:], bc(rk[:, :, bass.ds(e, 2)].unsqueeze(3), full),
                                         bc(slot_no[:].unsqueeze(1).unsqueeze(1), full), ALU.is_equal)

            def xg_high(p):
                return dve.tensor_copy(xg[p % 2][:, 4:8, :, :].rearrange("p k a s -> p (k a s)"), bank[1][:, :])

            def row_numbers(p, ab):
                out = None
                for dh in range(2):
                    out = dve.tensor_scalar(idx[2 * (p % 2) + ab][64 * dh:64 * dh + 64, :], bank[2][64 * ab:64 * ab + 64, ab:ab + 1],
                                            2.0 * DROP + dh, None, ALU.add)
                return out

            def mixture(l):
                norms(2 * l + 1)
                xt_high(2 * l + 1)
                route(l)
                G = l * (PAIRS + 1)
                E = l * NE
                select(0, 0).then_inc(sel_ok, 1)
                dve.wait_ge(g_mm, G + 1)
                xg_high(0).then_inc(xg_d, 1)
                dve.wait_ge(ix_mm, G + 1)
                row_numbers(0, 0)
                row_numbers(0, 1).then_inc(ix_ok, 1)
                with dve.Fori(0, NE // 4) as i:
                    for p in range(2):
                        select(p + 1, 4 * i + (2 * p + 2)).then_inc(sel_ok, 1)
                        for ab in range(2):
                            dve.wait_ge(sg_ok, i * 4 + (E + 2 * p + ab + 1))
                            dve.tensor_tensor(hh[ab][:], bank[3 + ab][:, P:2 * P], sg[ab][:], ALU.mult).then_inc(hh_ok, 1)
                        dve.wait_ge(t_mm, i * 4 + (E + 2 * p + 1))
                        dve.tensor_copy(hT[0][:], bank[5][:, 0:P]).then_inc(ht_ok, 1)
                        dve.wait_ge(g_mm, i * 2 + (G + p + 2))
                        xg_high(p + 1).then_inc(xg_d, 1)
                        dve.wait_ge(t_mm, i * 4 + (E + 2 * p + 2))
                        dve.tensor_copy(hT[1][:], bank[5][:, P:2 * P]).then_inc(ht_ok, 1)
                        dve.wait_ge(ix_mm, i * 2 + (G + p + 2))
                        dve.wait_ge(ys_free, i * 4 + (E + 2 * p + 2))
                        row_numbers(p + 1, 0)
                        row_numbers(p + 1, 1).then_inc(ix_ok, 1)
                dve.wait_ge(cnt_ok, l + 1)
                most = dve.value_load(cnt_i[0:1, l:l + 1], min_val=0, max_val=T)
                dve.wait_ge(ys_free, NE * (l + 1) + 2)
                o = ov[l]
                with dve.Fori(0, ROUNDS - 1) as r:
                    with dve.If(most > CAP * r + CAP):
                        dve.tensor_scalar(rk[:], rk[:], -float(CAP), None, ALU.add).then_inc(o["rk"], 1)
                        with dve.Fori(0, NE) as e:
                            n = r * NE + e
                            dve.wait_ge(o["rk"], r + 1)
                            dve.wait_ge(o["free"], n + 1)
                            select(0, e).then_inc(o["sel"], 1)
                            dve.wait_ge(o["g"], n + 1)
                            dve.tensor_copy(xg[0][:, 0:4, :, :].rearrange("p k a s -> p (k a s)"), bank[0][:, :])
                            xg_high(0).then_inc(o["xg"], 1)
                            dve.wait_ge(o["ixm"], n + 1)
                            row_numbers(0, 0).then_inc(o["ix"], 1)
                            dve.wait_ge(o["sg"], n + 1)
                            dve.tensor_tensor(hh[0][:], bank[3][:, P:2 * P], sg[0][:], ALU.mult).then_inc(o["hh"], 1)
                            dve.wait_ge(o["t"], n + 1)
                            dve.tensor_copy(hT[0][:], bank[5][:, 0:P]).then_inc(o["ht"], 1)
                for c in range(NC):
                    n = ROWS[c]
                    turn = l * (3 if c % 2 == 0 else 2) + c // 2 + 1
                    dve.wait_ge(yab_in[c % 2], 32 * turn)
                    h = H[0:n, c, :]
                    tie(dve.scalar_tensor_tensor(h, ya[c % 2][0:n, :], gate[0][0:n, c:c + 1], h, ALU.mult, ALU.add))
                    tie(dve.scalar_tensor_tensor(h, yb[c % 2][0:n, :], gate[1][0:n, c:c + 1], h, ALU.mult, ALU.add))
                    dve.nop().then_inc(h_ok, 1)
            mixture(0)

            norms(2)
            xt_high(2)
            dve.wait_ge(st_in, 48)
            tie(dve.memset(u[:, 0:2], 0.0))
            S0 = 2 + SEQ
            parts = [[(0, HALF, 0)], [(0, SEQ - HALF, HALF), (SEQ - HALF, HALF, SEQ)]]
            with dve.Fori(0, KT) as m:
                tie.loop(m, CONV_STEPS, KT)
                mm = bass.ds(m, 1)
                tie(dve.tensor_copy(u[:, S0:S0 + 2], hist[:, mm, :].rearrange("p k r -> p (k r)")))
                for half in range(2):
                    dve.wait_ge(hc_ok, m * 2 + (half + 1))
                    for a, b, t0 in parts[half]:
                        col = t0 + 2 + (2 if t0 == SEQ else 0)
                        tie(dve.tensor_tensor(u[:, col:col + b - a], bank[3 * half + 1][:, a:b], hc[half][:, a:b], ALU.mult))
                    for a, b, t0 in parts[half]:
                        col, w = t0 + (2 if t0 == SEQ else 0), b - a
                        c0 = cv[:, t0:t0 + w]
                        tie(dve.tensor_scalar(c0, u[:, col:col + w], convw[:, bass.ds(m, 1)], None, ALU.mult))
                        tie(dve.scalar_tensor_tensor(c0, u[:, col + 1:col + 1 + w], convw[:, bass.ds(m + KT, 1)], c0, ALU.mult, ALU.add))
                        tie(dve.scalar_tensor_tensor(c0, u[:, col + 2:col + 2 + w], convw[:, bass.ds(m + 2 * KT, 1)], c0, ALU.mult, ALU.add))
                    tie(dve.tensor_tensor(gT[:, mm, half * HALF:(half + 1) * HALF].rearrange("p k t -> p (k t)"), bank[3 * half][:, 0:HALF],
                                          cv[:, half * HALF:(half + 1) * HALF], ALU.mult))
                    dve.nop().then_inc(cg_ok, 1)
                tie(dve.tensor_copy(tails[:, 0, mm, :].rearrange("p k r -> p (k r)"), u[:, SEQ:SEQ + 2]))
                tie(dve.tensor_copy(tails[:, 1, mm, :].rearrange("p k r -> p (k r)"), u[:, UW - 2:UW]))
                dve.nop().then_inc(tail_ok, 1)
            tie.end()
            residual(1)
            mixture(1)


CONV_STEPS = 1 + 3 + 3 * 3 + 2 + 2

_INS = ['x_prompt', 'x_sample', 'cache_a_k', 'cache_a_v', 'state_hgrn', 'state_conv', 'norm_mix', 'norm_ffn', 'w_in_ab',
        'w_out_ab', 'q_norm', 'k_norm', 'rel_bias', 'hgrn_lb_logits', 'hgrn_out_norm', 'w_in_c', 'conv_w', 'w_out_c',
        'w_group', 'b_group', 'w_expert', 'b_expert', 'w1', 'w3', 'w2']
_OUTS = [(1, SEQ, D), (1, DEC, D), (1, 1, SEQ, NH, HD), (1, 1, SEQ, NH, HD), (1, 1, PAST, NH, HD), (1, 1, PAST, NH, HD),
         (1, 1, NH, HD, HD), (1, 1, NH, HD, HD), (1, 1, 2, D), (1, 1, 2, D)]


def kernel(**inputs):
    import numpy as _np
    import concourse.bacc as _bacc
    from concourse import mybir as _mybir
    from concourse.bass_utils import run_bass_kernel_spmd as _run

    nc = _bacc.Bacc("TRN2", target_bir_lowering=False, num_devices=1)
    arrays, args = {}, []
    for name in _INS:
        a = _np.ascontiguousarray(inputs[name])
        arrays[f"in_{name}_dram"] = a
        args.append(nc.dram_tensor(f"in_{name}_dram", a.shape, _mybir.dt.from_np(a.dtype), kind="ExternalInput").ap())
    for i, shape in enumerate(_OUTS):
        args.append(nc.dram_tensor(f"out_{i}_dram", shape, _mybir.dt.float32, kind="ExternalOutput").ap())
    hmoe_step(nc, *args)
    r = _run(nc, [arrays], core_ids=[0])
    return tuple(r.results[0][f"out_{i}_dram"] for i in range(len(_OUTS)))
```

```python
from contextlib import ExitStack

import numpy as np
import concourse.bass as bass
from concourse import mybir

F32 = mybir.dt.float32
F32R = mybir.dt.float32r
BF16 = mybir.dt.bfloat16
I32 = mybir.dt.int32
U32 = mybir.dt.uint32
ALU = mybir.AluOpType
ACT = mybir.ActivationFunctionType
AX = mybir.AxisListType

P = 128
D = 1024
KT = D // P
SEQ, DEC, PAST = 512, 32, 128
T = SEQ + DEC
NC = 5
ROWS = [128, 128, 128, 128, 32]
HALF = T // 2
NH, HD = 8, 64
DA = NH * HD
CH = 64
REL = 128
BLK = 16
NBLK = T // BLK
EPS = 1e-6
NG, EPG = 4, 8
NE = NG * EPG
DE = 256
CAP = 64
ROUNDS = -(-T // CAP)
NR = NG + NE
RKW = NE + 4
GROUPS = [3, 5, 6, 4, 0, 1, 2]
HG = DA // 2
UNIT_END = [4, 8, 12, 16, 20, 24, 29, 34, 39, 44, 49, 54, 59, 64]
MASKED = -1e30
DROP = 1100


def hmoe_step(nc, x_prompt, x_sample, cache_a_k, cache_a_v, state_hgrn, state_conv, norm_mix, norm_ffn,
              w_in_ab, w_out_ab, q_norm, k_norm, rel_bias, hgrn_lb_logits, hgrn_out_norm, w_in_c, conv_w,
              w_out_c, w_group, b_group, w_expert, b_expert, w1, w3, w2,
              y_prompt, y_sample, nk_p, nv_p, nk_s, nv_s, nh_p, nh_s, nconv_p, nconv_s):
    ctx = ExitStack()
    KB = 1024
    BASE = 16512

    def at(name, kb, shape, dt=F32):
        return nc.alloc_sbuf_tensor_at(name, shape, dt, offset=BASE + int(kb * KB))

    def sem(name):
        return ctx.enter_context(nc.semaphore(name))

    with ctx:
        H = at("H", 0, [P, NC, D])
        ident = at("ident", 20, [P, P])
        upper = at("upper", 20.5, [P, P])
        ones = at("ones", 21, [P, P])
        head_mean = at("head_mean", 21.5, [P, P])
        blk_mask = at("blk_mask", 22, [P, P])
        slot_no = at("slot_no", 22.5, [P, CAP])
        junk = at("junk", 22.75, [P, D], BF16)
        sm = 24.75
        def small(name, n, dt=F32):
            nonlocal sm
            t = at(name, sm, [P, n], dt)
            sm += -(-n * 4 // 32) * 32 / KB
            return t
        blk_sel = small("blk_sel", 4)
        even = small("even", 1)
        odd = small("odd", 1)
        frame_no = small("frame_no", NC)
        frame_ok = small("frame_ok", NC)
        rev4 = small("rev4", NG)
        rev8 = small("rev8", EPG)
        half_no = small("half_no", 1)
        epsc = small("epsc", 1)
        ssq = small("ssq", NC)
        rms = small("rms", NC)
        rstd = small("rstd", NC)
        lbl = small("lbl", 8)
        lbe = small("lbe", 8)
        lb = small("lb", 4)
        lbs = small("lbs", 4)
        onorm = small("onorm", 4)
        convw = small("convw", 3 * KT)
        qgain = small("qgain", HD)
        kgain = small("kgain", HD)
        hss = small("hss", 2 * NH)
        hms = small("hms", 2 * NH)
        hrs = small("hrs", 2 * NH)
        rsum = small("rsum", NC * NH)
        rinv = small("rinv", 2 * NH)
        nmaxs = small("nmaxs", NC * NH)
        dec = small("dec", 4 * NBLK)
        biasr = small("biasr", NR)
        cnt = small("cnt", 4)
        cnt_i = small("cnt_i", 2, I32)
        assert sm <= 28, sm
        gmix = at("gmix", 28, [P, D])
        gffn = at("gffn", 32, [P, D])
        RING = 36
        w13 = [at(f"w13_{s}", RING + 24 * s, [P, KT, 2, DE]) for s in range(4)]
        w2s = [at(f"w2_{s}", RING + 24 * s + 16, [P, 2, D]) for s in range(4)]
        XN = at("XN", 132, [P, NC, D])
        XT = at("XT", 152, [P, KT, T])
        MISC = 169
        wab = [at(f"wab{s}", RING + 16 * s, [P, KT, HG]) for s in range(3)]
        wab_lo = [at(f"wab_lo{s}", RING + 16 * s, [P, KT, HG], F32R) for s in range(3)]
        wab_hi = [at(f"wab_hi{s}", RING + 16 * s + 8, [P, KT, HG], F32R) for s in range(3)]
        xc_hi = at("xc_hi", 152, [P, KT, T], F32R)
        xp_lo = at("xp_lo", MISC + 20, [P, KT, T], F32R)
        HI = RING + 48
        q_tok = at("q_tok", HI, [P, NC, DA])
        k_tok = at("k_tok", HI + 10, [P, NC, DA])
        kinT = at("kinT", HI + 20, [P, 4, T])
        koutT = at("koutT", HI + 28.5, [P, 4, T])
        qdecT = at("qdecT", HI + 37, [P, 4, T])
        fT = at("fT", 132, [P, 4, T])
        gateT = at("gateT", 140.5, [P, 4, T])
        kcT = at("kcT", 149, [P, 4, P])
        va = at("va", MISC, [P, NC, DA])
        vb = at("vb", MISC + 10, [P, NC, DA])
        qT = at("qT", MISC + 20, [P, 4, T])
        kT = at("kT", MISC + 28.5, [P, 4, T])
        bias = at("bias", 152, [P, NH, 512])
        zB = at("zB", 132, [P, 4, T])
        reset = at("reset", HI + 45.5, [P, T])
        st = [at(f"st{i}", RING + 9 * i, [P, 9, 4, HD]) for i in range(2)]
        kout = [at(f"kout{i}", RING + 18 + 2 * i, [P, DA]) for i in range(2)]
        vx = [at(f"vx{i}", RING + 22 + 4 * i, [P, NH, 2, HD]) for i in range(2)]
        am = [at(f"am{i}", RING + 30 + 4 * i, [P, 2, 4, P]) for i in range(2)]
        osq = at("osq", RING + 38, [P, 4, P])
        orms = at("orms", RING + 40, [P, 4, P])
        dS = at("dS", RING + 42, [P, 4, HD])
        sneg = [at(f"sneg{i}", HI + 2 * i, [P, 512]) for i in range(2)]
        pr = [at(f"pr{i}", HI + 4 + 2 * i, [P, 512]) for i in range(2)]
        prT = [at(f"prT{i}", HI + 8 + 2 * i, [P, 4, P]) for i in range(2)]
        oa = [at(f"oa{i}", HI + 12 + 2 * i, [P, DA]) for i in range(2)]
        kc = at("kc", HI + 16, [P, DA])
        vc = at("vc", HI + 18, [P, DA])
        qsq = [at(f"qsq{i}", 149 + i, [P, HG]) for i in range(2)]
        wo = [at(f"wo{s}", RING + 32 * s, [P, KT, 512]) for s in range(2)]
        wo_lo = [at(f"wo_lo{s}", RING + 32 * s, [P, KT, 512], F32R) for s in range(2)]
        wo_hi = [at("wo_hi0", RING + 16, [P, KT, 512], F32R), at("wo_hi1", MISC + 20, [P, KT, 512], F32R)]
        zA_hi = at("zA_hi", HI + 20, [P, 4, T], F32R)
        zB_hi = at("zB_hi", HI + 28.5, [P, 4, T], F32R)
        zB_lo = at("zB_lo", HI + 37, [P, 4, T], F32R)
        zA_lo = at("zA_lo", MISC + 10, [P, 4, T], F32R)
        wr = at("wr", MISC + 36.5, [P, KT, NR])
        lg = at("lg", MISC + 29.5, [P, NC, NR])
        rt = [at(f"rt{i}", MISC + (30.25, 31, 3.5, 4.25, 5)[i], [P, NC, NE]) for i in range(5)]
        m1 = at("m1", MISC + 5.75, [P, NC, NE])
        m2 = at("m2", MISC + 6.5, [P, NC, NE])
        rk = at("rk", MISC + 7.25, [P, NC, RKW])
        dv = at("dv", MISC + 8, [P, NC, RKW], F32R)
        c1 = [at(f"c{i}", MISC + 8.75 + i * 0.03125, [P, NC]) for i in range(8)]
        gate = [at(f"gate{i}", MISC + 9 + i * 0.03125, [P, NC]) for i in range(2)]
        seln = at("seln", MISC + 9.25, [P, NC, 4, CAP], F32R)
        x_hi = at("x_hi", 152, [P, NC, D], F32R)
        x_lo = at("x_lo", 132, [P, NC, D], F32R)
        xg = [at("xg0", MISC + 14.25, [P, KT, 4, CAP]), at("xg1", 28, [P, KT, 4, CAP])]
        sg = [at(f"sg{i}", MISC + 22.25 + 0.5 * i, [P, P]) for i in range(2)]
        hh = [at(f"hh{i}", MISC + 23.25 + 0.5 * i, [P, P]) for i in range(2)]
        hT = [at(f"hT{i}", MISC + 24.25 + 0.5 * i, [P, P]) for i in range(2)]
        ys = [at(f"ys{i}", MISC + (25.25, 27.25, 32, 34)[i], [P, 512]) for i in range(4)]
        idx = [at(f"idx{i}", MISC + 29.25 + 0.03125 * i, [P, 1], I32) for i in range(4)]
        yab = [at(f"yab{c}", 132 + 8 * c, [P, 2, D]) for c in range(NC)]
        wc = [at(f"wc{s}", RING + 24 * s, [P, KT, 3, P]) for s in range(2)]
        wc_lo = [at(f"wc_lo{s}", RING + 24 * s, [P, KT, 3, P], F32R) for s in range(2)]
        wc_hi = [at(f"wc_hi{s}", RING + 24 * s + 12, [P, KT, 3, P], F32R) for s in range(2)]
        xc_lo = at("xc_lo", RING + 48, [P, KT, T], F32R)
        g_hi = at("g_hi", 152, [P, KT, T], F32R)
        g_lo = at("g_lo", MISC, [P, KT, T], F32R)
        woc = [at("woc0", RING + 65, [P, KT, 512]), at("woc1", RING, [P, KT, 512])]
        woc_lo = [at("woc_lo0", RING + 65, [P, KT, 512], F32R), at("woc_lo1", RING, [P, KT, 512], F32R)]
        woc0_hi = [at("woc0_hi0", RING + 81, [P, KT // 2, 512], F32R), at("woc0_hi1", MISC + 27.5, [P, KT // 2, 512], F32R)]
        woc1_hi = at("woc1_hi", RING + 16, [P, KT, 512], F32R)
        UW = 2 + SEQ + 2 + DEC
        gT = at("gT", MISC, [P, KT, T])
        u = at("u", MISC + 17, [P, UW])
        hc = [at(f"hc{i}", MISC + 21.5 + 1.25 * i, [P, HALF]) for i in range(2)]
        cv = at("cv", MISC + 24, [P, T])
        hist = at("hist", MISC + 26.25, [P, KT, 2])
        tails = at("tails", MISC + 26.5, [P, 2, KT, 2])

        bank = [ctx.enter_context(nc.psum_tensor(f"bank{i}", [P, 512], F32)) for i in range(8)]

        rev_dram = nc.dram_tensor("rev_bias", [NH, 640], F32, kind="Internal").ap()
        revs_dram = nc.dram_tensor("rev_bias_copies", [NH, 32, 640], F32, kind="Internal").ap()
        y_dram = [nc.dram_tensor(f"y_rows{i}", [2 * T * 2, 512], F32, kind="Internal").ap() for i in range(2)]

        x_in = sem("x_in"); gmix_in = sem("gmix_in"); gffn_in = sem("gffn_in"); tab_in = sem("tab_in");
        pool_c = sem("pool_c"); const_ok = sem("const_ok")
        h_ok = sem("h_ok")
        sq_done = sem("sq_done"); ms_ok = sem("ms_ok"); rt_ok = sem("rt_ok")
        xn_ok = sem("xn_ok"); xt_mm = sem("xt_mm"); xt_a = sem("xt_a"); xt_d = sem("xt_d")
        dch = sem("dch"); ach = sem("ach")
        wab_in = [sem(f"wab_in{s}") for s in range(3)]
        w_hi = sem("w_hi"); w_lo = sem("w_lo")
        z_hi = sem("z_hi"); z_lo = sem("z_lo")
        z_mm = sem("z_mm"); z_free = [sem(f"z_free{b}") for b in range(4)]

        f_ok = sem("f_ok"); ln_ok = sem("ln_ok"); cum_ok = sem("cum_ok"); exp_ok = sem("exp_ok")
        hg_ok = sem("hg_ok")
        qsq_ok = sem("qsq_ok"); qms_ok = sem("qms_ok"); qrt_ok = sem("qrt_ok"); qk_ok = sem("qk_ok")
        v_ok = sem("v_ok"); out_dma = sem("out_dma"); qkT_mm = sem("qkT_mm"); qkT_ok = sem("qkT_ok")
        rb_dma = sem("rb_dma"); rc_dma = sem("rc_dma"); bias_in = sem("bias_in");
        cache_in = sem("cache_in"); kc_mm = sem("kc_mm"); kc_ok = sem("kc_ok"); st_in = sem("st_in")
        ko_mm = sem("ko_mm"); ko_ok = sem("ko_ok"); vx_ok = sem("vx_ok"); a_mm = sem("a_mm"); a_ok = sem("a_ok")
        u_mm = sem("u_mm"); st_ok = sem("st_ok"); o_mm = sem("o_mm"); osq_ok = sem("osq_ok")
        stat_mm = sem("stat_mm"); orms_ok = sem("orms_ok"); zB_ok = sem("zB_ok")
        s_mm = sem("s_mm"); s_ok = sem("s_ok"); p_ok = sem("p_ok"); pT_mm = sem("pT_mm")
        pT_a = sem("pT_a"); pT_d = sem("pT_d"); pv_mm = sem("pv_mm"); oa_ok = sem("oa_ok")
        oaT_mm = sem("oaT_mm"); zAh_ok = sem("zAh_ok"); zA_ok = sem("zA_ok")
        wo_in = [sem(f"wo_in{s}") for s in range(2)]
        op_mm = sem("op_mm"); op_add = sem("op_add")
        wr_in = sem("wr_in"); lg_mm = sem("lg_mm"); lg_ok = sem("lg_ok"); ge_ok = sem("ge_ok"); gx_ok = sem("gx_ok")
        e2_ok = sem("e2_ok"); ex_ok = sem("ex_ok")
        msk_ok = sem("msk_ok"); rk_mm = sem("rk_mm"); rk_ok = sem("rk_ok"); xhi_ok = sem("xhi_ok"); xlo_ok = sem("xlo_ok"); cm_mm = sem("cm_mm"); cnt_ok = sem("cnt_ok")
        w13_in = [sem(f"w13_in{s}") for s in range(4)]
        w2_in = [sem(f"w2_in{s}") for s in range(4)]
        sel_ok = sem("sel_ok"); g_mm = sem("g_mm"); ix_mm = sem("ix_mm"); xg_a = sem("xg_a"); xg_d = sem("xg_d")
        ix_ok = sem("ix_ok"); h_mm = sem("h_mm"); sg_ok = sem("sg_ok"); hh_ok = sem("hh_ok"); t_mm = sem("t_mm")
        ht_ok = sem("ht_ok"); y_mm = sem("y_mm"); ys_ok = sem("ys_ok"); scat = [sem(f"scat{j}") for j in range(4)]
        yab_in = [sem(f"yab_in{c}") for c in range(NC)]

        ov = [{n: sem(f"ov{l}_{n}") for n in ("free", "w", "rk", "sel", "mm", "xg", "ix", "sg", "hh", "ht", "ys", "sc")}
              for l in range(2)]
        for o in ov:
            o.update({n: o["mm"] for n in ("g", "ixm", "h", "t", "y")})
        wc_in = [sem(f"wc_in{s}") for s in range(2)]
        c_mm = sem("c_mm"); hc_ok = sem("hc_ok"); cg_ok = sem("cg_ok"); tail_ok = sem("tail_ok")
        lbm_ok = sem("lbm_ok"); lbe_ok = sem("lbe_ok"); st0_ok = sem("st0_ok"); ys_free = sem("ys_free")
        woc_in = [sem(f"woc_in{s}") for s in range(2)]
        y_out = sem("y_out")

        NXT = 2 * NC
        PAIRS = NE // 2

        block = ctx.enter_context(nc.Block())


        class Chain:
            def __init__(self, eng, done):
                self.eng, self.done, self.n, self.run_on = eng, done, 0, 0

            def __call__(self, ins):
                self.n += 1
                ins.then_inc(self.done, 1)
                self.eng.wait_ge(self.done, self.n + self.run_on)

            def loop(self, i, steps, times):
                self.run_on, self.steps, self.times, self.first = i * steps, steps, times, self.n

            def end(self):
                assert self.n == self.first + self.steps, (self.n - self.first, self.steps)
                self.n, self.run_on = self.first + self.steps * self.times, 0

        def bc(ap, shape):
            return ap.to_broadcast(shape)

        @block.sync
        def _(sp):
            for c in range(4):
                sp.dma_start(H[:, c, :], x_prompt[0, c * P:(c + 1) * P, :]).then_inc(x_in, 16)
            sp.dma_start(H[0:DEC, 4, :], x_sample[0, :, :]).then_inc(x_in, 16)
            sp.dma_start(gmix[:], norm_mix[0:1, :].partition_broadcast(P)).then_inc(gmix_in, 16)

            def group_load(n):
                first = GROUPS[n // 2] * DA + (n % 2) * HG
                sp.dma_start(wab[n % 3][:], w_in_ab[0, :, first:first + HG].rearrange("(k p) n -> p k n", p=P))\
                    .then_inc(wab_in[n % 3], 16)
            for n in range(3):
                group_load(n)
            with nc.allow_non_contiguous_dma(reason="per-feature tables, one element per partition"):
                sp.dma_start(lbl[:].rearrange("p (r m) -> p r m", r=2), hgrn_lb_logits.rearrange("r (m p) -> p r m", p=P)).then_inc(tab_in, 16)
                sp.dma_start(onorm[:], hgrn_out_norm[0].rearrange("(m p) -> p m", p=P)).then_inc(tab_in, 16)
                sp.dma_start(convw[:].rearrange("p (j k) -> p j k", j=3), conv_w[0].rearrange("j (k p) -> p j k", p=P)).then_inc(tab_in, 16)
                sp.dma_start(rev_dram[:, 384:639].unsqueeze(2), bass.AP(rel_bias.tensor, 2 * REL - 1, [[2 * REL + 1, NH], [-1, 255], [1, 1]])).then_inc(rb_dma, 16)
                sp.dma_start(rev_dram[:, 0:384].unsqueeze(2), bass.AP(rel_bias.tensor, 2 * REL, [[2 * REL + 1, NH], [0, 384], [1, 1]])).then_inc(rb_dma, 16)
            sp.dma_start(qgain[:], q_norm[0:1, :].partition_broadcast(P)).then_inc(tab_in, 16)
            sp.dma_start(kgain[:], k_norm[0:1, :].partition_broadcast(P)).then_inc(tab_in, 16)
            sp.dma_start(gffn[:], norm_ffn[0:1, :].partition_broadcast(P)).then_inc(gffn_in, 16)
            for n in range(3, 14):
                sp.wait_ge(z_mm, UNIT_END[n - 3])
                group_load(n)
            sp.wait_ge(rb_dma, 32)
            sp.dma_start(revs_dram[:, :, 0:639], bc(rev_dram[:, 0:639].unsqueeze(1), [NH, 32, 639])).then_inc(rc_dma, 16)
            sp.dma_start(nk_s[0, 0, 0:PAST - DEC], cache_a_k[0, 0, DEC:]).then_inc(out_dma, 16)
            sp.dma_start(nv_s[0, 0, 0:PAST - DEC], cache_a_v[0, 0, DEC:]).then_inc(out_dma, 16)
            sp.wait_ge(qk_ok, 4 * NC)
            sp.dma_start(nk_p[0, 0].rearrange("(c p) h d -> p c (h d)", p=P), k_tok[:, 0:4, :]).then_inc(out_dma, 16)
            sp.dma_start(nk_s[0, 0, PAST - DEC:].rearrange("t h d -> t (h d)"), k_tok[0:DEC, 4, :]).then_inc(out_dma, 16)
            sp.wait_ge(rc_dma, 16)
            sp.wait_ge(z_mm, UNIT_END[-1])
            for a in range(4):
                sp.dma_start(bias[32 * a:32 * a + 32, :, :],
                             bass.AP(revs_dram.tensor, P - 1 - 32 * a, [[639, 32], [32 * 640, NH], [1, 512]])).then_inc(bias_in, 16)
            sp.wait_ge(v_ok, 2 * NC)
            sp.dma_start(nv_p[0, 0].rearrange("(c p) h d -> p c (h d)", p=P), va[:, 0:4, :]).then_inc(out_dma, 16)
            sp.dma_start(nv_s[0, 0, PAST - DEC:].rearrange("t h d -> t (h d)"), va[0:DEC, 4, :]).then_inc(out_dma, 16)
            sp.wait_ge(qkT_mm, 2 * NC)
            sp.wait_ge(out_dma, 16 * 6)
            sp.dma_start(kc[:], cache_a_k[0, 0].rearrange("t h d -> t (h d)")).then_inc(cache_in, 16)
            sp.dma_start(vc[:], cache_a_v[0, 0].rearrange("t h d -> t (h d)")).then_inc(cache_in, 16)
            sp.wait_ge(o_mm, 3)
            sp.wait_ge(st_ok, 4)
            sp.dma_start(st[0][:, 0, :, :], state_hgrn[0, 0].rearrange("(a b) k v -> (b k) a v", b=2)).then_inc(st_in, 16)
            sp.dma_start(nh_p[0, 0].rearrange("(a b) k v -> (b k) a v", b=2), st[1][:, 8, :, :]).then_inc(out_dma, 16)
            sp.wait_ge(st_ok, 5)
            sp.dma_start(nh_s[0, 0].rearrange("(a b) k v -> (b k) a v", b=2), st[0][:, 2, :, :]).then_inc(out_dma, 16)
            sp.wait_ge(zB_ok, NC)
            sp.wait_ge(out_dma, 16 * 8)
            for s in range(2):
                sp.dma_start(wo[s][:], w_out_ab[0, :, s * 512:(s + 1) * 512].rearrange("(k p) n -> p k n", p=P)).then_inc(wo_in[s], 16)

            def w13_load(l, e, s, done):
                for part, w in enumerate((w1, w3)):
                    sp.dma_start(w13[s][:, :, part, :], w[l, bass.ds(e, 1)].rearrange("e (k p) f -> p (e k) f", p=P)).then_inc(done, 16)

            def w2_load(l, e, s, done):
                sp.dma_start(w2s[s][:], w2[l, bass.ds(e, 1)].rearrange("e (a p) n -> p (e a) n", p=P)).then_inc(done, 16)

            def first_load(l, j):
                s = (j + 2) % 4
                w13_load(l, j, s, w13_in[s])
                w2_load(l, j, s, w2_in[s])

            def router_load(l):
                sp.dma_start(wr[:, :, 0:NG], w_group[l].rearrange("(k p) n -> p k n", p=P)).then_inc(wr_in, 16)
                sp.dma_start(wr[:, :, NG:NR], w_expert[l].rearrange("(k p) n -> p k n", p=P)).then_inc(wr_in, 16)
                sp.dma_start(biasr[:, 0:NG], b_group[l:l + 1, :].partition_broadcast(P)).then_inc(wr_in, 16)
                sp.dma_start(biasr[:, NG:NR], b_expert[l:l + 1, :].partition_broadcast(P)).then_inc(wr_in, 16)

            wcv = w_in_c[0].rearrange("(k p) (a m n) -> a m p k n", p=P, a=3, n=P)

            def conv_load(m, s):
                for a in range(3):
                    sp.dma_start(wc[s][:, :, a, :], wcv[a, bass.ds(m, 1)].rearrange("m p k n -> p (m k) n")).then_inc(wc_in[s], 16)

            def mixture(l):
                with sp.Fori(0, NE // 4 - 1) as i:
                    for j in range(4):
                        s = (j + 2) % 4
                        sp.wait_ge(h_mm, i * 4 + (l * NE + j + 1))
                        w13_load(l, 4 * i + 4 + j, s, w13_in[s])
                        sp.wait_ge(y_mm, i * 4 + (l * NE + j + 1))
                        w2_load(l, 4 * i + 4 + j, s, w2_in[s])
                sp.wait_ge(y_mm, NE * (l + 1))
                if l == 0:
                    sp.dma_start(gmix[:], norm_mix[1:2, :].partition_broadcast(P)).then_inc(gmix_in, 16)
                    for s in range(2):
                        conv_load(s, s)
                sp.wait_ge(cnt_ok, l + 1)
                for j in range(4):
                    sp.wait_ge(scat[j], 16 * (NE // 4) * (l + 1))
                most = sp.value_load(cnt_i[0:1, l:l + 1], min_val=0, max_val=T)
                with sp.If(most > CAP), sp.Fori(0, ROUNDS - 1) as r:
                    with sp.If(most > CAP * r + CAP):
                        with sp.Fori(0, NE) as e:
                            sp.wait_ge(ov[l]["free"], r * NE + e + 1)
                            w13_load(l, e, 3, ov[l]["w"])
                            w2_load(l, e, 3, ov[l]["w"])
                        sp.wait_ge(ov[l]["free"], r * NE + NE + 1)
                        sp.nop(nofuse=True)
                rows = y_dram[l].rearrange("(r b) d -> r (b d)", b=2)
                for c in range(NC):
                    for i in range(2):
                        first = i * T + c * P
                        sp.dma_start(yab[c][0:ROWS[c], i, :], rows[first:first + ROWS[c], :]).then_inc(yab_in[c], 16)

            sp.wait_ge(oaT_mm, NC)
            router_load(0)
            sp.wait_ge(op_mm, NC)
            first_load(0, 2)
            sp.wait_ge(op_mm, 2 * NC)
            for j in (0, 1, 3):
                first_load(0, j)
            mixture(0)

            sp.dma_start(gffn[:], norm_ffn[1:2, :].partition_broadcast(P)).then_inc(gffn_in, 16)
            sp.wait_ge(lg_ok, 1)
            sp.wait_ge(lg_mm, 1)
            router_load(1)
            with nc.allow_non_contiguous_dma(reason="two frames of each feature"):
                for r in range(2):
                    sp.dma_start(hist[:, :, r], state_conv[0, 0, r].rearrange("(k p) -> p k", p=P)).then_inc(st_in, 16)
            def woc_load(s):
                sp.dma_start(woc[s][:], w_out_c[0, :, s * 512:(s + 1) * 512].rearrange("(k p) n -> p k n", p=P)).then_inc(woc_in[s], 16)
            woc_load(0)
            with sp.Fori(0, KT // 2 - 1) as i:
                for s in range(2):
                    sp.wait_ge(c_mm, i * 4 + (2 * s + 2))
                    conv_load(2 * i + (2 + s), s)
            sp.wait_ge(c_mm, 2 * KT - 2)
            woc_load(1)
            sp.wait_ge(tail_ok, KT)
            with nc.allow_non_contiguous_dma(reason="two frames of each feature"):
                for j, dst in enumerate((nconv_p, nconv_s)):
                    for r in range(2):
                        sp.dma_start(dst[0, 0, r, :].rearrange("(k p) -> p k", p=P), tails[:, j, :, r]).then_inc(out_dma, 16)
            sp.wait_ge(op_mm, 3 * NC)
            for j in (0, 1):
                first_load(1, j)
            sp.wait_ge(op_mm, 4 * NC)
            for j in (2, 3):
                first_load(1, j)
            mixture(1)
            for c in range(NC):
                sp.wait_ge(h_ok, 3 * NC + c + 1)
                dst = y_prompt[0, c * P:(c + 1) * P, :] if c < 4 else y_sample[0, :, :]
                sp.dma_start(dst, H[0:ROWS[c], c, :]).then_inc(y_out, 16)
            sp.wait_ge(y_out, 16 * NC)
            sp.wait_ge(out_dma, 16 * 12)

        @block.gpsimd
        def _(pool):
            tie = Chain(pool, pool_c)

            def tri(t, view, pattern, base, mult, op, fill=0.0):
                tie(pool.affine_select(out=view, in_=view, compare_op=op, fill=fill, base=base, pattern=pattern,
                                       channel_multiplier=mult))
            tie(pool.memset(H[32:64, 4, :], 0.0))
            tie(pool.memset(H[64:128, 4, :], 0.0))
            tie(pool.memset(ident[:], 0.0))
            tri(ident, ident[:], [[-1, P]], 0, 1, ALU.not_equal, 1.0)
            tie(pool.memset(upper[:], 1.0))
            tri(upper, upper[:], [[1, P]], 0, -1, ALU.is_gt)
            tie(pool.memset(ones[:], 1.0))
            tie(pool.memset(head_mean[:], 0.0))
            tie(pool.memset(head_mean[0:HD, 0:HD], 1.0 / HD))
            tie(pool.memset(head_mean[HD:P, HD:P], 1.0 / HD))
            tie(pool.memset(blk_mask[:], 1.0))
            tri(blk_mask, blk_mask[:], [[1, P]], 0, -1, ALU.is_ge)
            tri(blk_mask, blk_mask[:].rearrange("p (b t) -> p b t", t=BLK), [[-BLK, P // BLK], [0, BLK]], 0, 1, ALU.is_ge)
            tie(pool.memset(blk_sel[:], 1.0))
            tri(blk_sel, blk_sel[:], [[-32, 4]], 0, 1, ALU.is_ge)
            tri(blk_sel, blk_sel[:], [[32, 4]], BLK - 1, -1, ALU.is_ge)
            tie(pool.iota(slot_no[:], [[1, CAP]], base=0, channel_multiplier=0, allow_small_or_imprecise_dtypes=True))
            tie(pool.iota(frame_no[:], [[P, NC]], base=0, channel_multiplier=1, allow_small_or_imprecise_dtypes=True))
            tie(pool.iota(rev4[:], [[-1, NG]], base=NG, channel_multiplier=0, allow_small_or_imprecise_dtypes=True))
            tie(pool.iota(rev8[:], [[-1, EPG]], base=EPG, channel_multiplier=0, allow_small_or_imprecise_dtypes=True))
            tie(pool.memset(frame_ok[:], 1.0))
            tri(frame_ok, frame_ok[:], [[-P, NC]], T - 1, -1, ALU.is_ge)
            tie(pool.memset(epsc[:], EPS))
            tie(pool.memset(reset[:], 1.0))
            tie(pool.memset(reset[:].rearrange("p (b t) -> p b t", t=BLK)[:, :, 0], 0.0))
            pool.nop().then_inc(const_ok, 1)
            pool.nop().then_inc(ys_free, 4)

            def split(raw, hi, lo):
                for r, x, y in zip(raw, hi, lo):
                    last = pool.tensor_copy(x, r)
                last.then_inc(w_hi, 1)
                pool.wait_ge(w_hi, split.n + 1)
                for r, x, y in zip(raw, hi, lo):
                    last = pool.tensor_tensor(y, r, x.bitcast(F32), ALU.subtract)
                last.then_inc(w_lo, 1)
                split.n += 1
            for n in range(14):
                pool.wait_ge(w_hi, n + 1)
                pool.tensor_tensor(wab_lo[n % 3][:], wab[n % 3][:], wab_hi[n % 3][:].bitcast(F32), ALU.subtract).then_inc(w_lo, 1)
            split.n = 14
            for s in range(2):
                pool.wait_ge(wo_in[s], 16)
                if s == 1:
                    pool.wait_ge(s_mm, NC * NH)
                split([wo[s][:]], [wo_hi[s][:]], [wo_lo[s][:]])

            def conv_splits():
                with pool.Fori(0, KT // 2) as i:
                    for s in range(2):
                        pool.wait_ge(wc_in[s], i * 48 + 48)
                        pool.wait_ge(w_hi, i * 2 + (16 + s + 1))
                        pool.tensor_tensor(wc_lo[s][:], wc[s][:], wc_hi[s][:].bitcast(F32), ALU.subtract).then_inc(w_lo, 1)

            for l in range(2):
                yd = y_dram[l]
                if l == 1:
                    conv_splits()
                    split.n += KT
                    k2 = KT // 2
                    pool.wait_ge(woc_in[0], 16)
                    split([woc[0][:, 0:k2, :], woc[0][:, k2:KT, :]], [woc0_hi[0][:], woc0_hi[1][:]],
                          [woc_lo[0][:, 0:k2, :], woc_lo[0][:, k2:KT, :]])
                    pool.wait_ge(woc_in[1], 16)
                    pool.wait_ge(c_mm, 2 * KT)
                    split([woc[1][:]], [woc1_hi[:]], [woc_lo[1][:]])

                def scatter(i, done):
                    pool.indirect_dma_start(yd[:, :], bass.IndirectOffsetOnAxis(ap=idx[i][:, 0:1].bitcast(U32), axis=0),
                                            ys[i][:, :], None, bounds_check=4 * T - 1, oob_is_err=False).then_inc(done, 16)
                for c in range(NC):
                    pool.wait_ge(xhi_ok, NC * l + c + 1)
                    pool.tensor_tensor(x_lo[:, c, :], XN[:, c, :], x_hi[:, c, :].bitcast(F32), ALU.subtract).then_inc(xlo_ok, 1)

                def stored(i, j):
                    pool.wait_ge(scat[j], i * 16 + 16 * (l * (NE // 4) + 1))
                    pool.nop().then_inc(ys_free, 1)

                def scatters(i, first):
                    for j in range(4):
                        pool.wait_ge(ix_ok, i * 2 + (l * (PAIRS + 1) + j // 2 + 1))
                        pool.wait_ge(ys_ok, i * 4 + (l * NE + j + 3))
                        pool.nop(nofuse=True)
                        scatter(j, scat[j])
                        if j >= 2:
                            stored(i, j - 2)
                        elif not first:
                            stored(i - 1, j + 2)
                scatters(0, True)
                with pool.Fori(1, NE // 4) as i:
                    scatters(i, False)
                for j in (2, 3):
                    stored(NE // 4 - 1, j)
                pool.wait_ge(cnt_ok, l + 1)
                most = pool.value_load(cnt_i[0:1, l:l + 1], min_val=0, max_val=T)
                o = ov[l]
                pool.nop().then_inc(o["free"], 1)
                with pool.If(most > CAP), pool.Fori(0, ROUNDS - 1) as r:
                    with pool.If(most > CAP * r + CAP):
                        with pool.Fori(0, NE) as e:
                            pool.wait_ge(o["ix"], r * NE + e + 1)
                            pool.wait_ge(o["ys"], r * NE + e + 1)
                            pool.nop(nofuse=True)
                            scatter(0, o["sc"])
                            pool.wait_ge(o["sc"], r * (16 * NE) + e * 16 + 16)
                            pool.nop().then_inc(o["free"], 1)

        @block.tensor
        def _(pe):
            def norm_transposes(n):
                for c in range(NC):
                    pe.wait_ge(xn_ok, NC * n + c + 1)
                    if n == 0 and c == 0:
                        pe.wait_ge(const_ok, 1)
                    low = 6 if n % 2 == 1 or c % 2 == 0 else 4
                    if n % 2 == 0 and c > 1:
                        pe.wait_ge(xt_d, NC * n + c - 1)
                    for half in range(2):
                        if n % 2 == 1 and c > 0:
                            pe.wait_ge(xt_a if half == 0 else xt_d, NC * n + c)
                        for kk in range(4):
                            k = 4 * half + kk
                            last = pe.transpose(bank[low + half][:, kk * P:kk * P + ROWS[c]], XN[0:ROWS[c], c, k * P:(k + 1) * P],
                                                ident[0:ROWS[c], 0:ROWS[c]])
                        last.then_inc(xt_mm, 1)

            norm_transposes(0)
            pe.wait_ge(xt_a, NC)
            pe.wait_ge(xt_d, NC)
            u_ = 0
            for n in range(14):
                pe.wait_ge(w_lo, n + 1)
                wh, wl = wab_hi[n % 3], wab_lo[n % 3]
                for a in range(4 if n < 6 else NC):
                    if u_ >= 4:
                        pe.wait_ge(z_free[u_ % 4], u_ // 4)
                    for k in range(KT):
                        for j, (w, x) in enumerate(((wh, xc_hi), (wh, xp_lo), (wl, xc_hi))):
                            flags = dict(start=k == 0 and j == 0, stop=k == KT - 1 and j == 2)
                            if n < 6:
                                m, half = a // 2, a % 2
                                last = pe.matmul(bank[u_ % 4][:, 0:HALF], w[:, k, m * P:(m + 1) * P],
                                                 x[:, k, half * HALF:(half + 1) * HALF], **flags)
                            else:
                                last = pe.matmul(bank[u_ % 4][0:ROWS[a], 0:HG], x[:, k, a * P:a * P + ROWS[a]], w[:, k, :], **flags)
                    last.then_inc(z_mm, 1)
                    u_ += 1
            for i in range(2 * NC):
                c, src = i // 2, (q_tok, k_tok)[i % 2]
                if i == 0:
                    pe.wait_ge(qk_ok, 4 * NC)
                if i >= 2:
                    pe.wait_ge(qkT_ok, i - 1)
                for m in range(4):
                    last = pe.transpose(bank[4 + i % 2][:, m * P:m * P + ROWS[c]], src[0:ROWS[c], c, m * P:(m + 1) * P],
                                        ident[0:ROWS[c], 0:ROWS[c]])
                last.then_inc(qkT_mm, 1)

            def hgrn_in(c):
                n, t0 = ROWS[c], c * P
                if c == 0:
                    pe.wait_ge(hg_ok, 3)
                    for b in range(4):
                        pe.wait_ge(z_free[b], 16)
                    pe.wait_ge(qkT_ok, 2 * NC)
                else:
                    pe.wait_ge(orms_ok, c - 1) if c > 1 else None
                for m in range(4):
                    last = pe.transpose(bank[0][0:n, m * P:(m + 1) * P], koutT[:, m, t0:t0 + n], ident[:])
                last.then_inc(ko_mm, 1)
                if c > 0:
                    pe.wait_ge(a_ok, 2 * c)
                for m in range(4):
                    for par in range(2):
                        last = pe.matmul(bank[1 + par][0:n, m * P:m * P + n], kinT[64 * par:64 * par + 64, m, t0:t0 + n],
                                         qdecT[64 * par:64 * par + 64, m, t0:t0 + n], start=True, stop=True)
                last.then_inc(a_mm, 1)
                pe.wait_ge(ko_ok, c + 1)
                pe.wait_ge(vx_ok, c + 1)
                if c > 0:
                    pe.wait_ge(st_ok, c)
                for h in range(NH):
                    for r in range(n // 32):
                        last = pe.matmul(bank[3 + r][64 * (h % 2):64 * (h % 2) + 64, (h // 2) * P:(h // 2 + 1) * P],
                                         kout[c % 2][32 * r:32 * r + 32, h * HD:(h + 1) * HD],
                                         vx[c % 2][32 * r:32 * r + 32, h, :, :].rearrange("p i v -> p (i v)"), start=True, stop=True)
                last.then_inc(u_mm, 1)

            def hgrn_out(c):
                n, t0 = ROWS[c], c * P
                pe.wait_ge(a_ok, 2 * c + 2)
                pe.wait_ge(st_ok, c + 1)
                if c > 0:
                    pe.wait_ge(zB_ok, c)
                for m in range(4):
                    out = [bank[7][64 * par:64 * par + 64, m * P:m * P + n] for par in range(2)]
                    for par in range(2):
                        h = 2 * m + par
                        pe.matmul(out[par], vb[0:n, c, h * HD:(h + 1) * HD], am[c % 2][0:n, par, m, 0:n], start=True, stop=False)
                    for b in range(n // BLK):
                        for par in range(2):
                            lo = 64 * par
                            last = pe.matmul(out[par][:, b * BLK:(b + 1) * BLK], st[c % 2][lo:lo + 64, b, m, :],
                                             qdecT[lo:lo + 64, m, t0 + b * BLK:t0 + (b + 1) * BLK],
                                             start=False, stop=b == n // BLK - 1)
                last.then_inc(o_mm, 1)
                pe.wait_ge(osq_ok, c + 1)
                pe.wait_ge(ko_ok, min(c + 2, NC))
                for m in range(4):
                    last = pe.matmul(bank[0][:, m * P:m * P + n], head_mean[:], osq[:, m, 0:n], start=True, stop=True)
                last.then_inc(stat_mm, 1)

            hgrn_in(0)
            for c in range(NC):
                if c + 1 < NC:
                    hgrn_in(c + 1)
                hgrn_out(c)

            NU = NC * NH
            pe.wait_ge(cache_in, 32)
            pe.wait_ge(zB_ok, NC)
            pe.wait_ge(orms_ok, NC)
            for m in range(4):
                last = pe.transpose(bank[6][:, m * P:(m + 1) * P], kc[:, m * P:(m + 1) * P], ident[:])
            last.then_inc(kc_mm, 1)

            def scores(i):
                c, h = divmod(i, NH)
                lo, m = 64 * (h % 2), h // 2
                if i >= 2:
                    pe.wait_ge(s_ok, i - 1)
                q = qT[lo:lo + 64, m, c * P:c * P + ROWS[c]]
                if c < 4:
                    last = pe.matmul(bank[i % 2][:, 0:P * (c + 1)], q, kT[lo:lo + 64, m, 0:P * (c + 1)], start=True, stop=True)
                else:
                    pe.matmul(bank[i % 2][0:DEC, 0:PAST], q, kcT[lo:lo + 64, m, :], start=True, stop=True)
                    last = pe.matmul(bank[i % 2][0:DEC, PAST:PAST + DEC], q, kT[lo:lo + 64, m, SEQ:T], start=True, stop=True)
                last.then_inc(s_mm, 1)

            def keys(c):
                return [(P * j, P) for j in range(c + 1)] if c < 4 else [(0, PAST), (PAST, DEC)]

            def probs_T(i):
                c, h = divmod(i, NH)
                n = ROWS[c]
                pe.wait_ge(p_ok, i + 1)
                if i >= 2:
                    pe.wait_ge(pT_a if i % 2 == 0 else pT_d, i // 2)
                for j, (k0, nk) in enumerate(keys(c)):
                    last = pe.transpose(bank[2 + i % 2][0:nk, j * P:j * P + n], pr[i % 2][0:n, k0:k0 + nk], ident[0:n, 0:n])
                last.then_inc(pT_mm, 1)

            def values(i):
                c, h = divmod(i, NH)
                n = ROWS[c]
                pe.wait_ge(pT_a if i % 2 == 0 else pT_d, i // 2 + 1)
                if h == 0 and c >= 2:
                    pe.wait_ge(oa_ok, c - 1)
                for j, (k0, nk) in enumerate(keys(c)):
                    v = va[:, j, :] if c < 4 else (vc[:, :], va[0:DEC, 4, :])[j]
                    last = pe.matmul(bank[4 + c % 2][0:n, h * HD:(h + 1) * HD], prT[i % 2][0:nk, j, 0:n],
                                     v[:, h * HD:(h + 1) * HD], start=j == 0, stop=j == len(keys(c)) - 1)
                last.then_inc(pv_mm, 1)

            def heads_T(c):
                n = ROWS[c]
                pe.wait_ge(oa_ok, c + 1)
                pe.wait_ge(kc_ok, 1) if c == 0 else pe.wait_ge(zA_ok, c)
                for m in range(4):
                    last = pe.transpose(bank[6][:, m * P:m * P + n], oa[c % 2][0:n, m * P:(m + 1) * P], ident[0:n, 0:n])
                last.then_inc(oaT_mm, 1)

            pe.wait_ge(kc_ok, 1)
            for i in range(NU + 4):
                if i < NU:
                    scores(i)
                if 1 <= i <= NU:
                    probs_T(i - 1)
                if 2 <= i <= NU + 1:
                    values(i - 2)
                if i >= 11 and (i - 11) % NH == 0:
                    heads_T((i - 11) // NH)
            pe.wait_ge(zA_ok, NC)

            def project_out(n, z, w, splits):
                for i in range(2 * NC):
                    s, c = divmod(i, NC)
                    if c == 0:
                        pe.wait_ge(w_lo, splits + s)
                    if i < NC:
                        z.arrived(c)
                    if i >= 4:
                        pe.wait_ge(op_add, 2 * NC * n + i - 3)
                    for k in range(KT):
                        for j, (a, b) in enumerate(((0, 0), (1, 0), (0, 1))):
                            last = pe.matmul(bank[i % 4][0:ROWS[c], :], z(a, k)[:, c * P:c * P + ROWS[c]], w(b, k, s),
                                             start=k == 0 and j == 0, stop=k == KT - 1 and j == 2)
                    last.then_inc(op_mm, 1)

            def z_ab(part, k):
                return ((zA_hi, zA_lo), (zB_hi, zB_lo))[k // 4][part][:, k % 4, :]
            z_ab.arrived = lambda c: pe.wait_ge(z_lo, 1) if c == 0 else None
            pe.wait_ge(zA_ok, NC)
            project_out(0, z_ab, lambda part, k, s: (wo_hi, wo_lo)[part][s][:, k, :], 15)

            def mixture(l):
                norm_transposes(2 * l + 1)
                pe.wait_ge(xt_a, NC * (2 * l + 2))
                pe.wait_ge(xt_d, NC * (2 * l + 2))
                pe.wait_ge(op_add, 2 * NC * (l + 1))
                pe.wait_ge(wr_in, 64 * (l + 1))
                for c in range(NC):
                    for k in range(KT):
                        last = pe.matmul(bank[0][0:ROWS[c], c * NR:(c + 1) * NR], XT[:, k, c * P:c * P + ROWS[c]], wr[:, k, :],
                                         start=k == 0, stop=k == KT - 1)
                last.then_inc(lg_mm, 1)
                pe.wait_ge(msk_ok, l + 1)
                mask = rt[0][:].rearrange("p c n -> p (c n)")
                pe.matmul(bank[1][:, 0:NC * NE], upper[:], mask, start=True, stop=False)
                for j in range(1, NC):
                    last = pe.matmul(bank[1][:, j * NE:NC * NE], ones[:], mask[:, 0:(NC - j) * NE], start=False, stop=j == NC - 1)
                last.then_inc(rk_mm, 1)
                pe.wait_ge(rk_ok, l + 1)
                pe.matmul(bank[2][0:1, 0:P], c1[7][:, 0:1], ident[:], start=True, stop=True).then_inc(cm_mm, 1)

                def gather(half, q):
                    for kk in range(4):
                        for c in range(NC):
                            for part in (x_hi, x_lo):
                                last = pe.matmul(bank[kk // 2][:, (kk % 2) * 4 * CAP:(kk % 2 + 1) * 4 * CAP],
                                                 part[:, c, (4 * half + kk) * P:(4 * half + kk + 1) * P],
                                                 seln[:, c, :, :].rearrange("p a s -> p (a s)"),
                                                 start=c == 0 and part is x_hi, stop=c == NC - 1 and part is x_lo)
                    last.then_inc(q["g"], 1)

                def numbers(e, q):
                    for b in range(2):
                        for c in range(NC):
                            last = pe.matmul(bank[2][:, 2 * b:2 * b + 2], seln[:, c, 2 * b:2 * b + 2, :].rearrange("p a s -> p (a s)"),
                                             dv[:, c, bass.ds(e + 2 * b, 2)], start=c == 0, stop=c == NC - 1)
                    last.then_inc(q["ixm"], 1)

                def hidden(s, buf, j, hb, q):
                    for k in range(KT):
                        for f in range(2):
                            last = pe.matmul(bank[hb][64 * f:64 * f + 64, 0:2 * P].rearrange("p (w j) -> p w j", w=2), xg[buf][:, k, j, :],
                                             w13[s][:, k, :, f * P:(f + 1) * P], start=k == 0, stop=k == KT - 1)
                    last.then_inc(q["h"], 1)

                def hidden_T(ab, q):
                    pe.transpose(bank[5][:, ab * P:(ab + 1) * P], hh[ab][:], ident[:]).then_inc(q["t"], 1)

                def rows_out(s, ab, q):
                    for f in range(2):
                        for n in range(2):
                            last = pe.matmul(bank[6 + ab][64 * n:64 * n + 64, :], hT[ab][:, 64 * f:64 * f + 64],
                                             w2s[s][:, f, n * 512:(n + 1) * 512], start=f == 0, stop=f == 1)
                    last.then_inc(q["y"], 1)

                q = dict(g=g_mm, ixm=ix_mm, h=h_mm, t=t_mm, y=y_mm)
                G = l * (PAIRS + 1)
                F = l * (PAIRS + 2)
                Q = l * (NE // 4 + 1)
                E = l * NE
                pe.wait_ge(sel_ok, Q + 1)
                pe.wait_ge(xlo_ok, NC * (l + 1))
                gather(0, q)
                pe.wait_ge(xg_a, F + 1)
                pe.wait_ge(xg_d, F + 1)
                gather(1, q)
                pe.wait_ge(cnt_ok, l + 1)
                numbers(0, q)
                with pe.Fori(0, NE // 8) as i:
                    for u_ in range(4):
                        p, buf = u_ % 2, u_ // 2
                        sl = [(2 * p + ab + 2) % 4 for ab in range(2)]
                        pe.wait_ge(xg_a, i * 4 + (F + u_ + 2))
                        pe.wait_ge(xg_d, i * 4 + (F + u_ + 2))
                        for ab in range(2):
                            pe.wait_ge(w13_in[sl[ab]], i * 64 + 32 * (8 * l + buf + 1))
                            pe.wait_ge(hh_ok, i * 8 + (E + 2 * u_ + ab + 1))
                            hidden(sl[ab], buf, 2 * p + ab, 3 + ab, q)
                        pe.wait_ge(hh_ok, i * 8 + (E + 2 * u_ + 3))
                        hidden_T(0, q)
                        pe.wait_ge(sel_ok, i * 2 + (Q + buf + 2))
                        gather(p, q)
                        if p == 1:
                            pe.wait_ge(ix_ok, i * 4 + (G + u_ + 1))
                            numbers(8 * i + (4 * buf + 4), q)
                        pe.wait_ge(hh_ok, i * 8 + (E + 2 * u_ + 4))
                        pe.wait_ge(ht_ok, i * 8 + (E + 2 * u_ + 1))
                        hidden_T(1, q)
                        for ab in range(2):
                            pe.wait_ge(ht_ok, i * 8 + (E + 2 * u_ + ab + 1))
                            pe.wait_ge(w2_in[sl[ab]], i * 32 + 16 * (8 * l + buf + 1))
                            pe.wait_ge(ys_ok, i * 8 + (E + 2 * u_ + ab + 1))
                            rows_out(sl[ab], ab, q)
                pe.wait_ge(ys_ok, NE * (l + 1) + 2)
                pe.wait_ge(xg_a, (l + 1) * (PAIRS + 2))
                pe.wait_ge(xg_d, (l + 1) * (PAIRS + 2))
                pe.wait_ge(ix_ok, (l + 1) * (PAIRS + 1))
                most = pe.value_load(cnt_i[0:1, l:l + 1], min_val=0, max_val=T)
                o = ov[l]
                with pe.If(most > CAP), pe.Fori(0, ROUNDS - 1) as r:
                    with pe.If(most > CAP * r + CAP):
                        with pe.Fori(0, NE) as e:
                            n = r * NE + e
                            pe.wait_ge(o["sel"], n + 1)
                            for half in range(2):
                                gather(half, o)
                                pe.wait_ge(o["xg"], n * 2 + (half + 1))
                            numbers(e, o)
                            pe.wait_ge(o["w"], n * 48 + 48)
                            hidden(3, 0, 0, 3, o)
                            pe.wait_ge(o["hh"], n + 1)
                            hidden_T(0, o)
                            pe.wait_ge(o["ht"], n + 1)
                            rows_out(3, 0, o)
            mixture(0)

            norm_transposes(2)
            pe.wait_ge(xt_a, NC * 3)
            pe.wait_ge(xt_d, NC * 3)
            with pe.Fori(0, KT // 2) as i:
                for s in range(2):
                    pe.wait_ge(w_lo, i * 2 + (16 + s + 1))
                    for half in range(2):
                        pe.wait_ge(cg_ok, i * 4 + (2 * s + half + 1))
                        for a in range(3):
                            for k in range(KT):
                                for j, (w, x) in enumerate(((wc_hi, xc_hi), (wc_hi, xc_lo), (wc_lo, xc_hi))):
                                    last = pe.matmul(bank[3 * half + a][:, 0:HALF], w[s][:, k, a, :],
                                                     x[:, k, half * HALF:(half + 1) * HALF],
                                                     start=k == 0 and j == 0, stop=k == KT - 1 and j == 2)
                        last.then_inc(c_mm, 1)
            pe.wait_ge(cg_ok, 2 * KT + 2)
            def z_c(part, k):
                return (g_hi, g_lo)[part][:, k, :]
            z_c.arrived = lambda c: pe.wait_ge(z_lo, 1 + c + 1)

            def w_c(part, k, s):
                if part == 1:
                    return woc_lo[s][:, k, :]
                return woc0_hi[k // 4][:, k % 4, :] if s == 0 else woc1_hi[:, k, :]
            project_out(1, z_c, w_c, 16 + KT + 1)
            mixture(1)

        @block.scalar
        def _(act):
            act.nop().then_inc(ys_ok, 2)

            def squares(n):
                for c in range(NC):
                    if n == 0:
                        act.wait_ge(x_in, 16 * NC)
                        act.wait_ge(const_ok, 1)
                    else:
                        act.wait_ge(h_ok, NC * (n - 1) + c + 1)
                    act.activation(junk[:], H[:, c, :], ACT.Square, accum_out=ssq[:, c:c + 1]).then_inc(sq_done, 1)
                    act.wait_ge(ms_ok, NC * n + c + 1)
                    act.activation(rms[:, c:c + 1], rms[:, c:c + 1], ACT.Sqrt).then_inc(rt_ok, 1)

            def xt_low(n):
                for c in range(NC):
                    act.wait_ge(xt_mm, NXT * n + 2 * c + 1)
                    act.activation(XT[:, 0:4, c * P:c * P + ROWS[c]],
                                   bank[6][:, :].rearrange("p (k t) -> p k t", k=4)[:, :, 0:ROWS[c]], ACT.Copy).then_inc(xt_a, 1)
            def group_hi(n):
                if n < 14:
                    act.wait_ge(wab_in[n % 3], 16 * (n // 3 + 1))
                    act.activation(wab_hi[n % 3][:], wab[n % 3][:], ACT.Copy).then_inc(w_hi, 1)

            def mixer_in_hi(n):
                for c in range(NC):
                    low = 6 - 2 * (c % 2)
                    for half in range(2):
                        act.wait_ge(xt_mm, NXT * n + 2 * c + half + 1)
                        last = act.activation(xc_hi[:, 4 * half:4 * half + 4, c * P:c * P + ROWS[c]],
                                              bank[low + half][:, :].rearrange("p (k t) -> p k t", k=4)[:, :, 0:ROWS[c]], ACT.Copy)
                    last.then_inc(xt_a, 1)
            squares(0)
            group_hi(0)
            mixer_in_hi(0)
            act.wait_ge(lbm_ok, 1)
            act.activation(lbe[:], lbe[:], ACT.Exp).then_inc(lbe_ok, 1)
            for n in range(6):
                dst, fn = ((fT, ACT.Sigmoid), (qdecT, ACT.Silu), (gateT, ACT.Silu))[n // 2]
                group_hi(n + 1)
                for b in range(4):
                    m, half = 2 * (n % 2) + b // 2, b % 2
                    act.wait_ge(z_mm, 4 * n + b + 1)
                    act.activation(dst[:, m, half * HALF:(half + 1) * HALF], bank[b][:, 0:HALF], fn).then_inc(z_free[b], 1)
            group_hi(7)
            act.wait_ge(f_ok, 5)
            act.activation(fT[:], fT[:], ACT.Ln).then_inc(ln_ok, 1)
            act.wait_ge(cum_ok, 4)
            act.activation(fT[:], koutT[:], ACT.Exp).then_inc(exp_ok, 1)
            act.activation(koutT[:], koutT[:], ACT.Exp, scale=-1.0).then_inc(exp_ok, 1)
            group_hi(8)
            for i in range(4 * NC):
                un = 34 + i
                n = ROWS[i % NC]
                if i % NC == 0:
                    group_hi(9 + i // NC)
                act.wait_ge(z_mm, un + 1)
                if i >= 2:
                    act.wait_ge(qms_ok, i - 1)
                act.activation(qsq[i % 2][0:n, :], bank[un % 4][0:n, 0:HG], ACT.Square).then_inc(qsq_ok, 1)
                act.wait_ge(qms_ok, i + 1)
                sl = slice((i % 2) * NH, (i % 2) * NH + NH // 2)
                act.activation(hms[0:n, sl], hms[0:n, sl], ACT.Sqrt).then_inc(qrt_ok, 1)
            for i in range(2 * NC):
                un, (hh_, c) = 54 + i, divmod(i, NC)
                if c == 0:
                    group_hi(13 + hh_)
                act.wait_ge(z_mm, un + 1)
                act.activation(va[0:ROWS[c], c, hh_ * HG:(hh_ + 1) * HG], bank[un % 4][0:ROWS[c], 0:HG], ACT.Copy).then_inc(z_free[un % 4], 1)
                act.wait_ge(z_free[un % 4], un // 4 + 1)
                act.nop().then_inc(v_ok, 1)
            for c in range(NC):
                n = ROWS[c]
                act.wait_ge(o_mm, c + 1)
                act.activation(osq[:, :, 0:n], bank[7][:, :].rearrange("p (m t) -> p m t", m=4)[:, :, 0:n], ACT.Square).then_inc(osq_ok, 1)
                act.wait_ge(stat_mm, c + 1)
                if c > 0:
                    act.wait_ge(zB_ok, c)
                act.activation(orms[:, :, 0:n], bank[0][:, :].rearrange("p (m t) -> p m t", m=4)[:, :, 0:n], ACT.Sqrt,
                               bias=epsc[:, 0:1]).then_inc(orms_ok, 1)
            act.wait_ge(kc_mm, 1)
            act.activation(kcT[:], bank[6][:, :].rearrange("p (m t) -> p m t", m=4), ACT.Copy).then_inc(kc_ok, 1)
            NU = NC * NH

            def prob_copy(i):
                if i % 2 == 0:
                    c = i // NH
                    act.wait_ge(pT_mm, i + 1)
                    if i >= 2:
                        act.wait_ge(pv_mm, i - 1)
                    if c < 4:
                        act.activation(prT[0][:, 0:c + 1, :], bank[2][:, 0:P * (c + 1)].rearrange("p (k t) -> p k t", t=P), ACT.Copy).then_inc(pT_a, 1)
                    else:
                        tie(act.activation(prT[0][:, 0, 0:DEC], bank[2][:, 0:DEC], ACT.Copy))
                        act.activation(prT[0][0:DEC, 1, 0:DEC], bank[2][0:DEC, P:P + DEC], ACT.Copy).then_inc(pT_a, 1)
            tie = Chain(act, ach)
            for i in range(NU + 2):
                if i < NU:
                    c, n = i // NH, ROWS[i // NH]
                    w = P * (c + 1) if c < 4 else PAST + DEC
                    act.wait_ge(s_ok, i + 1)
                    if i >= 2:
                        act.wait_ge(pT_mm, i - 1)
                    act.activation(pr[i % 2][0:n, 0:w], sneg[i % 2][0:n, 0:w], ACT.Exp, bias=nmaxs[0:n, i:i + 1], scale=-1.0,
                                   accum_out=rsum[0:n, i:i + 1]).then_inc(p_ok, 1)
                if 1 <= i <= NU:
                    prob_copy(i - 1)
                if i >= 11 and (i - 11) % NH == 0:
                    c = (i - 11) // NH
                    act.wait_ge(oaT_mm, c + 1)
                    act.activation(zA_hi[:, :, c * P:c * P + ROWS[c]], bank[6][:, :].rearrange("p (m t) -> p m t", m=4)[:, :, 0:ROWS[c]],
                                   ACT.Copy).then_inc(zAh_ok, 1)
                if i == 3:
                    act.activation(zB_hi[:], zB[:], ACT.Copy).then_inc(z_hi, 1)
            c = NC - 1
            act.wait_ge(oaT_mm, NC)
            act.activation(zA_hi[:, :, c * P:T], bank[6][:, :].rearrange("p (m t) -> p m t", m=4)[:, :, 0:DEC], ACT.Copy).then_inc(zAh_ok, 1)

            def mixture(l):
                squares(2 * l + 1)
                xt_low(2 * l + 1)
                act.wait_ge(lg_mm, l + 1)
                for c in range(NC):
                    act.activation(x_hi[:, c, :], XN[:, c, :], ACT.Copy).then_inc(xhi_ok, 1)
                act.wait_ge(ge_ok, l + 1)
                act.activation(rt[3][:, :, 0:NG], rt[3][:, :, 0:NG], ACT.Exp).then_inc(gx_ok, 1)
                act.wait_ge(e2_ok, l + 1)
                act.activation(c1[5][:], c1[5][:], ACT.Exp).then_inc(ex_ok, 1)
                E = l * NE

                def xg_low(half, buf):
                    return act.activation(xg[buf][:, 4 * half:4 * half + 2, :, :].rearrange("p k a s -> p (k a s)"), bank[0][:, :], ACT.Copy)
                F = l * (PAIRS + 2)
                for half in range(2):
                    act.wait_ge(g_mm, F + half + 1)
                    xg_low(half, 0).then_inc(xg_a, 1)
                with act.Fori(0, NE // 8) as i:
                    for u_ in range(4):
                        p, buf = u_ % 2, u_ // 2
                        for ab in range(2):
                            act.wait_ge(h_mm, i * 8 + (E + 2 * u_ + ab + 1))
                            act.activation(sg[ab][:], bank[3 + ab][:, 0:P], ACT.Silu).then_inc(sg_ok, 1)
                        act.wait_ge(g_mm, i * 4 + (F + u_ + 3))
                        xg_low(p, 1 - buf).then_inc(xg_a, 1)
                        for ab in range(2):
                            act.wait_ge(y_mm, i * 8 + (E + 2 * u_ + ab + 1))
                            act.wait_ge(ys_free, i * 8 + (E + 2 * u_ + ab + 1))
                            act.activation(ys[2 * p + ab][:], bank[6 + ab][:, :], ACT.Copy).then_inc(ys_ok, 1)
                act.wait_ge(cnt_ok, l + 1)
                most = act.value_load(cnt_i[0:1, l:l + 1], min_val=0, max_val=T)
                o = ov[l]
                with act.If(most > CAP), act.Fori(0, ROUNDS - 1) as r:
                    with act.If(most > CAP * r + CAP):
                        with act.Fori(0, NE) as e:
                            n = r * NE + e
                            act.wait_ge(o["mm"], n * 6 + 4)
                            act.activation(sg[0][:], bank[3][:, 0:P], ACT.Silu).then_inc(o["sg"], 1)
                            act.wait_ge(o["mm"], n * 6 + 6)
                            act.wait_ge(o["free"], n + 1)
                            act.activation(ys[0][:], bank[6][:, :], ACT.Copy).then_inc(o["ys"], 1)
            mixture(0)

            for s in range(2):
                act.wait_ge(wc_in[s], 48)
                act.activation(wc_hi[s][:], wc[s][:], ACT.Copy).then_inc(w_hi, 1)
            squares(2)
            mixer_in_hi(2)

            def conv_copies(m, half):
                act.wait_ge(c_mm, m * 2 + (half + 1))
                act.activation(hc[half][:], bank[3 * half + 2][:, 0:HALF], ACT.Copy).then_inc(hc_ok, 1)
            with act.Fori(0, KT // 2 - 1) as i:
                for s in range(2):
                    for half in range(2):
                        conv_copies(2 * i + s, half)
                    act.wait_ge(wc_in[s], i * 48 + 96)
                    act.activation(wc_hi[s][:], wc[s][:], ACT.Copy).then_inc(w_hi, 1)
            for s in range(2):
                for half in range(2):
                    conv_copies(KT - 2 + s, half)
            act.wait_ge(c_mm, 2 * KT)
            act.wait_ge(cg_ok, 2 * KT + 2)
            for c in range(NC):
                t = slice(c * P, c * P + ROWS[c])
                act.activation(g_hi[:, :, t], gT[:, :, t], ACT.Copy).then_inc(z_hi, 1)
            mixture(1)

        @block.vector
        def _(dve):
            tie = Chain(dve, dch)
            dve.nop().then_inc(hh_ok, 2)
            dve.nop().then_inc(cg_ok, 2)

            def norm(n, c):
                gain = gmix if n % 2 == 0 else gffn
                dve.wait_ge(sq_done, NC * n + c + 1)
                dve.tensor_scalar(rms[:, c:c + 1], ssq[:, c:c + 1], 1.0 / D, EPS, ALU.mult, ALU.add).then_inc(ms_ok, 1)
                dve.wait_ge(rt_ok, NC * n + c + 1)
                tie(dve.reciprocal(rstd[:, c:c + 1], rms[:, c:c + 1]))
                if c == 0:
                    dve.wait_ge(gmix_in if n % 2 == 0 else gffn_in, 16 * (n // 2 + 1))
                dve.scalar_tensor_tensor(XN[:, c, :], H[:, c, :], rstd[:, c:c + 1], gain[:], ALU.mult, ALU.mult).then_inc(xn_ok, 1)

            def xt_high(n):
                for c in range(NC):
                    dve.wait_ge(xt_mm, NXT * n + 2 * c + 2)
                    dve.tensor_copy(XT[:, 4:8, c * P:c * P + ROWS[c]],
                                    bank[7][:, :].rearrange("p (k t) -> p k t", k=4)[:, :, 0:ROWS[c]]).then_inc(xt_d, 1)

            def mixer_in_lo(n, lo):
                for c in range(NC):
                    low, t = 6 - 2 * (c % 2), slice(c * P, c * P + ROWS[c])
                    dve.wait_ge(xt_a, NC * n + c + 1)
                    for half in range(2):
                        last = dve.tensor_tensor(lo[:, 4 * half:4 * half + 4, t],
                                                 bank[low + half][:, :].rearrange("p (k t) -> p k t", k=4)[:, :, 0:ROWS[c]],
                                                 xc_hi[:, 4 * half:4 * half + 4, t].bitcast(F32), ALU.subtract)
                    last.then_inc(xt_d, 1)
            for c in range(NC):
                norm(0, c)
            mixer_in_lo(0, xp_lo)
            dve.wait_ge(tab_in, 16 * 5)
            tie(dve.tensor_tensor(lb[:], lbl[:, 0:4], lbl[:, 4:8], ALU.max))
            dve.tensor_tensor(lbe[:].rearrange("p (r m) -> p r m", r=2), lbl[:].rearrange("p (r m) -> p r m", r=2),
                              bc(lb[:].unsqueeze(1), [P, 2, 4]), ALU.subtract).then_inc(lbm_ok, 1)
            dve.wait_ge(lbe_ok, 1)
            tie(dve.tensor_tensor(lbs[:], lbe[:, 0:4], lbe[:, 4:8], ALU.add))
            tie(dve.reciprocal(lbs[:], lbs[:]))
            tie(dve.tensor_tensor(lb[:], lbe[:, 0:4], lbs[:], ALU.mult))
            tie(dve.tensor_scalar(lbs[:], lb[:], -1.0, 1.0, ALU.mult, ALU.add))
            tie(dve.tensor_scalar(qgain[:], qgain[:], HD ** -0.5, None, ALU.mult))
            dve.wait_ge(const_ok, 1)
            tie(dve.tensor_reduce(even[:], blk_sel[:], AX.X, ALU.add))
            tie(dve.tensor_scalar(odd[:], even[:], -1.0, 1.0, ALU.mult, ALU.add))
            for b in range(4):
                dve.wait_ge(z_free[b], 2)
            for m in range(4):
                dve.tensor_scalar(fT[:, m, :], fT[:, m, :], lbs[:, m:m + 1], lb[:, m:m + 1], ALU.mult, ALU.add).then_inc(f_ok, 1)
            dve.wait_ge(f_ok, 4)
            dve.tensor_scalar(kinT[:], fT[:], -1.0, 1.0, ALU.mult, ALU.add).then_inc(f_ok, 1)
            dve.wait_ge(ln_ok, 1)
            for m in range(4):
                dve.tensor_tensor_scan(koutT[:, m, :], reset[:], fT[:, m, :], 0.0, ALU.mult, ALU.add).then_inc(cum_ok, 1)
            dve.wait_ge(exp_ok, 2)
            dve.wait_ge(f_ok, 5)
            tie(dve.tensor_copy(dec[:].rearrange("p (m b) -> p m b", m=4), fT[:, :, BLK - 1::BLK]))
            dve.tensor_tensor(kinT[:], kinT[:], koutT[:], ALU.mult).then_inc(hg_ok, 1)
            for b in range(4):
                dve.wait_ge(z_free[b], 6)
            dve.tensor_tensor(qdecT[:], qdecT[:], fT[:], ALU.mult).then_inc(hg_ok, 1)
            dve.wait_ge(hg_ok, 2)
            dve.tensor_tensor(koutT[:].rearrange("p m (b t) -> p (m b) t", t=BLK), kinT[:].rearrange("p m (b t) -> p (m b) t", t=BLK),
                              bc(dec[:].unsqueeze(2), [P, 4 * NBLK, BLK]), ALU.mult).then_inc(hg_ok, 1)
            for m in range(4):
                tie(dve.tensor_scalar(gateT[:, m, :], gateT[:, m, :], onorm[:, m:m + 1], None, ALU.mult))
            for i in range(2 * NC):
                un, (hh_, c) = 24 + i, divmod(i, NC)
                dve.wait_ge(z_mm, un + 1)
                dve.tensor_copy(vb[0:ROWS[c], c, hh_ * HG:(hh_ + 1) * HG], bank[un % 4][0:ROWS[c], 0:HG]).then_inc(z_free[un % 4], 1)
            for i in range(4 * NC):
                un, c, n = 34 + i, i % NC, ROWS[i % NC]
                dst, gain = (q_tok, qgain) if i < 2 * NC else (k_tok, kgain)
                sl = slice((i % 2) * NH, (i % 2) * NH + NH // 2)
                four = [n, NH // 2, HD]
                lo = (i // NC % 2) * HG
                d = dst[0:n, c, lo:lo + HG].rearrange("p (h d) -> p h d", d=HD)
                dve.wait_ge(qsq_ok, i + 1)
                tie(dve.tensor_reduce(hss[0:n, sl], qsq[i % 2][0:n, :].rearrange("p (h d) -> p h d", d=HD), AX.X, ALU.add))
                dve.tensor_scalar(hms[0:n, sl], hss[0:n, sl], 1.0 / HD, EPS, ALU.mult, ALU.add).then_inc(qms_ok, 1)
                dve.wait_ge(qrt_ok, i + 1)
                tie(dve.reciprocal(hrs[0:n, sl], hms[0:n, sl]))
                dve.tensor_tensor(d, bank[un % 4][0:n, 0:HG].rearrange("p (h d) -> p h d", d=HD),
                                  bc(hrs[0:n, sl].unsqueeze(2), four), ALU.mult).then_inc(z_free[un % 4], 1)
                dve.wait_ge(z_free[un % 4], un // 4 + 1)
                dve.tensor_tensor(d, d, bc(gain[0:n, :].unsqueeze(1), four), ALU.mult).then_inc(qk_ok, 1)
            for i in range(2 * NC):
                c, dst = i // 2, (qT, kT)[i % 2]
                dve.wait_ge(qkT_mm, i + 1)
                dve.tensor_copy(dst[:, :, c * P:c * P + ROWS[c]],
                                bank[4 + i % 2][:, :].rearrange("p (m t) -> p m t", m=4)[:, :, 0:ROWS[c]]).then_inc(qkT_ok, 1)
            dve.memset(st[0][:, 0, :, :], 0.0).then_inc(st0_ok, 1)
            dve.wait_ge(st0_ok, 1)
            def hgrn_chain(c):
                n = ROWS[c]
                dve.wait_ge(ko_mm, c + 1)
                if c >= 2:
                    dve.wait_ge(u_mm, c - 1)
                dve.tensor_copy(kout[c % 2][0:n, :], bank[0][0:n, :]).then_inc(ko_ok, 1)
                v = vb[0:n, c, :].rearrange("p (h d) -> p h d", h=NH)
                if c == 0:
                    for b in range(4):
                        dve.wait_ge(z_free[b], 16)
                dve.tensor_scalar(vx[c % 2][0:n, :, 0, :], v, even[0:n, :], None, ALU.mult)
                tie(dve.tensor_scalar(vx[c % 2][0:n, :, 1, :], v, odd[0:n, :], None, ALU.mult))
                dve.nop().then_inc(vx_ok, 1)
                dve.wait_ge(a_mm, c + 1)
                if c >= 2:
                    dve.wait_ge(o_mm, c - 1)
                for par in range(2):
                    dve.tensor_tensor(am[c % 2][0:n, par, :, 0:n], bank[1 + par][0:n, :].rearrange("p (m t) -> p m t", m=4)[:, :, 0:n],
                                      bc(blk_mask[0:n, 0:n].unsqueeze(1), [n, 4, n]), ALU.mult).then_inc(a_ok, 1)
                dve.wait_ge(u_mm, c + 1)
                if c == 4:
                    dve.wait_ge(st_in, 16)
                for b in range(n // BLK):
                    t = dec[:].rearrange("p (m b) -> p m b", m=4)[:, :, 8 * c + b:8 * c + b + 1]
                    upd = bank[3 + b // 2][:, :].rearrange("p (m i v) -> p m i v", m=4, i=2)[:, :, b % 2, :]
                    tie(dve.tensor_tensor(dS[:], st[c % 2][:, b, :, :], bc(t, [P, 4, HD]), ALU.mult))
                    tie(dve.tensor_tensor(st[c % 2][:, b + 1, :, :], upd, dS[:], ALU.add))
                if c < 3:
                    if c >= 1:
                        dve.wait_ge(o_mm, c)
                    dve.tensor_copy(st[(c + 1) % 2][:, 0, :, :], st[c % 2][:, 8, :, :]).then_inc(st0_ok, 1)
                    dve.wait_ge(st0_ok, c + 2)
                dve.nop().then_inc(st_ok, 1)

            def hgrn_norm(c):
                n = ROWS[c]
                dve.wait_ge(orms_ok, c + 1)
                tie(dve.reciprocal(orms[:, :, 0:n], orms[:, :, 0:n]))
                z = zB[:, :, c * P:c * P + n]
                tie(dve.tensor_tensor(z, bank[7][:, :].rearrange("p (m t) -> p m t", m=4)[:, :, 0:n], orms[:, :, 0:n], ALU.mult))
                dve.tensor_tensor(z, z, gateT[:, :, c * P:c * P + n], ALU.mult).then_inc(zB_ok, 1)
            hgrn_chain(0)
            for c in range(NC):
                if c + 1 < NC:
                    hgrn_chain(c + 1)
                hgrn_norm(c)

            dve.wait_ge(bias_in, 16 * 4)
            tie(dve.memset(bias[0:CH, :, 512 - CH:512], MASKED))
            NU = NC * NH

            def score_max(i):
                c, h = divmod(i, NH)
                n = ROWS[c]
                w, b0 = (P * (c + 1), 384 - P * c) if c < 4 else (PAST + DEC, 256)
                dve.wait_ge(s_mm, i + 1)
                if i >= 2:
                    dve.wait_ge(p_ok, i - 1)
                dve.tensor_tensor_reduce(out=sneg[i % 2][0:n, 0:w], in0=bank[i % 2][0:n, 0:w], in1=bias[0:n, h, b0:b0 + w],
                                         scale=-1.0, scalar=-MASKED, op0=ALU.add, op1=ALU.min,
                                         accum_out=nmaxs[0:n, i:i + 1]).then_inc(s_ok, 1)

            def prob_copy(i):
                if i % 2 == 1:
                    c = i // NH
                    dve.wait_ge(pT_mm, i + 1)
                    if i >= 3:
                        dve.wait_ge(pv_mm, i - 1)
                    if c < 4:
                        dve.tensor_copy(prT[1][:, 0:c + 1, :], bank[3][:, 0:P * (c + 1)].rearrange("p (k t) -> p k t", t=P)).then_inc(pT_d, 1)
                    else:
                        tie(dve.tensor_copy(prT[1][:, 0, 0:DEC], bank[3][:, 0:DEC]))
                        dve.tensor_copy(prT[1][0:DEC, 1, 0:DEC], bank[3][0:DEC, P:P + DEC]).then_inc(pT_d, 1)

            def head_scale(c):
                n = ROWS[c]
                sl = slice((c % 2) * NH, (c % 2 + 1) * NH)
                dve.wait_ge(pv_mm, NH * (c + 1))
                tie(dve.reciprocal(rinv[0:n, sl], rsum[0:n, c * NH:(c + 1) * NH]))
                if c >= 2:
                    dve.wait_ge(oaT_mm, c - 1)
                dve.tensor_tensor(oa[c % 2][0:n, :].rearrange("p (h d) -> p h d", h=NH), bank[4 + c % 2][0:n, :].rearrange("p (h d) -> p h d", h=NH),
                                  bc(rinv[0:n, sl].unsqueeze(2), [n, NH, HD]), ALU.mult).then_inc(oa_ok, 1)
            def heads_lo(c):
                n = ROWS[c]
                dve.wait_ge(zAh_ok, c + 1)
                dve.tensor_tensor(zA_lo[:, :, c * P:c * P + n], bank[6][:, :].rearrange("p (m t) -> p m t", m=4)[:, :, 0:n],
                                  zA_hi[:, :, c * P:c * P + n].bitcast(F32), ALU.subtract).then_inc(zA_ok, 1)
            for i in range(NU + 3):
                if i < NU:
                    score_max(i)
                if 1 <= i <= NU:
                    prob_copy(i - 1)
                if i >= 10 and (i - 10) % NH == 0:
                    head_scale((i - 10) // NH)
                if i == 6:
                    dve.wait_ge(z_hi, 1)
                    dve.tensor_tensor(zB_lo[:], zB[:], zB_hi[:].bitcast(F32), ALU.subtract).then_inc(z_lo, 1)
                if i >= 13 and (i - 13) % NH == 0:
                    heads_lo((i - 13) // NH)
            heads_lo(NC - 1)

            def residual(n):
                for i in range(2 * NC):
                    s, c = divmod(i, NC)
                    dve.wait_ge(op_mm, 2 * NC * n + i + 1)
                    h = H[0:ROWS[c], c, s * 512:(s + 1) * 512]
                    dve.tensor_tensor(h, bank[i % 4][0:ROWS[c], :], h, ALU.add).then_inc(op_add, 1)
                    if s == 1:
                        dve.wait_ge(op_add, 2 * NC * n + i + 1)
                        dve.nop().then_inc(h_ok, 1)
                        if c > 0:
                            norm(2 * n + 1, c - 1)
                norm(2 * n + 1, NC - 1)
            residual(0)

            def route(l):
                lgg, lge = lg[:, :, 0:NG], lg[:, :, NG:NR].rearrange("p c (g j) -> p c g j", g=NG)
                tie(dve.memset(lg[:], 0.0))
                tie(dve.memset(rk[:, :, NE:RKW], -1.0))
                tie(dve.tensor_scalar(dv[:, :, NE:RKW], rk[:, :, NE:RKW], 1.0, None, ALU.add))
                dve.wait_ge(lg_mm, l + 1)
                dve.wait_ge(wr_in, 64 * (l + 1))
                z = bank[0][:, 0:NC * NR].rearrange("p (c n) -> p c n", c=NC)
                tie(dve.tensor_tensor(lg[:, 0:4, :], z[:, 0:4, :], bc(biasr[:].unsqueeze(1), [P, 4, NR]), ALU.add))
                dve.tensor_tensor(lg[0:DEC, 4, :], z[0:DEC, 4, :], biasr[0:DEC, :], ALU.add).then_inc(lg_ok, 1)
                dve.wait_ge(lg_ok, l + 1)

                def first_max(v, w, rev, eq, key, hot, top):
                    tie(dve.tensor_reduce(top, v, AX.X, ALU.max))
                    tie(dve.tensor_tensor(eq, v, bc(top.unsqueeze(2), [P, NC, w]), ALU.is_equal))
                    tie(dve.tensor_tensor(key, eq, bc(rev.unsqueeze(1), [P, NC, w]), ALU.mult))
                    tie(dve.tensor_reduce(c1[1][:], key, AX.X, ALU.max))
                    tie(dve.tensor_tensor(hot, key, bc(c1[1][:].unsqueeze(2), [P, NC, w]), ALU.is_equal))
                hot_g, hot1, hot2 = rt[2][:, :, 0:4], rt[2][:, :, 4:12], rt[2][:, :, 12:20]
                first_max(lgg, NG, rev4[:], rt[0][:, :, 0:4], rt[1][:, :, 0:4], hot_g, c1[0][:])
                dve.tensor_tensor(rt[3][:, :, 0:NG], lgg, bc(c1[0][:].unsqueeze(2), [P, NC, NG]), ALU.subtract).then_inc(ge_ok, 1)
                four = [P, NC, NG, EPG]
                r4 = [t[:].rearrange("p c (g j) -> p c g j", g=NG) for t in rt]
                tie(dve.tensor_tensor(r4[0], lge, bc(hot_g.unsqueeze(3), four), ALU.mult))
                sel8 = rt[1][:, :, 8:16]
                tie(dve.tensor_reduce(sel8, rt[0][:].rearrange("p c (g j) -> p c j g", g=NG), AX.X, ALU.add))
                first_max(sel8, EPG, rev8[:], rt[1][:, :, 16:24], rt[1][:, :, 24:32], hot1, c1[3][:])
                sel7 = rt[4][:, :, 0:8]
                tie(dve.scalar_tensor_tensor(sel7, hot1, -3e38, sel8, ALU.mult, ALU.add))
                first_max(sel7, EPG, rev8[:], rt[1][:, :, 16:24], rt[1][:, :, 24:32], hot2, c1[4][:])
                dve.tensor_tensor(c1[5][:], c1[4][:], c1[3][:], ALU.subtract).then_inc(e2_ok, 1)
                tie(dve.tensor_tensor(hot_g, hot_g, bc(frame_ok[:].unsqueeze(2), [P, NC, NG]), ALU.mult))
                for hot, m in ((hot1, m1), (hot2, m2)):
                    tie(dve.tensor_tensor(m[:].rearrange("p c (g j) -> p c g j", g=NG), bc(hot_g.unsqueeze(3), four),
                                          bc(hot.unsqueeze(2), four), ALU.mult))
                dve.tensor_tensor(rt[0][:], m1[:], m2[:], ALU.add).then_inc(msk_ok, 1)
                dve.wait_ge(gx_ok, l + 1)
                tie(dve.tensor_reduce(c1[2][:], rt[3][:, :, 0:NG], AX.X, ALU.add))
                tie(dve.reciprocal(c1[2][:], c1[2][:]))
                dve.wait_ge(ex_ok, l + 1)
                tie(dve.tensor_scalar(c1[6][:], c1[5][:], 1.0, None, ALU.add))
                tie(dve.reciprocal(c1[6][:], c1[6][:]))
                tie(dve.tensor_tensor(c1[2][:], c1[2][:], c1[6][:], ALU.mult))
                tie(dve.tensor_copy(gate[0][:], c1[2][:]))
                tie(dve.tensor_tensor(gate[1][:], c1[2][:], c1[5][:], ALU.mult))
                tie(dve.tensor_scalar(c1[3][:], frame_no[:], -float(DROP), None, ALU.add))
                tie(dve.tensor_scalar(c1[4][:], frame_no[:], float(T - DROP), None, ALU.add))
                tie(dve.tensor_tensor(rt[1][:], m1[:], bc(c1[3][:].unsqueeze(2), [P, NC, NE]), ALU.mult))
                tie(dve.tensor_tensor(rt[4][:], m2[:], bc(c1[4][:].unsqueeze(2), [P, NC, NE]), ALU.mult))
                tie(dve.tensor_tensor(dv[:, :, 0:NE], rt[1][:], rt[4][:], ALU.add))
                dve.wait_ge(rk_mm, l + 1)
                dve.wait_ge(msk_ok, l + 1)
                tie(dve.scalar_tensor_tensor(rt[3][:], bank[1][:, 0:NC * NE].rearrange("p (c n) -> p c n", c=NC), 1.0, rt[0][:], ALU.add, ALU.mult))
                tie(dve.tensor_reduce(c1[7][:, 0:1], rt[3][:], AX.XY, ALU.max))
                dve.tensor_scalar(rk[:, :, 0:NE], rt[3][:], -1.0, None, ALU.add).then_inc(rk_ok, 1)
                dve.wait_ge(rk_ok, l + 1)
                dve.wait_ge(cm_mm, l + 1)
                tie(dve.tensor_reduce(cnt[0:1, 0:1], bank[2][0:1, 0:P], AX.X, ALU.max))
                dve.tensor_copy(cnt_i[0:1, l:l + 1], cnt[0:1, 0:1]).then_inc(cnt_ok, 1)

            def select(e):
                full = [P, NC, 4, CAP]
                return dve.tensor_tensor(seln[:], bc(rk[:, :, bass.ds(e, 4)].unsqueeze(3), full),
                                         bc(slot_no[:].unsqueeze(1).unsqueeze(1), full), ALU.is_equal)

            def xg_high(half, buf, b=1):
                return dve.tensor_copy(xg[buf][:, 4 * half + 2 * b:4 * half + 2 * b + 2, :, :].rearrange("p k a s -> p (k a s)"), bank[b][:, :])

            def row_numbers(p, ab):
                out = None
                for dh in range(2):
                    out = dve.tensor_scalar(idx[2 * p + ab][64 * dh:64 * dh + 64, :], bank[2][64 * ab:64 * ab + 64, 2 * p + ab:2 * p + ab + 1],
                                            2.0, 2.0 * DROP + dh, ALU.mult, ALU.add)
                return out

            def mixture(l):
                xt_high(2 * l + 1)
                route(l)
                E = l * NE
                F = l * (PAIRS + 2)
                Q = l * (NE // 4 + 1)
                select(0).then_inc(sel_ok, 1)
                for half in range(2):
                    dve.wait_ge(g_mm, F + half + 1)
                    xg_high(half, 0).then_inc(xg_d, 1)
                dve.wait_ge(ix_mm, Q + 1)
                row_numbers(0, 0)
                row_numbers(0, 1).then_inc(ix_ok, 1)
                with dve.Fori(0, NE // 8) as i:
                    for u_ in range(4):
                        p, buf = u_ % 2, u_ // 2
                        if p == 0:
                            select(8 * i + (4 * buf + 4)).then_inc(sel_ok, 1)
                        for ab in range(2):
                            dve.wait_ge(sg_ok, i * 8 + (E + 2 * u_ + ab + 1))
                            dve.tensor_tensor(hh[ab][:], bank[3 + ab][:, P:2 * P], sg[ab][:], ALU.mult).then_inc(hh_ok, 1)
                        dve.wait_ge(t_mm, i * 8 + (E + 2 * u_ + 1))
                        dve.tensor_copy(hT[0][:], bank[5][:, 0:P]).then_inc(ht_ok, 1)
                        dve.wait_ge(g_mm, i * 4 + (F + u_ + 3))
                        xg_high(p, 1 - buf).then_inc(xg_d, 1)
                        dve.wait_ge(t_mm, i * 8 + (E + 2 * u_ + 2))
                        dve.tensor_copy(hT[1][:], bank[5][:, P:2 * P]).then_inc(ht_ok, 1)
                        dve.wait_ge(ix_mm, i * 2 + (Q + (u_ + 1) // 2 + 1))
                        dve.wait_ge(ys_free, i * 8 + (E + 2 * u_ + 4))
                        row_numbers(1 - p, 0)
                        row_numbers(1 - p, 1).then_inc(ix_ok, 1)
                dve.wait_ge(cnt_ok, l + 1)
                most = dve.value_load(cnt_i[0:1, l:l + 1], min_val=0, max_val=T)
                dve.wait_ge(ys_free, NE * (l + 1) + 4)
                o = ov[l]
                with dve.If(most > CAP), dve.Fori(0, ROUNDS - 1) as r:
                    with dve.If(most > CAP * r + CAP):
                        dve.tensor_scalar(rk[:], rk[:], -float(CAP), None, ALU.add).then_inc(o["rk"], 1)
                        with dve.Fori(0, NE) as e:
                            n = r * NE + e
                            dve.wait_ge(o["rk"], r + 1)
                            dve.wait_ge(o["free"], n + 1)
                            select(e).then_inc(o["sel"], 1)
                            for half in range(2):
                                dve.wait_ge(o["mm"], n * 6 + (half + 1))
                                xg_high(half, 0, 0)
                                xg_high(half, 0).then_inc(o["xg"], 1)
                            dve.wait_ge(o["mm"], n * 6 + 3)
                            row_numbers(0, 0).then_inc(o["ix"], 1)
                            dve.wait_ge(o["sg"], n + 1)
                            dve.tensor_tensor(hh[0][:], bank[3][:, P:2 * P], sg[0][:], ALU.mult).then_inc(o["hh"], 1)
                            dve.wait_ge(o["mm"], n * 6 + 5)
                            dve.tensor_copy(hT[0][:], bank[5][:, 0:P]).then_inc(o["ht"], 1)
                for c in range(NC):
                    n = ROWS[c]
                    dve.wait_ge(yab_in[c], 32 * (l + 1))
                    h = H[0:n, c, :]
                    for i in range(2):
                        tie(dve.scalar_tensor_tensor(h, yab[c][0:n, i, :], gate[i][0:n, c:c + 1], h, ALU.mult, ALU.add))
                    dve.nop().then_inc(h_ok, 1)
                    if l == 0 and c > 0:
                        norm(2, c - 1)
                if l == 0:
                    norm(2, NC - 1)
            mixture(0)

            mixer_in_lo(2, xc_lo)
            dve.wait_ge(st_in, 48)
            tie(dve.memset(u[:, 0:2], 0.0))
            S0 = 2 + SEQ
            parts = [[(0, HALF, 0)], [(0, SEQ - HALF, HALF), (SEQ - HALF, HALF, SEQ)]]
            with dve.Fori(0, KT) as m:
                tie.loop(m, CONV_STEPS, KT)
                mm = bass.ds(m, 1)
                tie(dve.tensor_copy(u[:, S0:S0 + 2], hist[:, mm, :].rearrange("p k r -> p (k r)")))
                for half in range(2):
                    dve.wait_ge(hc_ok, m * 2 + (half + 1))
                    for a, b, t0 in parts[half]:
                        col = t0 + 2 + (2 if t0 == SEQ else 0)
                        tie(dve.tensor_tensor(u[:, col:col + b - a], bank[3 * half + 1][:, a:b], hc[half][:, a:b], ALU.mult))
                    for a, b, t0 in parts[half]:
                        col, w = t0 + (2 if t0 == SEQ else 0), b - a
                        c0 = cv[:, t0:t0 + w]
                        tie(dve.tensor_scalar(c0, u[:, col:col + w], convw[:, bass.ds(m, 1)], None, ALU.mult))
                        tie(dve.scalar_tensor_tensor(c0, u[:, col + 1:col + 1 + w], convw[:, bass.ds(m + KT, 1)], c0, ALU.mult, ALU.add))
                        tie(dve.scalar_tensor_tensor(c0, u[:, col + 2:col + 2 + w], convw[:, bass.ds(m + 2 * KT, 1)], c0, ALU.mult, ALU.add))
                    tie(dve.tensor_tensor(gT[:, mm, half * HALF:(half + 1) * HALF].rearrange("p k t -> p (k t)"), bank[3 * half][:, 0:HALF],
                                          cv[:, half * HALF:(half + 1) * HALF], ALU.mult))
                    dve.nop().then_inc(cg_ok, 1)
                tie(dve.tensor_copy(tails[:, 0, mm, :].rearrange("p k r -> p (k r)"), u[:, SEQ:SEQ + 2]))
                tie(dve.tensor_copy(tails[:, 1, mm, :].rearrange("p k r -> p (k r)"), u[:, UW - 2:UW]))
                dve.nop().then_inc(tail_ok, 1)
            tie.end()
            for c in range(NC):
                t = slice(c * P, c * P + ROWS[c])
                dve.wait_ge(z_hi, 1 + c + 1)
                dve.tensor_tensor(g_lo[:, :, t], gT[:, :, t], g_hi[:, :, t].bitcast(F32), ALU.subtract).then_inc(z_lo, 1)
            residual(1)
            mixture(1)


CONV_STEPS = 1 + 3 + 3 * 3 + 2 + 2

_INS = ['x_prompt', 'x_sample', 'cache_a_k', 'cache_a_v', 'state_hgrn', 'state_conv', 'norm_mix', 'norm_ffn', 'w_in_ab',
        'w_out_ab', 'q_norm', 'k_norm', 'rel_bias', 'hgrn_lb_logits', 'hgrn_out_norm', 'w_in_c', 'conv_w', 'w_out_c',
        'w_group', 'b_group', 'w_expert', 'b_expert', 'w1', 'w3', 'w2']
_OUTS = [(1, SEQ, D), (1, DEC, D), (1, 1, SEQ, NH, HD), (1, 1, SEQ, NH, HD), (1, 1, PAST, NH, HD), (1, 1, PAST, NH, HD),
         (1, 1, NH, HD, HD), (1, 1, NH, HD, HD), (1, 1, 2, D), (1, 1, 2, D)]


def kernel(**inputs):
    import numpy as _np
    import concourse.bacc as _bacc
    from concourse import mybir as _mybir
    from concourse.bass_utils import run_bass_kernel_spmd as _run

    nc = _bacc.Bacc("TRN2", target_bir_lowering=False, num_devices=1)
    arrays, args = {}, []
    for name in _INS:
        a = _np.ascontiguousarray(inputs[name])
        arrays[f"in_{name}_dram"] = a
        args.append(nc.dram_tensor(f"in_{name}_dram", a.shape, _mybir.dt.from_np(a.dtype), kind="ExternalInput").ap())
    for i, shape in enumerate(_OUTS):
        args.append(nc.dram_tensor(f"out_{i}_dram", shape, _mybir.dt.float32, kind="ExternalOutput").ap())
    hmoe_step(nc, *args)
    r = _run(nc, [arrays], core_ids=[0])
    return tuple(r.results[0][f"out_{i}_dram"] for i in range(len(_OUTS)))
```

```python
from contextlib import ExitStack

import numpy as np
import concourse.bass as bass
from concourse import mybir

F32 = mybir.dt.float32
F32R = mybir.dt.float32r
BF16 = mybir.dt.bfloat16
I32 = mybir.dt.int32
U32 = mybir.dt.uint32
ALU = mybir.AluOpType
ACT = mybir.ActivationFunctionType
AX = mybir.AxisListType

P = 128
D = 1024
KT = D // P
SEQ, DEC, PAST = 512, 32, 128
T = SEQ + DEC
NC = 5
ROWS = [128, 128, 128, 128, 32]
HALF = T // 2
NH, HD = 8, 64
DA = NH * HD
CH = 64
REL = 128
BLK = 16
NBLK = T // BLK
EPS = 1e-6
NG, EPG = 4, 8
NE = NG * EPG
DE = 256
CAP = 64
ROUNDS = -(-T // CAP)
NR = NG + NE
RKW = NE + 4
GROUPS = [3, 5, 6, 4, 0, 1, 2]
HG = DA // 2
UNIT_END = [4, 8, 12, 16, 20, 24, 29, 34, 39, 44, 49, 54, 59, 64]
MASKED = -1e30
DROP = 1100


def hmoe_step(nc, x_prompt, x_sample, cache_a_k, cache_a_v, state_hgrn, state_conv, norm_mix, norm_ffn,
              w_in_ab, w_out_ab, q_norm, k_norm, rel_bias, hgrn_lb_logits, hgrn_out_norm, w_in_c, conv_w,
              w_out_c, w_group, b_group, w_expert, b_expert, w1, w3, w2,
              y_prompt, y_sample, nk_p, nv_p, nk_s, nv_s, nh_p, nh_s, nconv_p, nconv_s):
    ctx = ExitStack()
    KB = 1024
    BASE = 16512

    def at(name, kb, shape, dt=F32):
        return nc.alloc_sbuf_tensor_at(name, shape, dt, offset=BASE + int(kb * KB))

    def sem(name):
        return ctx.enter_context(nc.semaphore(name))

    with ctx:
        H = at("H", 0, [P, NC, D])
        ident = at("ident", 20, [P, P])
        upper = at("upper", 20.5, [P, P])
        ones = at("ones", 21, [P, P])
        blk_mask = at("blk_mask", 22, [P, P])
        slot_no = at("slot_no", 22.5, [P, CAP])
        junk = at("junk", 22.75, [P, D], BF16)
        sm = 24.75
        def small(name, n, dt=F32):
            nonlocal sm
            t = at(name, sm, [P, n], dt)
            sm += -(-n * 4 // 32) * 32 / KB
            return t
        blk_sel = small("blk_sel", 4)
        even = small("even", 1)
        odd = small("odd", 1)
        frame_no = small("frame_no", NC)
        frame_ok = small("frame_ok", NC)
        rev4 = small("rev4", NG)
        rev8 = small("rev8", EPG)
        half_no = small("half_no", 1)
        epsc = small("epsc", 1)
        ssq = small("ssq", NC)
        rms = small("rms", NC)
        rstd = small("rstd", NC)
        lbl = small("lbl", 8)
        lbe = small("lbe", 8)
        lb = small("lb", 4)
        lbs = small("lbs", 4)
        onorm = small("onorm", 4)
        convw = small("convw", 3 * KT)
        qgain = small("qgain", HD)
        kgain = small("kgain", HD)
        hss = small("hss", 2 * NH)
        hms = small("hms", 2 * NH)
        hrs = small("hrs", 2 * NH)
        rsum = small("rsum", NC * NH)
        rinv = small("rinv", 2 * NH)
        nmaxs = small("nmaxs", NC * NH)
        dec = small("dec", 4 * NBLK)
        biasr = small("biasr", NR)
        cnt = small("cnt", 4)
        cnt_i = small("cnt_i", 2, I32)
        assert sm <= 28, sm
        gmix = at("gmix", 28, [P, D])
        gffn = at("gffn", 32, [P, D])
        RING = 36
        w13 = [at(f"w13_{s}", RING + 24 * s, [P, KT, 2, DE]) for s in range(4)]
        w2s = [at(f"w2_{s}", RING + 24 * s + 16, [P, 2, D]) for s in range(4)]
        XN = at("XN", 132, [P, NC, D])
        XT = at("XT", 152, [P, KT, T])
        MISC = 169
        wab = [at(f"wab{s}", RING + 16 * s, [P, KT, HG]) for s in range(3)]
        wab_lo = [at(f"wab_lo{s}", RING + 16 * s, [P, KT, HG], F32R) for s in range(3)]
        wab_hi = [at(f"wab_hi{s}", RING + 16 * s + 8, [P, KT, HG], F32R) for s in range(3)]
        xc_hi = at("xc_hi", 152, [P, KT, T], F32R)
        xp_lo = at("xp_lo", MISC + 20, [P, KT, T], F32R)
        HI = RING + 48
        q_tok = at("q_tok", HI, [P, NC, DA])
        k_tok = at("k_tok", HI + 10, [P, NC, DA])
        kinT = at("kinT", HI + 20, [P, 4, T])
        koutT = at("koutT", HI + 28.5, [P, 4, T])
        qdecT = at("qdecT", HI + 37, [P, 4, T])
        fT = at("fT", 132, [P, 4, T])
        gateT = at("gateT", 140.5, [P, 4, T])
        kcT = at("kcT", 149, [P, 4, P])
        va = at("va", MISC, [P, NC, DA])
        vb = at("vb", MISC + 10, [P, NC, DA])
        qTs = [at("qT_even", MISC + 20, [P, 4, T]), at("qT_odd", 140.5, [P, 4, T])]
        kT = at("kT", MISC + 28.5, [P, 4, T])
        bias = at("bias", 152, [P, NH, 512])
        zB = at("zB", 132, [P, 4, T])
        reset = at("reset", HI + 45.5, [P, T])
        st = [at(f"st{i}", RING + 9 * i, [P, 9, 4, HD]) for i in range(2)]
        kout = at("kout", MISC + 20, [P, 4, DA])
        qdecs = [qdecT, at("qdec_odd", MISC + 28.5, [P, 4, T])]
        vx = [at(f"vx{i}", RING + 22 + 4 * i, [P, NH, 2, HD]) for i in range(2)]
        am = [at(f"am{i}", RING + 30 + 4 * i, [P, 2, 4, P]) for i in range(2)]
        ot = at("ot", RING + 38, [P, DA])
        osq = at("osq", RING + 40, [P, DA])
        dS = at("dS", RING + 42, [P, 4, HD])
        sneg = [at(f"sneg{i}", HI + 2 * i, [P, 512]) for i in range(2)]
        pr = [at(f"pr{i}", HI + 4 + 2 * i, [P, 512]) for i in range(2)]
        prT = [at(f"prT{i}", HI + 8 + 2 * i, [P, 4, P]) for i in range(2)]
        dg = at("dg", HI + 12, [P, 2, 4, P])
        rb = at("rb", 132, [P, 4, P])
        zA = at("zA", 134, [P, 4, P])
        kc = at("kc", HI + 16, [P, DA])
        vc = at("vc", HI + 18, [P, DA])
        qsq = [at(f"qsq{i}", 149 + i, [P, HG]) for i in range(2)]
        wo = [at(f"wo{s}", RING + 32 * s, [P, KT, 512]) for s in range(2)]
        wo_lo = [at(f"wo_lo{s}", RING + 32 * s, [P, KT, 512], F32R) for s in range(2)]
        wo_hi = [at("wo_hi0", RING + 16, [P, KT, 512], F32R), at("wo_hi1", MISC + 20, [P, KT, 512], F32R)]
        zA_hi = at("zA_hi", HI + 20, [P, 4, T], F32R)
        zB_hi = at("zB_hi", HI + 28.5, [P, 4, T], F32R)
        zB_lo = at("zB_lo", HI + 37, [P, 4, T], F32R)
        zA_lo = at("zA_lo", MISC + 10, [P, 4, T], F32R)
        wr = at("wr", MISC + 36.5, [P, KT, NR])
        lg = at("lg", MISC + 29.5, [P, NC, NR])
        rt = [at(f"rt{i}", MISC + (30.25, 31, 3.5, 4.25, 5)[i], [P, NC, NE]) for i in range(5)]
        m1 = at("m1", MISC + 5.75, [P, NC, NE])
        m2 = at("m2", MISC + 6.5, [P, NC, NE])
        rk = at("rk", MISC + 7.25, [P, NC, RKW])
        dv = at("dv", MISC + 8, [P, NC, RKW], F32R)
        c1 = [at(f"c{i}", MISC + 8.75 + i * 0.03125, [P, NC]) for i in range(8)]
        gate = [at(f"gate{i}", MISC + 9 + i * 0.03125, [P, NC]) for i in range(2)]
        seln = at("seln", MISC + 9.25, [P, NC, 4, CAP], F32R)
        x_hi = at("x_hi", 152, [P, NC, D], F32R)
        x_lo = at("x_lo", 132, [P, NC, D], F32R)
        xg = [at("xg0", MISC + 14.25, [P, KT, 4, CAP]), at("xg1", 28, [P, KT, 4, CAP])]
        sg = [at(f"sg{i}", MISC + 22.25 + 0.5 * i, [P, P]) for i in range(2)]
        hh = [at(f"hh{i}", MISC + 23.25 + 0.5 * i, [P, P]) for i in range(2)]
        hT = [at(f"hT{i}", MISC + 24.25 + 0.5 * i, [P, P]) for i in range(2)]
        ys = [at(f"ys{i}", MISC + (25.25, 27.25, 32, 34)[i], [P, 512]) for i in range(4)]
        idx = [at(f"idx{i}", MISC + 29.25 + 0.03125 * i, [P, 1], I32) for i in range(4)]
        yab = [at(f"yab{c}", 132 + 8 * c, [P, 2, D]) for c in range(NC)]
        wc = [at(f"wc{s}", RING + 24 * s, [P, KT, 3, P]) for s in range(2)]
        wc_lo = [at(f"wc_lo{s}", RING + 24 * s, [P, KT, 3, P], F32R) for s in range(2)]
        wc_hi = [at(f"wc_hi{s}", RING + 24 * s + 12, [P, KT, 3, P], F32R) for s in range(2)]
        xc_lo = at("xc_lo", RING + 48, [P, KT, T], F32R)
        g_hi = at("g_hi", 152, [P, KT, T], F32R)
        g_lo = at("g_lo", MISC, [P, KT, T], F32R)
        woc = [at("woc0", RING + 65, [P, KT, 512]), at("woc1", RING, [P, KT, 512])]
        woc_lo = [at("woc_lo0", RING + 65, [P, KT, 512], F32R), at("woc_lo1", RING, [P, KT, 512], F32R)]
        woc0_hi = [at("woc0_hi0", RING + 81, [P, KT // 2, 512], F32R), at("woc0_hi1", MISC + 27.5, [P, KT // 2, 512], F32R)]
        woc1_hi = at("woc1_hi", RING + 16, [P, KT, 512], F32R)
        UW = 2 + SEQ + 2 + DEC
        gT = at("gT", MISC, [P, KT, T])
        u = at("u", MISC + 17, [P, UW])
        hc = [at(f"hc{i}", MISC + 21.5 + 1.25 * i, [P, HALF]) for i in range(2)]
        cv = at("cv", MISC + 24, [P, T])
        hist = at("hist", MISC + 26.25, [P, KT, 2])
        tails = at("tails", MISC + 26.5, [P, 2, KT, 2])

        bank = [ctx.enter_context(nc.psum_tensor(f"bank{i}", [P, 512], F32)) for i in range(8)]

        rev_dram = nc.dram_tensor("rev_bias", [NH, 640], F32, kind="Internal").ap()
        revs_dram = nc.dram_tensor("rev_bias_copies", [NH, 32, 640], F32, kind="Internal").ap()
        y_dram = [nc.dram_tensor(f"y_rows{i}", [2 * T * 2, 512], F32, kind="Internal").ap() for i in range(2)]

        x_in = sem("x_in"); gmix_in = sem("gmix_in"); gffn_in = sem("gffn_in"); tab_in = sem("tab_in");
        pool_c = sem("pool_c"); const_ok = sem("const_ok")
        h_ok = sem("h_ok")
        sq_done = sem("sq_done"); ms_ok = sem("ms_ok"); rt_ok = sem("rt_ok")
        xn_ok = sem("xn_ok"); xt_mm = sem("xt_mm"); xt_a = sem("xt_a"); xt_d = sem("xt_d")
        dch = sem("dch"); ach = sem("ach")
        wab_in = [sem(f"wab_in{s}") for s in range(3)]
        w_hi = sem("w_hi"); w_lo = sem("w_lo")
        z_hi = sem("z_hi"); z_lo = sem("z_lo")
        z_mm = sem("z_mm"); z_free = [sem(f"z_free{b}") for b in range(4)]

        f_ok = sem("f_ok"); ln_ok = sem("ln_ok"); cum_ok = sem("cum_ok"); exp_ok = sem("exp_ok")
        hg_ok = sem("hg_ok")
        qsq_ok = sem("qsq_ok"); qms_ok = sem("qms_ok"); qrt_ok = sem("qrt_ok"); qk_ok = sem("qk_ok")
        v_ok = sem("v_ok"); out_dma = sem("out_dma"); qkT_mm = sem("qkT_mm"); qkT_ok = sem("qkT_ok")
        rb_dma = sem("rb_dma"); bias_in = sem("bias_in");
        cache_in = sem("cache_in"); kc_mm = sem("kc_mm"); kc_ok = sem("kc_ok"); st_in = sem("st_in")
        ko_mm = sem("ko_mm"); ko_ok = sem("ko_ok"); qd_ok = sem("qd_ok"); vx_ok = sem("vx_ok"); a_mm = sem("a_mm"); a_ok = sem("a_ok")
        u_mm = sem("u_mm"); st_ok = sem("st_ok"); o_mm = sem("o_mm"); osq_ok = sem("osq_ok"); hms_ok = sem("hms_ok")
        os_ok = sem("os_ok"); zt_ok = sem("zt_ok"); zt_mm = sem("zt_mm"); orms_ok = sem("orms_ok"); zB_ok = sem("zB_ok")
        s_mm = sem("s_mm"); s_ok = sem("s_ok"); p_ok = sem("p_ok"); pT_mm = sem("pT_mm")
        pT_a = sem("pT_a"); pT_d = sem("pT_d"); pv_mm = sem("pv_mm"); dg_ok = sem("dg_ok"); rb_mm = sem("rb_mm"); rb_ok = sem("rb_ok"); zn_ok = sem("zn_ok")
        zAh_ok = sem("zAh_ok"); zA_ok = sem("zA_ok")
        wo_in = [sem(f"wo_in{s}") for s in range(2)]
        op_mm = sem("op_mm"); op_add = sem("op_add")
        wr_in = sem("wr_in"); lg_mm = sem("lg_mm"); lg_ok = sem("lg_ok"); ge_ok = sem("ge_ok"); gx_ok = sem("gx_ok")
        e2_ok = sem("e2_ok"); ex_ok = sem("ex_ok")
        msk_ok = sem("msk_ok"); rk_mm = sem("rk_mm"); rk_ok = sem("rk_ok"); xhi_ok = sem("xhi_ok"); xlo_ok = sem("xlo_ok"); cm_mm = sem("cm_mm"); cnt_ok = sem("cnt_ok")
        w13_in = [sem(f"w13_in{s}") for s in range(4)]
        w2_in = [sem(f"w2_in{s}") for s in range(4)]
        sel_ok = sem("sel_ok"); g_mm = sem("g_mm"); ix_mm = sem("ix_mm"); xg_a = sem("xg_a"); xg_d = sem("xg_d")
        ix_ok = sem("ix_ok"); h_mm = sem("h_mm"); sg_ok = sem("sg_ok"); hh_ok = sem("hh_ok"); t_mm = sem("t_mm")
        ht_ok = sem("ht_ok"); y_mm = sem("y_mm"); ys_ok = sem("ys_ok"); scat = [sem(f"scat{j}") for j in range(4)]
        yab_in = [sem(f"yab_in{c}") for c in range(NC)]

        ov = [{n: sem(f"ov{l}_{n}") for n in ("free", "w", "rk", "sel", "mm", "xg", "ix", "act", "hid", "sc")}
              for l in range(2)]
        for o in ov:
            o.update({n: o["mm"] for n in ("g", "ixm", "h", "t", "y")})
        wc_in = [sem(f"wc_in{s}") for s in range(2)]
        c_mm = sem("c_mm"); hc_ok = sem("hc_ok"); cg_ok = sem("cg_ok"); tail_ok = sem("tail_ok")
        lbm_ok = sem("lbm_ok"); lbe_ok = sem("lbe_ok"); ys_free = sem("ys_free")
        woc_in = [sem(f"woc_in{s}") for s in range(2)]
        y_out = sem("y_out")

        NXT = 2 * NC
        PAIRS = NE // 2

        block = ctx.enter_context(nc.Block())


        class Chain:
            def __init__(self, eng, done):
                self.eng, self.done, self.n, self.run_on = eng, done, 0, 0

            def __call__(self, ins):
                self.n += 1
                ins.then_inc(self.done, 1)
                self.eng.wait_ge(self.done, self.n + self.run_on)

            def loop(self, i, steps, times):
                self.run_on, self.steps, self.times, self.first = i * steps, steps, times, self.n

            def end(self):
                assert self.n == self.first + self.steps, (self.n - self.first, self.steps)
                self.n, self.run_on = self.first + self.steps * self.times, 0

        def bc(ap, shape):
            return ap.to_broadcast(shape)

        zeroed = []

        @block.sync
        def _(sp):
            for c in range(4):
                sp.dma_start(H[:, c, :], x_prompt[0, c * P:(c + 1) * P, :]).then_inc(x_in, 16)
            sp.dma_start(H[0:DEC, 4, :], x_sample[0, :, :]).then_inc(x_in, 16)
            sp.dma_start(gmix[:], norm_mix[0:1, :].partition_broadcast(P)).then_inc(gmix_in, 16)

            def group_load(n):
                first = GROUPS[n // 2] * DA + (n % 2) * HG
                sp.dma_start(wab[n % 3][:], w_in_ab[0, :, first:first + HG].rearrange("(k p) n -> p k n", p=P))\
                    .then_inc(wab_in[n % 3], 16)
            for n in range(3):
                group_load(n)
            with nc.allow_non_contiguous_dma(reason="per-feature tables, one element per partition"):
                sp.dma_start(lbl[:].rearrange("p (r m) -> p r m", r=2), hgrn_lb_logits.rearrange("r (m p) -> p r m", p=P)).then_inc(tab_in, 16)
                sp.dma_start(onorm[:], hgrn_out_norm[0].rearrange("(m p) -> p m", p=P)).then_inc(tab_in, 16)
                sp.dma_start(convw[:].rearrange("p (j k) -> p j k", j=3), conv_w[0].rearrange("j (k p) -> p j k", p=P)).then_inc(tab_in, 16)
                sp.dma_start(rev_dram[:, 384:639].unsqueeze(2), bass.AP(rel_bias.tensor, 2 * REL - 1, [[2 * REL + 1, NH], [-1, 255], [1, 1]])).then_inc(rb_dma, 16)
                sp.dma_start(rev_dram[:, 0:384].unsqueeze(2), bass.AP(rel_bias.tensor, 2 * REL, [[2 * REL + 1, NH], [0, 384], [1, 1]])).then_inc(rb_dma, 16)
            sp.dma_start(qgain[:], q_norm[0:1, :].partition_broadcast(P)).then_inc(tab_in, 16)
            sp.dma_start(kgain[:], k_norm[0:1, :].partition_broadcast(P)).then_inc(tab_in, 16)
            sp.dma_start(gffn[:], norm_ffn[0:1, :].partition_broadcast(P)).then_inc(gffn_in, 16)
            for n in range(3, 14):
                sp.wait_ge(z_mm, UNIT_END[n - 3])
                group_load(n)
            sp.wait_ge(rb_dma, 32)
            sp.dma_start(revs_dram[:, :, 0:639], bc(rev_dram[:, 0:639].unsqueeze(1), [NH, 32, 639])).then_inc(rb_dma, 16)
            sp.dma_start(nk_s[0, 0, 0:PAST - DEC], cache_a_k[0, 0, DEC:]).then_inc(out_dma, 16)
            sp.dma_start(nv_s[0, 0, 0:PAST - DEC], cache_a_v[0, 0, DEC:]).then_inc(out_dma, 16)
            sp.wait_ge(qk_ok, 4 * NC)
            sp.dma_start(nk_p[0, 0].rearrange("(c p) h d -> p c (h d)", p=P), k_tok[:, 0:4, :]).then_inc(out_dma, 16)
            sp.dma_start(nk_s[0, 0, PAST - DEC:].rearrange("t h d -> t (h d)"), k_tok[0:DEC, 4, :]).then_inc(out_dma, 16)
            sp.wait_ge(rb_dma, 48)
            sp.wait_ge(z_mm, UNIT_END[-1])
            for a in range(4):
                sp.dma_start(bias[32 * a:32 * a + 32, :, :],
                             bass.AP(revs_dram.tensor, P - 1 - 32 * a, [[639, 32], [32 * 640, NH], [1, 512]])).then_inc(bias_in, 16)
            sp.wait_ge(v_ok, 2 * NC)
            sp.dma_start(nv_p[0, 0].rearrange("(c p) h d -> p c (h d)", p=P), va[:, 0:4, :]).then_inc(out_dma, 16)
            sp.dma_start(nv_s[0, 0, PAST - DEC:].rearrange("t h d -> t (h d)"), va[0:DEC, 4, :]).then_inc(out_dma, 16)
            sp.wait_ge(o_mm, 3)
            sp.wait_ge(st_ok, 4)
            sp.dma_start(st[0][:, 0, :, :], state_hgrn[0, 0].rearrange("(a b) k v -> (b k) a v", b=2)).then_inc(st_in, 16)
            sp.dma_start(nh_p[0, 0].rearrange("(a b) k v -> (b k) a v", b=2), st[1][:, 8, :, :]).then_inc(out_dma, 16)
            sp.wait_ge(st_ok, 5)
            sp.dma_start(nh_s[0, 0].rearrange("(a b) k v -> (b k) a v", b=2), st[0][:, 2, :, :]).then_inc(out_dma, 16)
            sp.wait_ge(zB_ok, NC)
            sp.wait_ge(out_dma, 16 * 8)
            for s in range(2):
                sp.dma_start(wo[s][:], w_out_ab[0, :, s * 512:(s + 1) * 512].rearrange("(k p) n -> p k n", p=P)).then_inc(wo_in[s], 16)
            sp.wait_ge(qkT_mm, 2 * NC)
            sp.dma_start(kc[:], cache_a_k[0, 0].rearrange("t h d -> t (h d)")).then_inc(cache_in, 16)
            sp.dma_start(vc[:], cache_a_v[0, 0].rearrange("t h d -> t (h d)")).then_inc(cache_in, 16)

            def w13_load(l, e, s, done):
                for part, w in enumerate((w1, w3)):
                    sp.dma_start(w13[s][:, :, part, :], w[l, bass.ds(e, 1)].rearrange("e (k p) f -> p (e k) f", p=P)).then_inc(done, 16)

            def w2_load(l, e, s, done):
                sp.dma_start(w2s[s][:], w2[l, bass.ds(e, 1)].rearrange("e (a p) n -> p (e a) n", p=P)).then_inc(done, 16)

            def first_load(l, j):
                s = (j + 2) % 4
                w13_load(l, j, s, w13_in[s])
                w2_load(l, j, s, w2_in[s])

            def router_load(l):
                sp.dma_start(wr[:, :, 0:NG], w_group[l].rearrange("(k p) n -> p k n", p=P)).then_inc(wr_in, 16)
                sp.dma_start(wr[:, :, NG:NR], w_expert[l].rearrange("(k p) n -> p k n", p=P)).then_inc(wr_in, 16)
                sp.dma_start(biasr[:, 0:NG], b_group[l:l + 1, :].partition_broadcast(P)).then_inc(wr_in, 16)
                sp.dma_start(biasr[:, NG:NR], b_expert[l:l + 1, :].partition_broadcast(P)).then_inc(wr_in, 16)

            wcv = w_in_c[0].rearrange("(k p) (a m n) -> a m p k n", p=P, a=3, n=P)

            def conv_load(m, s):
                for a in range(3):
                    sp.dma_start(wc[s][:, :, a, :], wcv[a, bass.ds(m, 1)].rearrange("m p k n -> p (m k) n")).then_inc(wc_in[s], 16)

            def mixture(l):
                with sp.Fori(0, NE // 4 - 1) as i:
                    for j in range(4):
                        s = (j + 2) % 4
                        sp.wait_ge(h_mm, i * 4 + (l * NE + j + 1))
                        w13_load(l, 4 * i + 4 + j, s, w13_in[s])
                        sp.wait_ge(y_mm, i * 4 + (l * NE + j + 1))
                        w2_load(l, 4 * i + 4 + j, s, w2_in[s])
                sp.wait_ge(y_mm, NE * (l + 1))
                if l == 0:
                    sp.dma_start(gmix[:], norm_mix[1:2, :].partition_broadcast(P)).then_inc(gmix_in, 16)
                    for s in range(2):
                        conv_load(s, s)
                sp.wait_ge(cnt_ok, l + 1)
                for j in range(4):
                    sp.wait_ge(scat[j], 16 * (NE // 4) * (l + 1))
                most = sp.value_load(cnt_i[0:1, l:l + 1], min_val=0, max_val=T)
                with sp.If(most > CAP), sp.Fori(0, ROUNDS - 1) as r:
                    with sp.If(most > CAP * r + CAP):
                        with sp.Fori(0, NE) as e:
                            sp.wait_ge(ov[l]["free"], r * NE + e + 1)
                            w13_load(l, e, 3, ov[l]["w"])
                            w2_load(l, e, 3, ov[l]["w"])
                        sp.wait_ge(ov[l]["free"], r * NE + NE + 1)
                        sp.nop(nofuse=True)
                rows = y_dram[l].rearrange("(r b) d -> r (b d)", b=2)
                for c in range(NC):
                    for i in range(2):
                        first = i * T + c * P
                        sp.dma_start(yab[c][0:ROWS[c], i, :], rows[first:first + ROWS[c], :]).then_inc(yab_in[c], 16)

            sp.wait_ge(rb_mm, NC)
            router_load(0)
            sp.wait_ge(op_mm, NC)
            first_load(0, 2)
            sp.wait_ge(op_mm, 2 * NC)
            for j in (0, 1, 3):
                first_load(0, j)
            mixture(0)

            sp.dma_start(gffn[:], norm_ffn[1:2, :].partition_broadcast(P)).then_inc(gffn_in, 16)
            sp.wait_ge(lg_ok, 1)
            sp.wait_ge(lg_mm, 1)
            router_load(1)
            with nc.allow_non_contiguous_dma(reason="two frames of each feature"):
                for r in range(2):
                    sp.dma_start(hist[:, :, r], state_conv[0, 0, r].rearrange("(k p) -> p k", p=P)).then_inc(st_in, 16)
            def woc_load(s):
                sp.dma_start(woc[s][:], w_out_c[0, :, s * 512:(s + 1) * 512].rearrange("(k p) n -> p k n", p=P)).then_inc(woc_in[s], 16)
            woc_load(0)
            with sp.Fori(0, KT // 2 - 1) as i:
                for s in range(2):
                    sp.wait_ge(c_mm, i * 4 + (2 * s + 2))
                    conv_load(2 * i + (2 + s), s)
            sp.wait_ge(c_mm, 2 * KT - 2)
            woc_load(1)
            sp.wait_ge(tail_ok, KT)
            with nc.allow_non_contiguous_dma(reason="two frames of each feature"):
                for j, dst in enumerate((nconv_p, nconv_s)):
                    for r in range(2):
                        sp.dma_start(dst[0, 0, r, :].rearrange("(k p) -> p k", p=P), tails[:, j, :, r]).then_inc(out_dma, 16)
            sp.wait_ge(op_mm, 3 * NC)
            for j in (0, 1):
                first_load(1, j)
            sp.wait_ge(op_mm, 4 * NC)
            for j in (2, 3):
                first_load(1, j)
            mixture(1)
            for c in range(NC):
                sp.wait_ge(h_ok, 3 * NC + c + 1)
                dst = y_prompt[0, c * P:(c + 1) * P, :] if c < 4 else y_sample[0, :, :]
                sp.dma_start(dst, H[0:ROWS[c], c, :]).then_inc(y_out, 16)
            sp.wait_ge(y_out, 16 * NC)
            sp.wait_ge(out_dma, 16 * 12)

        @block.gpsimd
        def _(pool):
            tie = Chain(pool, pool_c)

            def tri(t, view, pattern, base, mult, op, fill=0.0):
                tie(pool.affine_select(out=view, in_=view, compare_op=op, fill=fill, base=base, pattern=pattern,
                                       channel_multiplier=mult))
            tie(pool.memset(H[32:64, 4, :], 0.0))
            tie(pool.memset(H[64:128, 4, :], 0.0))
            tie(pool.memset(ident[:], 0.0))
            tri(ident, ident[:], [[-1, P]], 0, 1, ALU.not_equal, 1.0)
            tie(pool.memset(upper[:], 1.0))
            tri(upper, upper[:], [[1, P]], 0, -1, ALU.is_gt)
            tie(pool.memset(ones[:], 1.0))
            tie(pool.memset(blk_mask[:], 1.0))
            tri(blk_mask, blk_mask[:], [[1, P]], 0, -1, ALU.is_ge)
            tri(blk_mask, blk_mask[:].rearrange("p (b t) -> p b t", t=BLK), [[-BLK, P // BLK], [0, BLK]], 0, 1, ALU.is_ge)
            tie(pool.memset(blk_sel[:], 1.0))
            tri(blk_sel, blk_sel[:], [[-32, 4]], 0, 1, ALU.is_ge)
            tri(blk_sel, blk_sel[:], [[32, 4]], BLK - 1, -1, ALU.is_ge)
            tie(pool.iota(slot_no[:], [[1, CAP]], base=0, channel_multiplier=0, allow_small_or_imprecise_dtypes=True))
            tie(pool.iota(frame_no[:], [[P, NC]], base=0, channel_multiplier=1, allow_small_or_imprecise_dtypes=True))
            tie(pool.iota(rev4[:], [[-1, NG]], base=NG, channel_multiplier=0, allow_small_or_imprecise_dtypes=True))
            tie(pool.iota(rev8[:], [[-1, EPG]], base=EPG, channel_multiplier=0, allow_small_or_imprecise_dtypes=True))
            tie(pool.memset(frame_ok[:], 1.0))
            tri(frame_ok, frame_ok[:], [[-P, NC]], T - 1, -1, ALU.is_ge)
            tie(pool.memset(epsc[:], EPS))
            tie(pool.memset(reset[:], 1.0))
            tie(pool.memset(reset[:].rearrange("p (b t) -> p b t", t=BLK)[:, :, 0], 0.0))
            pool.nop().then_inc(const_ok, 1)
            pool.nop().then_inc(ys_free, 4)

            def split(raw, hi, lo):
                for r, x, y in zip(raw, hi, lo):
                    last = pool.tensor_copy(x, r)
                last.then_inc(w_hi, 1)
                pool.wait_ge(w_hi, split.n + 1)
                for r, x, y in zip(raw, hi, lo):
                    last = pool.tensor_tensor(y, r, x.bitcast(F32), ALU.subtract)
                last.then_inc(w_lo, 1)
                split.n += 1
            for n in range(14):
                pool.wait_ge(w_hi, n + 1)
                pool.tensor_tensor(wab_lo[n % 3][:], wab[n % 3][:], wab_hi[n % 3][:].bitcast(F32), ALU.subtract).then_inc(w_lo, 1)
            split.n = 14
            pool.wait_ge(z_mm, UNIT_END[-1])
            tie(pool.memset(kout[:], 0.0))
            tie(pool.memset(qdecs[1][0:64, :, :], 0.0))
            zeroed.append(tie.n)
            for b in range(4):
                pool.wait_ge(z_free[b], 16)
            for c in range(NC):
                n = ROWS[c]
                v = vb[0:n, c, :].rearrange("p (h d) -> p h d", h=NH)
                if c >= 2:
                    pool.wait_ge(o_mm, c - 1)
                for i, own in enumerate((even, odd)):
                    last = pool.tensor_tensor(vx[c % 2][0:n, :, i, :], v, bc(own[0:n, :].unsqueeze(2), [n, NH, HD]), ALU.mult)
                last.then_inc(vx_ok, 1)
            pool.wait_ge(zB_ok, NC)
            tie(pool.memset(qTs[0][64:128, :, :], 0.0))
            tie(pool.memset(qTs[1][0:64, :, :], 0.0))
            zeroed.append(tie.n)
            for s in range(2):
                pool.wait_ge(wo_in[s], 16)
                if s == 1:
                    pool.wait_ge(s_mm, NC * NH)
                split([wo[s][:]], [wo_hi[s][:]], [wo_lo[s][:]])

            def conv_splits():
                with pool.Fori(0, KT // 2) as i:
                    for s in range(2):
                        pool.wait_ge(wc_in[s], i * 48 + 48)
                        pool.wait_ge(w_hi, i * 2 + (16 + s + 1))
                        pool.tensor_tensor(wc_lo[s][:], wc[s][:], wc_hi[s][:].bitcast(F32), ALU.subtract).then_inc(w_lo, 1)

            for l in range(2):
                yd = y_dram[l]
                if l == 1:
                    conv_splits()
                    split.n += KT
                    k2 = KT // 2
                    pool.wait_ge(woc_in[0], 16)
                    split([woc[0][:, 0:k2, :], woc[0][:, k2:KT, :]], [woc0_hi[0][:], woc0_hi[1][:]],
                          [woc_lo[0][:, 0:k2, :], woc_lo[0][:, k2:KT, :]])
                    pool.wait_ge(woc_in[1], 16)
                    pool.wait_ge(c_mm, 2 * KT)
                    split([woc[1][:]], [woc1_hi[:]], [woc_lo[1][:]])

                def scatter(i, done):
                    pool.indirect_dma_start(yd[:, :], bass.IndirectOffsetOnAxis(ap=idx[i][:, 0:1].bitcast(U32), axis=0),
                                            ys[i][:, :], None, bounds_check=4 * T - 1, oob_is_err=False).then_inc(done, 16)
                for c in range(NC):
                    pool.wait_ge(xhi_ok, NC * l + c + 1)
                    pool.tensor_tensor(x_lo[:, c, :], XN[:, c, :], x_hi[:, c, :].bitcast(F32), ALU.subtract).then_inc(xlo_ok, 1)

                def stored(i, j):
                    pool.wait_ge(scat[j], i * 16 + 16 * (l * (NE // 4) + 1))
                    pool.nop().then_inc(ys_free, 1)

                def scatters(i, first):
                    for j in range(4):
                        pool.wait_ge(ix_ok, i * 2 + (l * (PAIRS + 1) + j // 2 + 1))
                        pool.wait_ge(ys_ok, i * 4 + (l * NE + j + 3))
                        pool.nop(nofuse=True)
                        scatter(j, scat[j])
                        if j >= 2:
                            stored(i, j - 2)
                        elif not first:
                            stored(i - 1, j + 2)
                scatters(0, True)
                with pool.Fori(1, NE // 4) as i:
                    scatters(i, False)
                for j in (2, 3):
                    stored(NE // 4 - 1, j)
                pool.wait_ge(cnt_ok, l + 1)
                most = pool.value_load(cnt_i[0:1, l:l + 1], min_val=0, max_val=T)
                o = ov[l]
                pool.nop().then_inc(o["free"], 1)
                with pool.If(most > CAP), pool.Fori(0, ROUNDS - 1) as r:
                    with pool.If(most > CAP * r + CAP):
                        with pool.Fori(0, NE) as e:
                            pool.wait_ge(o["ix"], r * NE + e + 1)
                            pool.wait_ge(o["act"], r * (2 * NE) + e * 2 + 2)
                            pool.nop(nofuse=True)
                            scatter(0, o["sc"])
                            pool.wait_ge(o["sc"], r * (16 * NE) + e * 16 + 16)
                            pool.nop().then_inc(o["free"], 1)

        @block.tensor
        def _(pe):
            def norm_transposes(n):
                for c in range(NC):
                    pe.wait_ge(xn_ok, NC * n + c + 1)
                    if n == 0 and c == 0:
                        pe.wait_ge(const_ok, 1)
                    low = 6 if n % 2 == 1 or c % 2 == 0 else 4
                    if n % 2 == 0 and c > 1:
                        pe.wait_ge(xt_d, NC * n + c - 1)
                    for half in range(2):
                        if n % 2 == 1 and c > 0:
                            pe.wait_ge(xt_a if half == 0 else xt_d, NC * n + c)
                        for kk in range(4):
                            k = 4 * half + kk
                            last = pe.transpose(bank[low + half][:, kk * P:kk * P + ROWS[c]], XN[0:ROWS[c], c, k * P:(k + 1) * P],
                                                ident[0:ROWS[c], 0:ROWS[c]])
                        last.then_inc(xt_mm, 1)

            norm_transposes(0)
            pe.wait_ge(xt_a, NC)
            pe.wait_ge(xt_d, NC)
            u_ = 0
            for n in range(14):
                pe.wait_ge(w_lo, n + 1)
                wh, wl = wab_hi[n % 3], wab_lo[n % 3]
                for a in range(4 if n < 6 else NC):
                    if u_ >= 4:
                        pe.wait_ge(z_free[u_ % 4], u_ // 4)
                    for k in range(KT):
                        for j, (w, x) in enumerate(((wh, xc_hi), (wh, xp_lo), (wl, xc_hi))):
                            flags = dict(start=k == 0 and j == 0, stop=k == KT - 1 and j == 2)
                            if n < 6:
                                m, half = a // 2, a % 2
                                last = pe.matmul(bank[u_ % 4][:, 0:HALF], w[:, k, m * P:(m + 1) * P],
                                                 x[:, k, half * HALF:(half + 1) * HALF], **flags)
                            else:
                                last = pe.matmul(bank[u_ % 4][0:ROWS[a], 0:HG], x[:, k, a * P:a * P + ROWS[a]], w[:, k, :], **flags)
                    last.then_inc(z_mm, 1)
                    u_ += 1
            def hgrn_keys(c):
                if c == 0:
                    pe.wait_ge(hg_ok, 3)
                    for b in range(4):
                        pe.wait_ge(z_free[b], 16)
                else:
                    pe.wait_ge(a_ok, 2 * c)
                for m in range(4):
                    last = pe.transpose(bank[1][0:ROWS[c], m * P:(m + 1) * P], koutT[:, m, c * P:c * P + ROWS[c]], ident[:])
                last.then_inc(ko_mm, 1)

            def hgrn_products(c):
                n, t0 = ROWS[c], c * P
                if c == 0:
                    pe.wait_ge(qd_ok, 1)
                    pe.wait_ge(pool_c, zeroed[0])
                pe.wait_ge(ko_ok, c + 1)
                for m in range(4):
                    for par in range(2):
                        last = pe.matmul(bank[1 + par][0:n, m * P:m * P + n], kinT[:, m, t0:t0 + n],
                                         qdecs[par][:, m, t0:t0 + n], start=True, stop=True)
                last.then_inc(a_mm, 1)

            def hgrn_updates(c):
                n = ROWS[c]
                pe.wait_ge(vx_ok, c + 1)
                if c > 0:
                    pe.wait_ge(st_ok, c)
                for r in range(n // 32):
                    for h in range(NH):
                        last = pe.matmul(bank[3 + r][64 * (h % 2):64 * (h % 2) + 64, (h // 2) * P:(h // 2 + 1) * P],
                                         kout[0:n, r, h * HD:(h + 1) * HD],
                                         vx[c % 2][0:n, h, :, :].rearrange("p i v -> p (i v)"), start=True, stop=True)
                last.then_inc(u_mm, 1)

            def hgrn_out(c):
                n, t0 = ROWS[c], c * P
                outs = (bank[0], bank[7])
                pe.wait_ge(a_ok, 2 * c + 2)
                pe.wait_ge(st_ok, c + 1)
                if c > 0:
                    pe.wait_ge(zB_ok, c)
                for m in range(4):
                    for par in range(2):
                        pe.matmul(outs[par][0:n, m * P:(m + 1) * P], am[c % 2][0:n, par, m, 0:n],
                                  vx[c % 2][0:n, 2 * m + par, :, :].rearrange("p i v -> p (i v)"), start=True, stop=False)
                    for par in range(2):
                        for r in range(n // 32):
                            last = pe.matmul(outs[par][32 * r:32 * r + 32, m * P:(m + 1) * P].rearrange("p (i v) -> p i v", i=2),
                                             qdecs[par][:, m, t0 + 32 * r:t0 + 32 * r + 32],
                                             st[c % 2][:, 2 * r:2 * r + 2, m, :], start=False, stop=True)
                last.then_inc(o_mm, 1)

            def hgrn_T(c):
                n = ROWS[c]
                pe.wait_ge(zt_ok, c + 1)
                for m in range(4):
                    last = pe.transpose(bank[7][:, m * P:m * P + n], ot[0:n, m * P:(m + 1) * P], ident[0:n, 0:n])
                last.then_inc(zt_mm, 1)

            for c in range(2):
                hgrn_keys(c)
                hgrn_products(c)
                hgrn_updates(c)
            for c in range(NC):
                if c + 2 < NC:
                    hgrn_keys(c + 2)
                hgrn_out(c)
                if c + 2 < NC:
                    hgrn_products(c + 2)
                    hgrn_updates(c + 2)
                hgrn_T(c)

            for i in range(2 * NC):
                c, src = i // 2, (q_tok, k_tok)[i % 2]
                if i == 0:
                    pe.wait_ge(qk_ok, 4 * NC)
                    pe.wait_ge(zB_ok, NC)
                if i >= 2:
                    pe.wait_ge(qkT_ok, i - 1)
                for m in range(4):
                    last = pe.transpose(bank[4 + i % 2][:, m * P:m * P + ROWS[c]], src[0:ROWS[c], c, m * P:(m + 1) * P],
                                        ident[0:ROWS[c], 0:ROWS[c]])
                last.then_inc(qkT_mm, 1)

            NU = NC * NH
            pe.wait_ge(qkT_ok, 2 * NC)
            pe.wait_ge(pool_c, zeroed[1])

            def cached_T():
                pe.wait_ge(cache_in, 32)
                for m in range(4):
                    last = pe.transpose(bank[7][:, m * P:(m + 1) * P], kc[:, m * P:(m + 1) * P], ident[:])
                last.then_inc(kc_mm, 1)

            def scores(i):
                c, h = divmod(i, NH)
                m = h // 2
                if i >= 2:
                    pe.wait_ge(s_ok, i - 1)
                q = qTs[h % 2][:, m, c * P:c * P + ROWS[c]]
                if c < 4:
                    last = pe.matmul(bank[i % 2][:, 0:P * (c + 1)], q, kT[:, m, 0:P * (c + 1)], start=True, stop=True)
                else:
                    pe.wait_ge(kc_ok, 1)
                    pe.matmul(bank[i % 2][0:DEC, 0:PAST], q, kcT[:, m, :], start=True, stop=True)
                    last = pe.matmul(bank[i % 2][0:DEC, PAST:PAST + DEC], q, kT[:, m, SEQ:T], start=True, stop=True)
                last.then_inc(s_mm, 1)

            def keys(c):
                return [(P * j, P) for j in range(c + 1)] if c < 4 else [(0, PAST), (PAST, DEC)]

            def probs_T(i):
                c, h = divmod(i, NH)
                n = ROWS[c]
                pe.wait_ge(p_ok, i + 1)
                if i >= 2:
                    pe.wait_ge(pT_a if i % 2 == 0 else pT_d, i // 2)
                for j, (k0, nk) in enumerate(keys(c)):
                    last = pe.transpose(bank[2 + i % 2][0:nk, j * P:j * P + n], pr[i % 2][0:n, k0:k0 + nk], ident[0:n, 0:n])
                last.then_inc(pT_mm, 1)

            def values(i):
                c, h = divmod(i, NH)
                n = ROWS[c]
                pe.wait_ge(pT_a if i % 2 == 0 else pT_d, i // 2 + 1)
                if h == 0 and c >= 2:
                    pe.wait_ge(zn_ok, c - 1)
                for j, (k0, nk) in enumerate(keys(c)):
                    v = va[:, j, :] if c < 4 else (vc[:, :], va[0:DEC, 4, :])[j]
                    last = pe.matmul(bank[4 + c % 2][64 * (h % 2):64 * (h % 2) + 64, (h // 2) * P:(h // 2) * P + n],
                                     v[:, h * HD:(h + 1) * HD], prT[i % 2][0:nk, j, 0:n],
                                     start=j == 0, stop=j == len(keys(c)) - 1)
                last.then_inc(pv_mm, 1)

            def sums_along(c):
                n = ROWS[c]
                pe.wait_ge(dg_ok, c + 1)
                if c > 0:
                    pe.wait_ge(rb_ok, c)
                for par in range(2):
                    last = pe.matmul(bank[6][64 * par:64 * par + 64, :].rearrange("p (m t) -> p m t", m=4)[:, :, 0:n],
                                     ones[0:n, 0:64], dg[0:n, par, :, 0:n], start=True, stop=True)
                last.then_inc(rb_mm, 1)

            for i in range(NU + 4):
                if i < NU:
                    scores(i)
                if 1 <= i <= NU:
                    probs_T(i - 1)
                if 2 <= i <= NU + 1:
                    values(i - 2)
                if i >= 10 and (i - 10) % NH == 0:
                    sums_along((i - 10) // NH)
                if i == 2 * NH:
                    cached_T()
            pe.wait_ge(zA_ok, NC)

            def project_out(n, z, w, splits):
                for i in range(2 * NC):
                    s, c = divmod(i, NC)
                    if c == 0:
                        pe.wait_ge(w_lo, splits + s)
                    if i < NC:
                        z.arrived(c)
                    if i >= 4:
                        pe.wait_ge(op_add, 2 * NC * n + i - 3)
                    for k in range(KT):
                        for j, (a, b) in enumerate(((0, 0), (1, 0), (0, 1))):
                            last = pe.matmul(bank[i % 4][0:ROWS[c], :], z(a, k)[:, c * P:c * P + ROWS[c]], w(b, k, s),
                                             start=k == 0 and j == 0, stop=k == KT - 1 and j == 2)
                    last.then_inc(op_mm, 1)

            def z_ab(part, k):
                return ((zA_hi, zA_lo), (zB_hi, zB_lo))[k // 4][part][:, k % 4, :]
            z_ab.arrived = lambda c: pe.wait_ge(z_lo, 1) if c == 0 else None
            pe.wait_ge(zA_ok, NC)
            project_out(0, z_ab, lambda part, k, s: (wo_hi, wo_lo)[part][s][:, k, :], 15)

            def mixture(l):
                norm_transposes(2 * l + 1)
                pe.wait_ge(xt_a, NC * (2 * l + 2))
                pe.wait_ge(xt_d, NC * (2 * l + 2))
                pe.wait_ge(op_add, 2 * NC * (l + 1))
                pe.wait_ge(wr_in, 64 * (l + 1))
                for c in range(NC):
                    for k in range(KT):
                        last = pe.matmul(bank[0][0:ROWS[c], c * NR:(c + 1) * NR], XT[:, k, c * P:c * P + ROWS[c]], wr[:, k, :],
                                         start=k == 0, stop=k == KT - 1)
                last.then_inc(lg_mm, 1)
                pe.wait_ge(msk_ok, l + 1)
                mask = rt[0][:].rearrange("p c n -> p (c n)")
                pe.matmul(bank[1][:, 0:NC * NE], upper[:], mask, start=True, stop=False)
                for j in range(1, NC):
                    last = pe.matmul(bank[1][:, j * NE:NC * NE], ones[:], mask[:, 0:(NC - j) * NE], start=False, stop=j == NC - 1)
                last.then_inc(rk_mm, 1)
                pe.wait_ge(rk_ok, l + 1)
                pe.matmul(bank[2][0:1, 0:P], c1[7][:, 0:1], ident[:], start=True, stop=True).then_inc(cm_mm, 1)

                def gather(half, q):
                    for kk in range(4):
                        for c in range(NC):
                            for part in (x_hi, x_lo):
                                last = pe.matmul(bank[kk // 2][:, (kk % 2) * 4 * CAP:(kk % 2 + 1) * 4 * CAP],
                                                 part[:, c, (4 * half + kk) * P:(4 * half + kk + 1) * P],
                                                 seln[:, c, :, :].rearrange("p a s -> p (a s)"),
                                                 start=c == 0 and part is x_hi, stop=c == NC - 1 and part is x_lo)
                    last.then_inc(q["g"], 1)

                def numbers(e, q):
                    for b in range(2):
                        for c in range(NC):
                            last = pe.matmul(bank[2][:, 2 * b:2 * b + 2], seln[:, c, 2 * b:2 * b + 2, :].rearrange("p a s -> p (a s)"),
                                             dv[:, c, bass.ds(e + 2 * b, 2)], start=c == 0, stop=c == NC - 1)
                    last.then_inc(q["ixm"], 1)

                def hidden(s, buf, j, hb, q):
                    for k in range(KT):
                        for f in range(2):
                            last = pe.matmul(bank[hb][64 * f:64 * f + 64, 0:2 * P].rearrange("p (w j) -> p w j", w=2), xg[buf][:, k, j, :],
                                             w13[s][:, k, :, f * P:(f + 1) * P], start=k == 0, stop=k == KT - 1)
                    last.then_inc(q["h"], 1)

                def hidden_T(ab, q):
                    pe.transpose(bank[5][:, ab * P:(ab + 1) * P], hh[ab][:], ident[:]).then_inc(q["t"], 1)

                def rows_out(s, ab, q):
                    for f in range(2):
                        for n in range(2):
                            last = pe.matmul(bank[6 + ab][64 * n:64 * n + 64, :], hT[ab][:, 64 * f:64 * f + 64],
                                             w2s[s][:, f, n * 512:(n + 1) * 512], start=f == 0, stop=f == 1)
                    last.then_inc(q["y"], 1)

                q = dict(g=g_mm, ixm=ix_mm, h=h_mm, t=t_mm, y=y_mm)
                G = l * (PAIRS + 1)
                F = l * (PAIRS + 2)
                Q = l * (NE // 4 + 1)
                E = l * NE
                pe.wait_ge(sel_ok, Q + 1)
                pe.wait_ge(xlo_ok, NC * (l + 1))
                gather(0, q)
                pe.wait_ge(xg_a, F + 1)
                pe.wait_ge(xg_d, F + 1)
                gather(1, q)
                pe.wait_ge(cnt_ok, l + 1)
                numbers(0, q)
                with pe.Fori(0, NE // 8) as i:
                    for u_ in range(4):
                        p, buf = u_ % 2, u_ // 2
                        sl = [(2 * p + ab + 2) % 4 for ab in range(2)]
                        pe.wait_ge(xg_a, i * 4 + (F + u_ + 2))
                        pe.wait_ge(xg_d, i * 4 + (F + u_ + 2))
                        for ab in range(2):
                            pe.wait_ge(w13_in[sl[ab]], i * 64 + 32 * (8 * l + buf + 1))
                            pe.wait_ge(hh_ok, i * 8 + (E + 2 * u_ + ab + 1))
                            hidden(sl[ab], buf, 2 * p + ab, 3 + ab, q)
                        pe.wait_ge(hh_ok, i * 8 + (E + 2 * u_ + 3))
                        hidden_T(0, q)
                        pe.wait_ge(sel_ok, i * 2 + (Q + buf + 2))
                        gather(p, q)
                        if p == 1:
                            pe.wait_ge(ix_ok, i * 4 + (G + u_ + 1))
                            numbers(8 * i + (4 * buf + 4), q)
                        pe.wait_ge(hh_ok, i * 8 + (E + 2 * u_ + 4))
                        pe.wait_ge(ht_ok, i * 8 + (E + 2 * u_ + 1))
                        hidden_T(1, q)
                        for ab in range(2):
                            pe.wait_ge(ht_ok, i * 8 + (E + 2 * u_ + ab + 1))
                            pe.wait_ge(w2_in[sl[ab]], i * 32 + 16 * (8 * l + buf + 1))
                            pe.wait_ge(ys_ok, i * 8 + (E + 2 * u_ + ab + 1))
                            rows_out(sl[ab], ab, q)
                pe.wait_ge(ys_ok, NE * (l + 1) + 2)
                pe.wait_ge(xg_a, (l + 1) * (PAIRS + 2))
                pe.wait_ge(xg_d, (l + 1) * (PAIRS + 2))
                pe.wait_ge(ix_ok, (l + 1) * (PAIRS + 1))
                most = pe.value_load(cnt_i[0:1, l:l + 1], min_val=0, max_val=T)
                o = ov[l]
                with pe.If(most > CAP), pe.Fori(0, ROUNDS - 1) as r:
                    with pe.If(most > CAP * r + CAP):
                        with pe.Fori(0, NE) as e:
                            n = r * NE + e
                            pe.wait_ge(o["sel"], n + 1)
                            for half in range(2):
                                gather(half, o)
                                pe.wait_ge(o["xg"], n * 2 + (half + 1))
                            numbers(e, o)
                            pe.wait_ge(o["w"], n * 48 + 48)
                            hidden(3, 0, 0, 3, o)
                            pe.wait_ge(o["hid"], n * 2 + 1)
                            hidden_T(0, o)
                            pe.wait_ge(o["hid"], n * 2 + 2)
                            rows_out(3, 0, o)
            mixture(0)

            norm_transposes(2)
            pe.wait_ge(xt_a, NC * 3)
            pe.wait_ge(xt_d, NC * 3)
            with pe.Fori(0, KT // 2) as i:
                for s in range(2):
                    pe.wait_ge(w_lo, i * 2 + (16 + s + 1))
                    for half in range(2):
                        pe.wait_ge(cg_ok, i * 4 + (2 * s + half + 1))
                        for a in range(3):
                            for k in range(KT):
                                for j, (w, x) in enumerate(((wc_hi, xc_hi), (wc_hi, xc_lo), (wc_lo, xc_hi))):
                                    last = pe.matmul(bank[3 * half + a][:, 0:HALF], w[s][:, k, a, :],
                                                     x[:, k, half * HALF:(half + 1) * HALF],
                                                     start=k == 0 and j == 0, stop=k == KT - 1 and j == 2)
                        last.then_inc(c_mm, 1)
            pe.wait_ge(cg_ok, 2 * KT + 2)
            def z_c(part, k):
                return (g_hi, g_lo)[part][:, k, :]
            z_c.arrived = lambda c: pe.wait_ge(z_lo, 1 + c + 1)

            def w_c(part, k, s):
                if part == 1:
                    return woc_lo[s][:, k, :]
                return woc0_hi[k // 4][:, k % 4, :] if s == 0 else woc1_hi[:, k, :]
            project_out(1, z_c, w_c, 16 + KT + 1)
            mixture(1)

        @block.scalar
        def _(act):
            act.nop().then_inc(ys_ok, 2)

            def squares(n):
                for c in range(NC):
                    if n == 0:
                        act.wait_ge(x_in, 16 * NC)
                        act.wait_ge(const_ok, 1)
                    else:
                        act.wait_ge(h_ok, NC * (n - 1) + c + 1)
                    act.activation(junk[:], H[:, c, :], ACT.Square, accum_out=ssq[:, c:c + 1]).then_inc(sq_done, 1)
                    act.wait_ge(ms_ok, NC * n + c + 1)
                    act.activation(rms[:, c:c + 1], rms[:, c:c + 1], ACT.Sqrt).then_inc(rt_ok, 1)

            def xt_low(n):
                for c in range(NC):
                    act.wait_ge(xt_mm, NXT * n + 2 * c + 1)
                    act.activation(XT[:, 0:4, c * P:c * P + ROWS[c]],
                                   bank[6][:, :].rearrange("p (k t) -> p k t", k=4)[:, :, 0:ROWS[c]], ACT.Copy).then_inc(xt_a, 1)
            def group_hi(n):
                if n < 14:
                    act.wait_ge(wab_in[n % 3], 16 * (n // 3 + 1))
                    act.activation(wab_hi[n % 3][:], wab[n % 3][:], ACT.Copy).then_inc(w_hi, 1)

            def mixer_in_hi(n):
                for c in range(NC):
                    low = 6 - 2 * (c % 2)
                    for half in range(2):
                        act.wait_ge(xt_mm, NXT * n + 2 * c + half + 1)
                        last = act.activation(xc_hi[:, 4 * half:4 * half + 4, c * P:c * P + ROWS[c]],
                                              bank[low + half][:, :].rearrange("p (k t) -> p k t", k=4)[:, :, 0:ROWS[c]], ACT.Copy)
                    last.then_inc(xt_a, 1)
            squares(0)
            group_hi(0)
            mixer_in_hi(0)
            act.wait_ge(lbm_ok, 1)
            act.activation(lbe[:], lbe[:], ACT.Exp).then_inc(lbe_ok, 1)
            for n in range(6):
                if n == 2:
                    act.wait_ge(f_ok, 5)
                    act.activation(fT[:], fT[:], ACT.Ln).then_inc(ln_ok, 1)
                if n == 3:
                    act.wait_ge(cum_ok, 4)
                    act.activation(fT[:], koutT[:], ACT.Exp).then_inc(exp_ok, 1)
                    act.activation(koutT[:], koutT[:], ACT.Exp, scale=-1.0).then_inc(exp_ok, 1)
                dst, fn = ((fT, ACT.Sigmoid), (qdecT, ACT.Silu), (gateT, ACT.Silu))[n // 2]
                group_hi(n + 1)
                for b in range(4):
                    m, half = 2 * (n % 2) + b // 2, b % 2
                    act.wait_ge(z_mm, 4 * n + b + 1)
                    act.activation(dst[:, m, half * HALF:(half + 1) * HALF], bank[b][:, 0:HALF], fn).then_inc(z_free[b], 1)
            group_hi(7)
            group_hi(8)
            for i in range(4 * NC):
                un = 34 + i
                n = ROWS[i % NC]
                if i % NC == 0:
                    group_hi(9 + i // NC)
                act.wait_ge(z_mm, un + 1)
                if i >= 2:
                    act.wait_ge(qms_ok, i - 1)
                act.activation(qsq[i % 2][0:n, :], bank[un % 4][0:n, 0:HG], ACT.Square).then_inc(qsq_ok, 1)
                act.wait_ge(qms_ok, i + 1)
                sl = slice((i % 2) * NH, (i % 2) * NH + NH // 2)
                act.activation(hms[0:n, sl], hms[0:n, sl], ACT.Sqrt).then_inc(qrt_ok, 1)
            for i in range(2 * NC):
                un, (hh_, c) = 54 + i, divmod(i, NC)
                if c == 0:
                    group_hi(13 + hh_)
                act.wait_ge(z_mm, un + 1)
                act.activation(va[0:ROWS[c], c, hh_ * HG:(hh_ + 1) * HG], bank[un % 4][0:ROWS[c], 0:HG], ACT.Copy).then_inc(z_free[un % 4], 1)
                act.wait_ge(z_free[un % 4], un // 4 + 1)
                act.nop().then_inc(v_ok, 1)
            def kout_rows(c):
                act.wait_ge(ko_mm, c + 1)
                if c == 0:
                    act.wait_ge(pool_c, zeroed[0])
                else:
                    act.wait_ge(u_mm, c)
                for r in range(ROWS[c] // 32):
                    last = act.activation(kout[32 * r:32 * r + 32, r, :], bank[1][32 * r:32 * r + 32, :], ACT.Copy)
                last.then_inc(ko_ok, 1)
            kout_rows(0)
            kout_rows(1)
            for c in range(NC):
                n = ROWS[c]
                if c + 2 < NC:
                    kout_rows(c + 2)
                act.wait_ge(os_ok, c + 1)
                act.activation(osq[0:n, :], ot[0:n, :], ACT.Square).then_inc(osq_ok, 1)
                act.wait_ge(hms_ok, c + 1)
                act.activation(hms[0:n, 0:NH], hss[0:n, 0:NH], ACT.Sqrt, bias=epsc[0:n, 0:1], scale=1.0 / HD).then_inc(orms_ok, 1)
            NU = NC * NH

            def prob_copy(i):
                if i % 2 == 0:
                    c = i // NH
                    act.wait_ge(pT_mm, i + 1)
                    if i >= 2:
                        act.wait_ge(pv_mm, i - 1)
                    if c < 4:
                        act.activation(prT[0][:, 0:c + 1, :], bank[2][:, 0:P * (c + 1)].rearrange("p (k t) -> p k t", t=P), ACT.Copy).then_inc(pT_a, 1)
                    else:
                        tie(act.activation(prT[0][:, 0, 0:DEC], bank[2][:, 0:DEC], ACT.Copy))
                        act.activation(prT[0][0:DEC, 1, 0:DEC], bank[2][0:DEC, P:P + DEC], ACT.Copy).then_inc(pT_a, 1)
            tie = Chain(act, ach)
            for i in range(NU + 6):
                if i < NU:
                    c, n = i // NH, ROWS[i // NH]
                    w = P * (c + 1) if c < 4 else PAST + DEC
                    act.wait_ge(s_ok, i + 1)
                    if i >= 2:
                        act.wait_ge(pT_mm, i - 1)
                    act.activation(pr[i % 2][0:n, 0:w], sneg[i % 2][0:n, 0:w], ACT.Exp, bias=nmaxs[0:n, i:i + 1], scale=-1.0,
                                   accum_out=rsum[0:n, i:i + 1]).then_inc(p_ok, 1)
                if 1 <= i <= NU:
                    prob_copy(i - 1)
                if i == 3:
                    act.activation(zB_hi[:], zB[:], ACT.Copy).then_inc(z_hi, 1)
                if i == 2 * NH + 2:
                    act.wait_ge(kc_mm, 1)
                    act.activation(kcT[:], bank[7][:, :].rearrange("p (m t) -> p m t", m=4), ACT.Copy).then_inc(kc_ok, 1)
                if i >= 11 and (i - 11) % NH == 0:
                    c = (i - 11) // NH
                    act.wait_ge(rb_mm, c + 1)
                    if c > 0:
                        act.wait_ge(zn_ok, c)
                    else:
                        act.wait_ge(z_lo, 1)
                    act.activation(rb[:, :, 0:ROWS[c]], bank[6][:, :].rearrange("p (m t) -> p m t", m=4)[:, :, 0:ROWS[c]],
                                   ACT.Copy).then_inc(rb_ok, 1)
                if i >= 13 and (i - 13) % NH == 0:
                    c = (i - 13) // NH
                    act.wait_ge(zn_ok, c + 1)
                    act.activation(zA_hi[:, :, c * P:c * P + ROWS[c]], zA[:, :, 0:ROWS[c]], ACT.Copy).then_inc(zAh_ok, 1)

            def mixture(l):
                squares(2 * l + 1)
                xt_low(2 * l + 1)
                act.wait_ge(lg_mm, l + 1)
                for c in range(NC):
                    act.activation(x_hi[:, c, :], XN[:, c, :], ACT.Copy).then_inc(xhi_ok, 1)
                act.wait_ge(ge_ok, l + 1)
                act.activation(rt[3][:, :, 0:NG], rt[3][:, :, 0:NG], ACT.Exp).then_inc(gx_ok, 1)
                act.wait_ge(e2_ok, l + 1)
                act.activation(c1[5][:], c1[5][:], ACT.Exp).then_inc(ex_ok, 1)
                E = l * NE

                def xg_low(half, buf):
                    return act.activation(xg[buf][:, 4 * half:4 * half + 2, :, :].rearrange("p k a s -> p (k a s)"), bank[0][:, :], ACT.Copy)
                F = l * (PAIRS + 2)
                for half in range(2):
                    act.wait_ge(g_mm, F + half + 1)
                    xg_low(half, 0).then_inc(xg_a, 1)
                with act.Fori(0, NE // 8) as i:
                    for u_ in range(4):
                        p, buf = u_ % 2, u_ // 2
                        for ab in range(2):
                            act.wait_ge(h_mm, i * 8 + (E + 2 * u_ + ab + 1))
                            act.activation(sg[ab][:], bank[3 + ab][:, 0:P], ACT.Silu).then_inc(sg_ok, 1)
                        act.wait_ge(g_mm, i * 4 + (F + u_ + 3))
                        xg_low(p, 1 - buf).then_inc(xg_a, 1)
                        for ab in range(2):
                            act.wait_ge(y_mm, i * 8 + (E + 2 * u_ + ab + 1))
                            act.wait_ge(ys_free, i * 8 + (E + 2 * u_ + ab + 1))
                            act.activation(ys[2 * p + ab][:], bank[6 + ab][:, :], ACT.Copy).then_inc(ys_ok, 1)
                act.wait_ge(cnt_ok, l + 1)
                most = act.value_load(cnt_i[0:1, l:l + 1], min_val=0, max_val=T)
                o = ov[l]
                with act.If(most > CAP), act.Fori(0, ROUNDS - 1) as r:
                    with act.If(most > CAP * r + CAP):
                        with act.Fori(0, NE) as e:
                            n = r * NE + e
                            act.wait_ge(o["mm"], n * 6 + 4)
                            act.activation(sg[0][:], bank[3][:, 0:P], ACT.Silu).then_inc(o["act"], 1)
                            act.wait_ge(o["mm"], n * 6 + 6)
                            act.wait_ge(o["free"], n + 1)
                            act.activation(ys[0][:], bank[6][:, :], ACT.Copy).then_inc(o["act"], 1)
            mixture(0)

            for s in range(2):
                act.wait_ge(wc_in[s], 48)
                act.activation(wc_hi[s][:], wc[s][:], ACT.Copy).then_inc(w_hi, 1)
            squares(2)
            mixer_in_hi(2)

            def conv_copies(m, half):
                act.wait_ge(c_mm, m * 2 + (half + 1))
                act.activation(hc[half][:], bank[3 * half + 2][:, 0:HALF], ACT.Copy).then_inc(hc_ok, 1)
            with act.Fori(0, KT // 2 - 1) as i:
                for s in range(2):
                    for half in range(2):
                        conv_copies(2 * i + s, half)
                    act.wait_ge(wc_in[s], i * 48 + 96)
                    act.activation(wc_hi[s][:], wc[s][:], ACT.Copy).then_inc(w_hi, 1)
            for s in range(2):
                for half in range(2):
                    conv_copies(KT - 2 + s, half)
            act.wait_ge(c_mm, 2 * KT)
            act.wait_ge(cg_ok, 2 * KT + 2)
            for c in range(NC):
                t = slice(c * P, c * P + ROWS[c])
                act.activation(g_hi[:, :, t], gT[:, :, t], ACT.Copy).then_inc(z_hi, 1)
            mixture(1)

        @block.vector
        def _(dve):
            tie = Chain(dve, dch)
            dve.nop().then_inc(hh_ok, 2)
            dve.nop().then_inc(cg_ok, 2)

            def norm(n, c):
                gain = gmix if n % 2 == 0 else gffn
                dve.wait_ge(sq_done, NC * n + c + 1)
                dve.tensor_scalar(rms[:, c:c + 1], ssq[:, c:c + 1], 1.0 / D, EPS, ALU.mult, ALU.add).then_inc(ms_ok, 1)
                dve.wait_ge(rt_ok, NC * n + c + 1)
                tie(dve.reciprocal(rstd[:, c:c + 1], rms[:, c:c + 1]))
                if c == 0:
                    dve.wait_ge(gmix_in if n % 2 == 0 else gffn_in, 16 * (n // 2 + 1))
                dve.scalar_tensor_tensor(XN[:, c, :], H[:, c, :], rstd[:, c:c + 1], gain[:], ALU.mult, ALU.mult).then_inc(xn_ok, 1)

            def xt_high(n):
                for c in range(NC):
                    dve.wait_ge(xt_mm, NXT * n + 2 * c + 2)
                    dve.tensor_copy(XT[:, 4:8, c * P:c * P + ROWS[c]],
                                    bank[7][:, :].rearrange("p (k t) -> p k t", k=4)[:, :, 0:ROWS[c]]).then_inc(xt_d, 1)

            def mixer_in_lo(n, lo):
                for c in range(NC):
                    low, t = 6 - 2 * (c % 2), slice(c * P, c * P + ROWS[c])
                    dve.wait_ge(xt_a, NC * n + c + 1)
                    for half in range(2):
                        last = dve.tensor_tensor(lo[:, 4 * half:4 * half + 4, t],
                                                 bank[low + half][:, :].rearrange("p (k t) -> p k t", k=4)[:, :, 0:ROWS[c]],
                                                 xc_hi[:, 4 * half:4 * half + 4, t].bitcast(F32), ALU.subtract)
                    last.then_inc(xt_d, 1)
            for c in range(NC):
                norm(0, c)
            mixer_in_lo(0, xp_lo)
            dve.wait_ge(tab_in, 16 * 5)
            tie(dve.tensor_tensor(lb[:], lbl[:, 0:4], lbl[:, 4:8], ALU.max))
            dve.tensor_tensor(lbe[:].rearrange("p (r m) -> p r m", r=2), lbl[:].rearrange("p (r m) -> p r m", r=2),
                              bc(lb[:].unsqueeze(1), [P, 2, 4]), ALU.subtract).then_inc(lbm_ok, 1)
            dve.wait_ge(lbe_ok, 1)
            tie(dve.tensor_tensor(lbs[:], lbe[:, 0:4], lbe[:, 4:8], ALU.add))
            tie(dve.reciprocal(lbs[:], lbs[:]))
            tie(dve.tensor_tensor(lb[:], lbe[:, 0:4], lbs[:], ALU.mult))
            tie(dve.tensor_scalar(lbs[:], lb[:], -1.0, 1.0, ALU.mult, ALU.add))
            tie(dve.tensor_scalar(qgain[:], qgain[:], HD ** -0.5, None, ALU.mult))
            dve.wait_ge(const_ok, 1)
            tie(dve.tensor_reduce(even[:], blk_sel[:], AX.X, ALU.add))
            tie(dve.tensor_scalar(odd[:], even[:], -1.0, 1.0, ALU.mult, ALU.add))
            for b in range(4):
                dve.wait_ge(z_free[b], 2)
            for m in range(4):
                dve.tensor_scalar(fT[:, m, :], fT[:, m, :], lbs[:, m:m + 1], lb[:, m:m + 1], ALU.mult, ALU.add).then_inc(f_ok, 1)
            dve.wait_ge(f_ok, 4)
            dve.tensor_scalar(kinT[:], fT[:], -1.0, 1.0, ALU.mult, ALU.add).then_inc(f_ok, 1)
            dve.wait_ge(ln_ok, 1)
            for m in range(4):
                dve.tensor_tensor_scan(koutT[:, m, :], reset[:], fT[:, m, :], 0.0, ALU.mult, ALU.add).then_inc(cum_ok, 1)
            dve.wait_ge(exp_ok, 2)
            dve.wait_ge(f_ok, 5)
            tie(dve.tensor_copy(dec[:].rearrange("p (m b) -> p m b", m=4), fT[:, :, BLK - 1::BLK]))
            dve.tensor_tensor(kinT[:], kinT[:], koutT[:], ALU.mult).then_inc(hg_ok, 1)
            for b in range(4):
                dve.wait_ge(z_free[b], 4)
            dve.tensor_tensor(qdecT[:], qdecT[:], fT[:], ALU.mult).then_inc(hg_ok, 1)
            dve.wait_ge(hg_ok, 2)
            dve.tensor_tensor(koutT[:].rearrange("p m (b t) -> p (m b) t", t=BLK), kinT[:].rearrange("p m (b t) -> p (m b) t", t=BLK),
                              bc(dec[:].unsqueeze(2), [P, 4 * NBLK, BLK]), ALU.mult).then_inc(hg_ok, 1)
            for i in range(2 * NC):
                un, (hh_, c) = 24 + i, divmod(i, NC)
                dve.wait_ge(z_mm, un + 1)
                dve.tensor_copy(vb[0:ROWS[c], c, hh_ * HG:(hh_ + 1) * HG], bank[un % 4][0:ROWS[c], 0:HG]).then_inc(z_free[un % 4], 1)
            for b in range(4):
                dve.wait_ge(z_free[b], 6)
            for m in range(4):
                tie(dve.tensor_scalar(gateT[:, m, :], gateT[:, m, :], onorm[:, m:m + 1], None, ALU.mult))
            for i in range(4 * NC):
                un, c, n = 34 + i, i % NC, ROWS[i % NC]
                dst, gain = (q_tok, qgain) if i < 2 * NC else (k_tok, kgain)
                sl = slice((i % 2) * NH, (i % 2) * NH + NH // 2)
                four = [n, NH // 2, HD]
                lo = (i // NC % 2) * HG
                d = dst[0:n, c, lo:lo + HG].rearrange("p (h d) -> p h d", d=HD)
                dve.wait_ge(qsq_ok, i + 1)
                tie(dve.tensor_reduce(hss[0:n, sl], qsq[i % 2][0:n, :].rearrange("p (h d) -> p h d", d=HD), AX.X, ALU.add))
                dve.tensor_scalar(hms[0:n, sl], hss[0:n, sl], 1.0 / HD, EPS, ALU.mult, ALU.add).then_inc(qms_ok, 1)
                dve.wait_ge(qrt_ok, i + 1)
                tie(dve.reciprocal(hrs[0:n, sl], hms[0:n, sl]))
                dve.tensor_tensor(d, bank[un % 4][0:n, 0:HG].rearrange("p (h d) -> p h d", d=HD),
                                  bc(hrs[0:n, sl].unsqueeze(2), four), ALU.mult).then_inc(z_free[un % 4], 1)
                dve.wait_ge(z_free[un % 4], un // 4 + 1)
                dve.tensor_tensor(d, d, bc(gain[0:n, :].unsqueeze(1), four), ALU.mult).then_inc(qk_ok, 1)
            dve.wait_ge(z_mm, UNIT_END[-1])
            tie(dve.tensor_copy(qdecs[1][64:128, :, :], qdecT[64:128, :, :]))
            dve.memset(qdecT[64:128, :, :], 0.0).then_inc(qd_ok, 1)
            tie(dve.memset(st[0][:, 0, :, :], 0.0))

            def hgrn_prepare(c):
                n = ROWS[c]
                if c >= 2:
                    dve.wait_ge(o_mm, c - 1)
                dve.wait_ge(a_mm, c + 1)
                for par in range(2):
                    dve.tensor_tensor(am[c % 2][0:n, par, :, 0:n], bank[1 + par][0:n, :].rearrange("p (m t) -> p m t", m=4)[:, :, 0:n],
                                      bc(blk_mask[0:n, 0:n].unsqueeze(1), [n, 4, n]), ALU.mult).then_inc(a_ok, 1)

            def hgrn_chain(c):
                n = ROWS[c]
                dve.wait_ge(u_mm, c + 1)
                if c == 4:
                    dve.wait_ge(st_in, 16)
                for b in range(n // BLK):
                    t = dec[:].rearrange("p (m b) -> p m b", m=4)[:, :, 8 * c + b:8 * c + b + 1]
                    upd = bank[3 + b // 2][:, :].rearrange("p (m i v) -> p m i v", m=4, i=2)[:, :, b % 2, :]
                    tie(dve.tensor_tensor(dS[:], st[c % 2][:, b, :, :], bc(t, [P, 4, HD]), ALU.mult))
                    tie(dve.tensor_tensor(st[c % 2][:, b + 1, :, :], upd, dS[:], ALU.add))
                if c < 3:
                    if c >= 1:
                        dve.wait_ge(o_mm, c)
                    tie(dve.tensor_copy(st[(c + 1) % 2][:, 0, :, :], st[c % 2][:, 8, :, :]))
                dve.nop().then_inc(st_ok, 1)

            def hgrn_select(c):
                n = ROWS[c]
                dve.wait_ge(o_mm, c + 1)
                o4 = ot[0:n, :].rearrange("p (m q v) -> p m q v", m=4, q=2)
                for par, b in enumerate((bank[0], bank[7])):
                    both = b[0:n, :].rearrange("p (m i v) -> p m i v", m=4, i=2)
                    tie(dve.tensor_scalar(o4[:, :, par, :], both[:, :, 0, :], even[0:n, :], None, ALU.mult))
                    tie(dve.scalar_tensor_tensor(o4[:, :, par, :], both[:, :, 1, :], odd[0:n, :], o4[:, :, par, :], ALU.mult, ALU.add))
                dve.nop().then_inc(os_ok, 1)

            def hgrn_norm(c):
                n = ROWS[c]
                o3 = ot[0:n, :].rearrange("p (h v) -> p h v", h=NH)
                dve.wait_ge(osq_ok, c + 1)
                dve.tensor_reduce(hss[0:n, 0:NH], osq[0:n, :].rearrange("p (h v) -> p h v", h=NH), AX.X, ALU.add).then_inc(hms_ok, 1)
                dve.wait_ge(orms_ok, c + 1)
                tie(dve.reciprocal(hrs[0:n, 0:NH], hms[0:n, 0:NH]))
                dve.tensor_tensor(o3, o3, bc(hrs[0:n, 0:NH].unsqueeze(2), [n, NH, HD]), ALU.mult).then_inc(zt_ok, 1)
                dve.wait_ge(zt_mm, c + 1)
                dve.tensor_tensor(zB[:, :, c * P:c * P + n], bank[7][:, :].rearrange("p (m t) -> p m t", m=4)[:, :, 0:n],
                                  gateT[:, :, c * P:c * P + n], ALU.mult).then_inc(zB_ok, 1)
            hgrn_prepare(0)
            hgrn_chain(0)
            hgrn_prepare(1)
            for c in range(NC):
                if c + 1 < NC:
                    hgrn_chain(c + 1)
                hgrn_select(c)
                if c + 2 < NC:
                    hgrn_prepare(c + 2)
                hgrn_norm(c)

            for i in range(2 * NC):
                c = i // 2
                t = slice(c * P, c * P + ROWS[c])
                src = bank[4 + i % 2][:, :].rearrange("p (m t) -> p m t", m=4)[:, :, 0:ROWS[c]]
                dve.wait_ge(qkT_mm, i + 1)
                if i % 2 == 0:
                    dve.tensor_copy(qTs[0][0:64, :, t], src[0:64])
                    dve.tensor_copy(qTs[1][64:128, :, t], src[64:128]).then_inc(qkT_ok, 1)
                else:
                    dve.tensor_copy(kT[:, :, t], src).then_inc(qkT_ok, 1)
            dve.wait_ge(bias_in, 16 * 4)
            tie(dve.memset(bias[0:CH, :, 512 - CH:512], MASKED))
            NU = NC * NH

            def score_max(i):
                c, h = divmod(i, NH)
                n = ROWS[c]
                w, b0 = (P * (c + 1), 384 - P * c) if c < 4 else (PAST + DEC, 256)
                dve.wait_ge(s_mm, i + 1)
                if i >= 2:
                    dve.wait_ge(p_ok, i - 1)
                dve.tensor_tensor_reduce(out=sneg[i % 2][0:n, 0:w], in0=bank[i % 2][0:n, 0:w], in1=bias[0:n, h, b0:b0 + w],
                                         scale=-1.0, scalar=-MASKED, op0=ALU.add, op1=ALU.min,
                                         accum_out=nmaxs[0:n, i:i + 1]).then_inc(s_ok, 1)

            def prob_copy(i):
                if i % 2 == 1:
                    c = i // NH
                    dve.wait_ge(pT_mm, i + 1)
                    if i >= 3:
                        dve.wait_ge(pv_mm, i - 1)
                    if c < 4:
                        dve.tensor_copy(prT[1][:, 0:c + 1, :], bank[3][:, 0:P * (c + 1)].rearrange("p (k t) -> p k t", t=P)).then_inc(pT_d, 1)
                    else:
                        tie(dve.tensor_copy(prT[1][:, 0, 0:DEC], bank[3][:, 0:DEC]))
                        dve.tensor_copy(prT[1][0:DEC, 1, 0:DEC], bank[3][0:DEC, P:P + DEC]).then_inc(pT_d, 1)

            def sums_diagonal(c):
                n = ROWS[c]
                sl = slice((c % 2) * NH, (c % 2 + 1) * NH)
                dve.wait_ge(p_ok, NH * (c + 1))
                tie(dve.reciprocal(rinv[0:n, sl], rsum[0:n, c * NH:(c + 1) * NH]))
                if c > 0:
                    dve.wait_ge(rb_mm, c)
                dve.tensor_tensor(dg[0:n, :, :, 0:n], bc(ident[0:n, 0:n].unsqueeze(1).unsqueeze(1), [n, 2, 4, n]),
                                  bc(rinv[0:n, sl].rearrange("p (m q) -> p q m", q=2).unsqueeze(3), [n, 2, 4, n]), ALU.mult).then_inc(dg_ok, 1)

            def heads_norm(c):
                n = ROWS[c]
                dve.wait_ge(pv_mm, NH * (c + 1))
                dve.wait_ge(rb_ok, c + 1)
                dve.tensor_tensor(zA[:, :, 0:n], bank[4 + c % 2][:, :].rearrange("p (m t) -> p m t", m=4)[:, :, 0:n],
                                  rb[:, :, 0:n], ALU.mult).then_inc(zn_ok, 1)

            def heads_lo(c):
                n = ROWS[c]
                dve.wait_ge(zAh_ok, c + 1)
                dve.tensor_tensor(zA_lo[:, :, c * P:c * P + n], zA[:, :, 0:n],
                                  zA_hi[:, :, c * P:c * P + n].bitcast(F32), ALU.subtract).then_inc(zA_ok, 1)
            for i in range(NU + 7):
                if i < NU:
                    score_max(i)
                if 1 <= i <= NU:
                    prob_copy(i - 1)
                if i >= 9 and (i - 9) % NH == 0:
                    sums_diagonal((i - 9) // NH)
                if i == 6:
                    dve.wait_ge(z_hi, 1)
                    dve.tensor_tensor(zB_lo[:], zB[:], zB_hi[:].bitcast(F32), ALU.subtract).then_inc(z_lo, 1)
                if i >= 12 and (i - 12) % NH == 0:
                    heads_norm((i - 12) // NH)
                if i >= 14 and (i - 14) % NH == 0:
                    heads_lo((i - 14) // NH)

            def residual(n):
                for i in range(2 * NC):
                    s, c = divmod(i, NC)
                    dve.wait_ge(op_mm, 2 * NC * n + i + 1)
                    h = H[0:ROWS[c], c, s * 512:(s + 1) * 512]
                    dve.tensor_tensor(h, bank[i % 4][0:ROWS[c], :], h, ALU.add).then_inc(op_add, 1)
                    if s == 1:
                        dve.wait_ge(op_add, 2 * NC * n + i + 1)
                        dve.nop().then_inc(h_ok, 1)
                        if c > 0:
                            norm(2 * n + 1, c - 1)
                norm(2 * n + 1, NC - 1)
            residual(0)

            def route(l):
                lgg, lge = lg[:, :, 0:NG], lg[:, :, NG:NR].rearrange("p c (g j) -> p c g j", g=NG)
                tie(dve.memset(lg[:], 0.0))
                tie(dve.memset(rk[:, :, NE:RKW], -1.0))
                tie(dve.tensor_scalar(dv[:, :, NE:RKW], rk[:, :, NE:RKW], 1.0, None, ALU.add))
                dve.wait_ge(lg_mm, l + 1)
                dve.wait_ge(wr_in, 64 * (l + 1))
                z = bank[0][:, 0:NC * NR].rearrange("p (c n) -> p c n", c=NC)
                tie(dve.tensor_tensor(lg[:, 0:4, :], z[:, 0:4, :], bc(biasr[:].unsqueeze(1), [P, 4, NR]), ALU.add))
                dve.tensor_tensor(lg[0:DEC, 4, :], z[0:DEC, 4, :], biasr[0:DEC, :], ALU.add).then_inc(lg_ok, 1)
                dve.wait_ge(lg_ok, l + 1)

                def first_max(v, w, rev, eq, key, hot, top):
                    tie(dve.tensor_reduce(top, v, AX.X, ALU.max))
                    tie(dve.tensor_tensor(eq, v, bc(top.unsqueeze(2), [P, NC, w]), ALU.is_equal))
                    tie(dve.tensor_tensor(key, eq, bc(rev.unsqueeze(1), [P, NC, w]), ALU.mult))
                    tie(dve.tensor_reduce(c1[1][:], key, AX.X, ALU.max))
                    tie(dve.tensor_tensor(hot, key, bc(c1[1][:].unsqueeze(2), [P, NC, w]), ALU.is_equal))
                hot_g, hot1, hot2 = rt[2][:, :, 0:4], rt[2][:, :, 4:12], rt[2][:, :, 12:20]
                first_max(lgg, NG, rev4[:], rt[0][:, :, 0:4], rt[1][:, :, 0:4], hot_g, c1[0][:])
                dve.tensor_tensor(rt[3][:, :, 0:NG], lgg, bc(c1[0][:].unsqueeze(2), [P, NC, NG]), ALU.subtract).then_inc(ge_ok, 1)
                four = [P, NC, NG, EPG]
                r4 = [t[:].rearrange("p c (g j) -> p c g j", g=NG) for t in rt]
                tie(dve.tensor_tensor(r4[0], lge, bc(hot_g.unsqueeze(3), four), ALU.mult))
                sel8 = rt[1][:, :, 8:16]
                tie(dve.tensor_reduce(sel8, rt[0][:].rearrange("p c (g j) -> p c j g", g=NG), AX.X, ALU.add))
                first_max(sel8, EPG, rev8[:], rt[1][:, :, 16:24], rt[1][:, :, 24:32], hot1, c1[3][:])
                sel7 = rt[4][:, :, 0:8]
                tie(dve.scalar_tensor_tensor(sel7, hot1, -3e38, sel8, ALU.mult, ALU.add))
                first_max(sel7, EPG, rev8[:], rt[1][:, :, 16:24], rt[1][:, :, 24:32], hot2, c1[4][:])
                dve.tensor_tensor(c1[5][:], c1[4][:], c1[3][:], ALU.subtract).then_inc(e2_ok, 1)
                tie(dve.tensor_tensor(hot_g, hot_g, bc(frame_ok[:].unsqueeze(2), [P, NC, NG]), ALU.mult))
                for hot, m in ((hot1, m1), (hot2, m2)):
                    tie(dve.tensor_tensor(m[:].rearrange("p c (g j) -> p c g j", g=NG), bc(hot_g.unsqueeze(3), four),
                                          bc(hot.unsqueeze(2), four), ALU.mult))
                dve.tensor_tensor(rt[0][:], m1[:], m2[:], ALU.add).then_inc(msk_ok, 1)
                dve.wait_ge(gx_ok, l + 1)
                tie(dve.tensor_reduce(c1[2][:], rt[3][:, :, 0:NG], AX.X, ALU.add))
                tie(dve.reciprocal(c1[2][:], c1[2][:]))
                dve.wait_ge(ex_ok, l + 1)
                tie(dve.tensor_scalar(c1[6][:], c1[5][:], 1.0, None, ALU.add))
                tie(dve.reciprocal(c1[6][:], c1[6][:]))
                tie(dve.tensor_tensor(c1[2][:], c1[2][:], c1[6][:], ALU.mult))
                tie(dve.tensor_copy(gate[0][:], c1[2][:]))
                tie(dve.tensor_tensor(gate[1][:], c1[2][:], c1[5][:], ALU.mult))
                tie(dve.tensor_scalar(c1[3][:], frame_no[:], -float(DROP), None, ALU.add))
                tie(dve.tensor_scalar(c1[4][:], frame_no[:], float(T - DROP), None, ALU.add))
                tie(dve.tensor_tensor(rt[1][:], m1[:], bc(c1[3][:].unsqueeze(2), [P, NC, NE]), ALU.mult))
                tie(dve.tensor_tensor(rt[4][:], m2[:], bc(c1[4][:].unsqueeze(2), [P, NC, NE]), ALU.mult))
                tie(dve.tensor_tensor(dv[:, :, 0:NE], rt[1][:], rt[4][:], ALU.add))
                dve.wait_ge(rk_mm, l + 1)
                dve.wait_ge(msk_ok, l + 1)
                tie(dve.scalar_tensor_tensor(rt[3][:], bank[1][:, 0:NC * NE].rearrange("p (c n) -> p c n", c=NC), 1.0, rt[0][:], ALU.add, ALU.mult))
                tie(dve.tensor_reduce(c1[7][:, 0:1], rt[3][:], AX.XY, ALU.max))
                dve.tensor_scalar(rk[:, :, 0:NE], rt[3][:], -1.0, None, ALU.add).then_inc(rk_ok, 1)
                dve.wait_ge(rk_ok, l + 1)
                dve.wait_ge(cm_mm, l + 1)
                tie(dve.tensor_reduce(cnt[0:1, 0:1], bank[2][0:1, 0:P], AX.X, ALU.max))
                dve.tensor_copy(cnt_i[0:1, l:l + 1], cnt[0:1, 0:1]).then_inc(cnt_ok, 1)

            def select(e):
                full = [P, NC, 4, CAP]
                return dve.tensor_tensor(seln[:], bc(rk[:, :, bass.ds(e, 4)].unsqueeze(3), full),
                                         bc(slot_no[:].unsqueeze(1).unsqueeze(1), full), ALU.is_equal)

            def xg_high(half, buf, b=1):
                return dve.tensor_copy(xg[buf][:, 4 * half + 2 * b:4 * half + 2 * b + 2, :, :].rearrange("p k a s -> p (k a s)"), bank[b][:, :])

            def row_numbers(p, ab):
                out = None
                for dh in range(2):
                    out = dve.tensor_scalar(idx[2 * p + ab][64 * dh:64 * dh + 64, :], bank[2][64 * ab:64 * ab + 64, 2 * p + ab:2 * p + ab + 1],
                                            2.0, 2.0 * DROP + dh, ALU.mult, ALU.add)
                return out

            def mixture(l):
                xt_high(2 * l + 1)
                route(l)
                E = l * NE
                F = l * (PAIRS + 2)
                Q = l * (NE // 4 + 1)
                select(0).then_inc(sel_ok, 1)
                for half in range(2):
                    dve.wait_ge(g_mm, F + half + 1)
                    xg_high(half, 0).then_inc(xg_d, 1)
                dve.wait_ge(ix_mm, Q + 1)
                row_numbers(0, 0)
                row_numbers(0, 1).then_inc(ix_ok, 1)
                with dve.Fori(0, NE // 8) as i:
                    for u_ in range(4):
                        p, buf = u_ % 2, u_ // 2
                        if p == 0:
                            select(8 * i + (4 * buf + 4)).then_inc(sel_ok, 1)
                        for ab in range(2):
                            dve.wait_ge(sg_ok, i * 8 + (E + 2 * u_ + ab + 1))
                            dve.tensor_tensor(hh[ab][:], bank[3 + ab][:, P:2 * P], sg[ab][:], ALU.mult).then_inc(hh_ok, 1)
                        dve.wait_ge(t_mm, i * 8 + (E + 2 * u_ + 1))
                        dve.tensor_copy(hT[0][:], bank[5][:, 0:P]).then_inc(ht_ok, 1)
                        dve.wait_ge(g_mm, i * 4 + (F + u_ + 3))
                        xg_high(p, 1 - buf).then_inc(xg_d, 1)
                        dve.wait_ge(t_mm, i * 8 + (E + 2 * u_ + 2))
                        dve.tensor_copy(hT[1][:], bank[5][:, P:2 * P]).then_inc(ht_ok, 1)
                        dve.wait_ge(ix_mm, i * 2 + (Q + (u_ + 1) // 2 + 1))
                        dve.wait_ge(ys_free, i * 8 + (E + 2 * u_ + 4))
                        row_numbers(1 - p, 0)
                        row_numbers(1 - p, 1).then_inc(ix_ok, 1)
                dve.wait_ge(cnt_ok, l + 1)
                most = dve.value_load(cnt_i[0:1, l:l + 1], min_val=0, max_val=T)
                dve.wait_ge(ys_free, NE * (l + 1) + 4)
                o = ov[l]
                with dve.If(most > CAP), dve.Fori(0, ROUNDS - 1) as r:
                    with dve.If(most > CAP * r + CAP):
                        dve.tensor_scalar(rk[:], rk[:], -float(CAP), None, ALU.add).then_inc(o["rk"], 1)
                        with dve.Fori(0, NE) as e:
                            n = r * NE + e
                            dve.wait_ge(o["rk"], r + 1)
                            dve.wait_ge(o["free"], n + 1)
                            select(e).then_inc(o["sel"], 1)
                            for half in range(2):
                                dve.wait_ge(o["mm"], n * 6 + (half + 1))
                                xg_high(half, 0, 0)
                                xg_high(half, 0).then_inc(o["xg"], 1)
                            dve.wait_ge(o["mm"], n * 6 + 3)
                            row_numbers(0, 0).then_inc(o["ix"], 1)
                            dve.wait_ge(o["act"], n * 2 + 1)
                            dve.tensor_tensor(hh[0][:], bank[3][:, P:2 * P], sg[0][:], ALU.mult).then_inc(o["hid"], 1)
                            dve.wait_ge(o["mm"], n * 6 + 5)
                            dve.tensor_copy(hT[0][:], bank[5][:, 0:P]).then_inc(o["hid"], 1)
                for c in range(NC):
                    n = ROWS[c]
                    dve.wait_ge(yab_in[c], 32 * (l + 1))
                    h = H[0:n, c, :]
                    for i in range(2):
                        tie(dve.scalar_tensor_tensor(h, yab[c][0:n, i, :], gate[i][0:n, c:c + 1], h, ALU.mult, ALU.add))
                    dve.nop().then_inc(h_ok, 1)
                    if l == 0 and c > 0:
                        norm(2, c - 1)
                if l == 0:
                    norm(2, NC - 1)
            mixture(0)

            mixer_in_lo(2, xc_lo)
            dve.wait_ge(st_in, 48)
            tie(dve.memset(u[:, 0:2], 0.0))
            S0 = 2 + SEQ
            parts = [[(0, HALF, 0)], [(0, SEQ - HALF, HALF), (SEQ - HALF, HALF, SEQ)]]
            with dve.Fori(0, KT) as m:
                tie.loop(m, CONV_STEPS, KT)
                mm = bass.ds(m, 1)
                tie(dve.tensor_copy(u[:, S0:S0 + 2], hist[:, mm, :].rearrange("p k r -> p (k r)")))
                for half in range(2):
                    dve.wait_ge(hc_ok, m * 2 + (half + 1))
                    for a, b, t0 in parts[half]:
                        col = t0 + 2 + (2 if t0 == SEQ else 0)
                        tie(dve.tensor_tensor(u[:, col:col + b - a], bank[3 * half + 1][:, a:b], hc[half][:, a:b], ALU.mult))
                    for a, b, t0 in parts[half]:
                        col, w = t0 + (2 if t0 == SEQ else 0), b - a
                        c0 = cv[:, t0:t0 + w]
                        tie(dve.tensor_scalar(c0, u[:, col:col + w], convw[:, bass.ds(m, 1)], None, ALU.mult))
                        tie(dve.scalar_tensor_tensor(c0, u[:, col + 1:col + 1 + w], convw[:, bass.ds(m + KT, 1)], c0, ALU.mult, ALU.add))
                        tie(dve.scalar_tensor_tensor(c0, u[:, col + 2:col + 2 + w], convw[:, bass.ds(m + 2 * KT, 1)], c0, ALU.mult, ALU.add))
                    tie(dve.tensor_tensor(gT[:, mm, half * HALF:(half + 1) * HALF].rearrange("p k t -> p (k t)"), bank[3 * half][:, 0:HALF],
                                          cv[:, half * HALF:(half + 1) * HALF], ALU.mult))
                    dve.nop().then_inc(cg_ok, 1)
                tie(dve.tensor_copy(tails[:, 0, mm, :].rearrange("p k r -> p (k r)"), u[:, SEQ:SEQ + 2]))
                tie(dve.tensor_copy(tails[:, 1, mm, :].rearrange("p k r -> p (k r)"), u[:, UW - 2:UW]))
                dve.nop().then_inc(tail_ok, 1)
            tie.end()
            for c in range(NC):
                t = slice(c * P, c * P + ROWS[c])
                dve.wait_ge(z_hi, 1 + c + 1)
                dve.tensor_tensor(g_lo[:, :, t], gT[:, :, t], g_hi[:, :, t].bitcast(F32), ALU.subtract).then_inc(z_lo, 1)
            residual(1)
            mixture(1)


CONV_STEPS = 1 + 3 + 3 * 3 + 2 + 2

_INS = ['x_prompt', 'x_sample', 'cache_a_k', 'cache_a_v', 'state_hgrn', 'state_conv', 'norm_mix', 'norm_ffn', 'w_in_ab',
        'w_out_ab', 'q_norm', 'k_norm', 'rel_bias', 'hgrn_lb_logits', 'hgrn_out_norm', 'w_in_c', 'conv_w', 'w_out_c',
        'w_group', 'b_group', 'w_expert', 'b_expert', 'w1', 'w3', 'w2']
_OUTS = [(1, SEQ, D), (1, DEC, D), (1, 1, SEQ, NH, HD), (1, 1, SEQ, NH, HD), (1, 1, PAST, NH, HD), (1, 1, PAST, NH, HD),
         (1, 1, NH, HD, HD), (1, 1, NH, HD, HD), (1, 1, 2, D), (1, 1, 2, D)]


def kernel(**inputs):
    import numpy as _np
    import concourse.bacc as _bacc
    from concourse import mybir as _mybir
    from concourse.bass_utils import run_bass_kernel_spmd as _run

    nc = _bacc.Bacc("TRN2", target_bir_lowering=False, num_devices=1)
    arrays, args = {}, []
    for name in _INS:
        a = _np.ascontiguousarray(inputs[name])
        arrays[f"in_{name}_dram"] = a
        args.append(nc.dram_tensor(f"in_{name}_dram", a.shape, _mybir.dt.from_np(a.dtype), kind="ExternalInput").ap())
    for i, shape in enumerate(_OUTS):
        args.append(nc.dram_tensor(f"out_{i}_dram", shape, _mybir.dt.float32, kind="ExternalOutput").ap())
    hmoe_step(nc, *args)
    r = _run(nc, [arrays], core_ids=[0])
    return tuple(r.results[0][f"out_{i}_dram"] for i in range(len(_OUTS)))
```
